# Optimizing a Trainium2 kernel written in Bass

```python
import jax, jax.numpy as jnp
from jax import lax
import numpy as np

D_MODEL = 1024
BATCH = 1
SEQ = 256
DEPTH = 2

N_HEADS = 8
N_KV_HEADS = 2
HEAD_DIM = 64
ATTN_WIDTH = N_HEADS * HEAD_DIM
KV_WIDTH = N_KV_HEADS * HEAD_DIM
WINDOW = 128
BLOCK = 128
ROPE_DIM = HEAD_DIM // 4
ROPE_THETA = 500000.0
CONV_WIDTH = D_MODEL - ATTN_WIDTH
CONV_K = 3
MIX_WIDTH = ATTN_WIDTH + CONV_WIDTH
IN_WIDTH = ATTN_WIDTH + 2 * KV_WIDTH + 3 * CONV_WIDTH
SPLITS = (ATTN_WIDTH, ATTN_WIDTH + KV_WIDTH, ATTN_WIDTH + 2 * KV_WIDTH,
          ATTN_WIDTH + 2 * KV_WIDTH + CONV_WIDTH, ATTN_WIDTH + 2 * KV_WIDTH + 2 * CONV_WIDTH)
N_EXPERT_GROUPS = 4
EXPERTS_PER_GROUP = 8
N_EXPERTS = N_EXPERT_GROUPS * EXPERTS_PER_GROUP
TOP_K = 2
D_EXPERT = 512
MOE_BLOCK = 256
EPS = 1e-6
NEG_INF = -1e30


def rmsnorm(x, g):
    xf = x.astype(jnp.float32)
    y = xf * lax.rsqrt(jnp.mean(xf * xf, axis=-1, keepdims=True) + EPS)
    return (y * g.astype(jnp.float32)).astype(x.dtype)

def rope_tables(seq):
    pos = jnp.arange(seq, dtype=jnp.float32)
    inv_freq = ROPE_THETA ** (-jnp.arange(0, ROPE_DIM, 2, dtype=jnp.float32) / ROPE_DIM)
    ang = pos[:, None] * inv_freq[None, :]
    return jnp.cos(ang)[:, None, :], jnp.sin(ang)[:, None, :]

def partial_rope(x, cos, sin):
    half = ROPE_DIM // 2
    xf = x.astype(jnp.float32)
    x1, x2, rest = xf[..., :half], xf[..., half:ROPE_DIM], xf[..., ROPE_DIM:]
    out = jnp.concatenate([x1 * cos - x2 * sin, x2 * cos + x1 * sin, rest], axis=-1)
    return out.astype(x.dtype)

def windowed_gqa_with_sink(q, k, v, sink):
    b, s = q.shape[0], q.shape[1]
    nb = s // BLOCK
    grp = N_HEADS // N_KV_HEADS
    qb = q.reshape(b, nb, BLOCK, N_KV_HEADS, grp, HEAD_DIM)

    def band(t):
        tp = jnp.pad(t, ((0, 0), (BLOCK, BLOCK), (0, 0), (0, 0)))
        tp = tp.reshape(b, nb + 2, BLOCK, N_KV_HEADS, HEAD_DIM)
        return jnp.concatenate([tp[:, :-2], tp[:, 1:-1], tp[:, 2:]], axis=2)

    kb, vb = band(k), band(v)
    scores = jnp.einsum('bnqhgd,bnkhd->bnhgqk', qb, kb,
                        preferred_element_type=jnp.float32) * (HEAD_DIM ** -0.5)
    qi = jnp.arange(BLOCK)[:, None]
    kj = jnp.arange(3 * BLOCK)[None, :]
    k_pos = (jnp.arange(nb)[:, None, None] - 1) * BLOCK + kj
    mask = (jnp.abs(kj - BLOCK - qi) <= WINDOW) & (k_pos >= 0) & (k_pos < s)
    scores = jnp.where(mask[None, :, None, None], scores, NEG_INF)
    sink_col = jnp.broadcast_to(
        sink.astype(jnp.float32).reshape(N_KV_HEADS, grp)[None, None, :, :, None, None],
        scores.shape[:-1] + (1,))
    probs = jax.nn.softmax(jnp.concatenate([scores, sink_col], axis=-1), axis=-1)[..., :-1]
    out = jnp.einsum('bnhgqk,bnkhd->bnqhgd', probs.astype(v.dtype), vb)
    return out.reshape(b, s, ATTN_WIDTH)

def centred_short_conv(u, w):
    up = jnp.pad(u, ((0, 0), (1, 1), (0, 0)))
    return up[:, :-2] * w[0] + up[:, 1:-1] * w[1] + up[:, 2:] * w[2]

def hybrid_mixer(h, w_in, sink, conv_w, g_attn, g_conv, w_out, cos, sin):
    b, s, _ = h.shape
    proj = h @ w_in
    q, k, v, gate_b, gate_c, u = jnp.split(proj, SPLITS, axis=-1)
    q = partial_rope(q.reshape(b, s, N_HEADS, HEAD_DIM), cos, sin)
    k = partial_rope(k.reshape(b, s, N_KV_HEADS, HEAD_DIM), cos, sin)
    v = v.reshape(b, s, N_KV_HEADS, HEAD_DIM)
    y_attn = windowed_gqa_with_sink(q, k, v, sink)
    y_conv = gate_b * centred_short_conv(gate_c * u, conv_w)
    y = jnp.concatenate([rmsnorm(y_attn, g_attn), rmsnorm(y_conv, g_conv)], axis=-1)
    return y @ w_out

def hierarchical_moe(h, w_rg, b_rg, w_re, b_re, w_gate, w_up, w_down):
    b, s, d = h.shape
    t = b * s
    xf = h.reshape(t, d)
    group_logits = (xf @ w_rg).astype(jnp.float32) + b_rg.astype(jnp.float32)
    group_prob = jax.nn.softmax(group_logits, axis=-1)
    grp = jnp.argmax(group_logits, axis=-1)
    p_grp = jnp.take_along_axis(group_prob, grp[:, None], axis=-1)
    expert_logits = ((xf @ w_re).astype(jnp.float32) + b_re.astype(jnp.float32)
                     ).reshape(t, N_EXPERT_GROUPS, EXPERTS_PER_GROUP)
    in_group = jnp.take_along_axis(expert_logits, grp[:, None, None], axis=1)[:, 0]
    top_logit, top_local = lax.top_k(in_group, TOP_K)
    gates = p_grp * jax.nn.softmax(top_logit, axis=-1)
    experts = grp[:, None] * EXPERTS_PER_GROUP + top_local

    a = t * TOP_K
    flat_e = experts.reshape(a)
    flat_tok = jnp.arange(a, dtype=jnp.int32) // TOP_K
    flat_g = gates.reshape(a)
    order = jnp.argsort(flat_e)
    e_sorted, tok_sorted, g_sorted = flat_e[order], flat_tok[order], flat_g[order]
    counts = jnp.bincount(flat_e, length=N_EXPERTS)
    starts = jnp.cumsum(counts) - counts
    padded = (counts + MOE_BLOCK - 1) // MOE_BLOCK * MOE_BLOCK
    padded_end = jnp.cumsum(padded)
    dest = (padded_end - padded)[e_sorted] + jnp.arange(a) - starts[e_sorted]
    n_blocks = -(-a // MOE_BLOCK) + N_EXPERTS
    cap = n_blocks * MOE_BLOCK
    slot_tok = jnp.zeros((cap,), jnp.int32).at[dest].set(tok_sorted)
    block_expert = jnp.minimum(
        jnp.searchsorted(padded_end, jnp.arange(n_blocks) * MOE_BLOCK, side='right'),
        N_EXPERTS - 1)
    x_slots = xf[slot_tok].reshape(n_blocks, MOE_BLOCK, d)

    def expert_block(args):
        xb, e = args
        return (jax.nn.silu(xb @ w_gate[e]) * (xb @ w_up[e])) @ w_down[e]

    y_slots = lax.map(expert_block, (x_slots, block_expert)).reshape(cap, d)
    y_assign = y_slots[dest] * g_sorted[:, None].astype(h.dtype)
    y = jax.ops.segment_sum(y_assign, tok_sorted, num_segments=t)
    return y.reshape(b, s, d)

def first_inputs(seed: int = 0) -> dict:
    key = jax.random.key(seed)
    ks = jax.random.split(key, 17)
    f32 = jnp.float32
    nrm = lambda k, shape, scale: jax.random.normal(k, shape, f32) * scale
    res_scale = (2.0 * DEPTH) ** -0.5
    return {
        "x": nrm(ks[0], (BATCH, SEQ, D_MODEL), 1.0),
        "norm_mix": 1.0 + nrm(ks[1], (DEPTH, D_MODEL), 0.02),
        "w_in": nrm(ks[2], (DEPTH, D_MODEL, IN_WIDTH), D_MODEL ** -0.5),
        "attn_sink": nrm(ks[3], (DEPTH, N_HEADS), 0.5),
        "conv_w": nrm(ks[4], (DEPTH, CONV_K, CONV_WIDTH), CONV_K ** -0.5),
        "norm_attn_out": 1.0 + nrm(ks[5], (DEPTH, ATTN_WIDTH), 0.02),
        "norm_conv_out": 1.0 + nrm(ks[6], (DEPTH, CONV_WIDTH), 0.02),
        "w_out": nrm(ks[7], (DEPTH, MIX_WIDTH, D_MODEL), MIX_WIDTH ** -0.5 * res_scale),
        "norm_ffn": 1.0 + nrm(ks[8], (DEPTH, D_MODEL), 0.02),
        "w_router_group": nrm(ks[9], (DEPTH, D_MODEL, N_EXPERT_GROUPS), D_MODEL ** -0.5),
        "b_router_group": nrm(ks[10], (DEPTH, N_EXPERT_GROUPS), 0.01),
        "w_router_expert": nrm(ks[11], (DEPTH, D_MODEL, N_EXPERTS), D_MODEL ** -0.5),
        "b_router_expert": nrm(ks[12], (DEPTH, N_EXPERTS), 0.01),
        "w_expert_gate": nrm(ks[13], (DEPTH, N_EXPERTS, D_MODEL, D_EXPERT), D_MODEL ** -0.5),
        "w_expert_up": nrm(ks[14], (DEPTH, N_EXPERTS, D_MODEL, D_EXPERT), D_MODEL ** -0.5),
        "w_expert_down": nrm(ks[15], (DEPTH, N_EXPERTS, D_EXPERT, D_MODEL), D_EXPERT ** -0.5 * res_scale),
        "norm_final": 1.0 + nrm(ks[16], (D_MODEL,), 0.02),
    }

def first_block(x, norm_mix, w_in, attn_sink, conv_w, norm_attn_out, norm_conv_out, w_out,
              norm_ffn, w_router_group, b_router_group, w_router_expert, b_router_expert,
              w_expert_gate, w_expert_up, w_expert_down, norm_final):
    cos, sin = rope_tables(x.shape[1])
    for l in range(DEPTH):
        x = x + hybrid_mixer(rmsnorm(x, norm_mix[l]), w_in[l], attn_sink[l], conv_w[l],
                             norm_attn_out[l], norm_conv_out[l], w_out[l], cos, sin)
        x = x + hierarchical_moe(rmsnorm(x, norm_ffn[l]), w_router_group[l], b_router_group[l],
                                 w_router_expert[l], b_router_expert[l], w_expert_gate[l],
                                 w_expert_up[l], w_expert_down[l])
    return rmsnorm(x, norm_final)


HEAD_DIM_2 = 128
ATTN_WIDTH_2 = N_HEADS * HEAD_DIM_2
IDX_HEADS = 16
IDX_DIM = 64
TOPK_MAX = 256
Q_BLOCK = 128
D_RNN = 1408
RNN_BLOCKS = 16
RNN_BLOCK_DIM = D_RNN // RNN_BLOCKS
CONV_WIDTH_2 = 4
LRU_C = 8.0
ROPE_THETA_2 = 10000.0
NORM_EPS = 1e-6

SPLIT_SIZES = (ATTN_WIDTH_2, ATTN_WIDTH_2, ATTN_WIDTH_2, ATTN_WIDTH_2,
               IDX_HEADS * IDX_DIM, IDX_DIM, IDX_HEADS,
               D_RNN, D_RNN, D_MODEL, D_MODEL)
N_IN = sum(SPLIT_SIZES)


def rmsnorm_2(x, g):
    xf = x.astype(jnp.float32)
    y = xf * lax.rsqrt(jnp.mean(xf * xf, axis=-1, keepdims=True) + NORM_EPS)
    return (y * g.astype(jnp.float32)).astype(x.dtype)

def rope_tables_2(positions, dim):
    inv = ROPE_THETA_2 ** (-jnp.arange(0, dim, 2, dtype=jnp.float32) / dim)
    ang = positions.astype(jnp.float32)[..., None] * inv
    return jnp.cos(ang), jnp.sin(ang)

def apply_rope(x, cos, sin):
    extra = x.ndim - cos.ndim
    shape = cos.shape[:2] + (1,) * extra + cos.shape[2:]
    c, s = cos.reshape(shape), sin.reshape(shape)
    x1, x2 = jnp.split(x.astype(jnp.float32), 2, axis=-1)
    return jnp.concatenate([x1 * c - x2 * s, x2 * c + x1 * s], axis=-1).astype(x.dtype)

def dsa_attention(q, k, v, iq, ik, iw):
    B, S, H, Dh = q.shape
    topk = min(TOPK_MAX, S // 4)
    n_blk = S // Q_BLOCK
    key_pos = jnp.arange(S)
    scale = HEAD_DIM_2 ** -0.5
    iw = iw.astype(jnp.float32) * (IDX_HEADS ** -0.5) * (IDX_DIM ** -0.5)

    def block(i):
        q0 = i * Q_BLOCK
        qb = lax.dynamic_slice_in_dim(q, q0, Q_BLOCK, axis=1)
        iqb = lax.dynamic_slice_in_dim(iq, q0, Q_BLOCK, axis=1)
        iwb = lax.dynamic_slice_in_dim(iw, q0, Q_BLOCK, axis=1)
        qpos = q0 + jnp.arange(Q_BLOCK)
        causal = key_pos[None, :] <= qpos[:, None]
        dots = jnp.einsum('bqhd,bsd->bqhs', iqb, ik, preferred_element_type=jnp.float32)
        idx_score = jnp.einsum('bqh,bqhs->bqs', iwb, jax.nn.relu(dots))
        idx_score = jnp.where(causal[None], idx_score, -jnp.inf)
        _, sel = lax.top_k(idx_score, topk)
        valid = sel <= qpos[None, :, None]
        k_sel = jax.vmap(lambda kb, ib: kb[ib])(k, sel)
        v_sel = jax.vmap(lambda vb, ib: vb[ib])(v, sel)
        logits = jnp.einsum('bqhd,bqkhd->bhqk', qb, k_sel, preferred_element_type=jnp.float32) * scale
        logits = jnp.where(valid[:, None], logits, -jnp.inf)
        p = jax.nn.softmax(logits, axis=-1)
        return jnp.einsum('bhqk,bqkhd->bqhd', p.astype(v.dtype), v_sel)

    out = lax.map(block, jnp.arange(n_blk))
    return out.transpose(1, 0, 2, 3, 4).reshape(B, S, H, Dh)

def causal_depthwise_conv(x, w, b):
    y = lax.conv_general_dilated(
        x, w[:, None, :].astype(x.dtype), window_strides=(1,),
        padding=[(CONV_WIDTH_2 - 1, 0)], dimension_numbers=('NWC', 'WIO', 'NWC'),
        feature_group_count=x.shape[-1])
    return y + b.astype(x.dtype)

def rg_lru(x, w_r, b_r, w_i, b_i, lam):
    B, S, _ = x.shape
    xb = x.reshape(B, S, RNN_BLOCKS, RNN_BLOCK_DIM)
    r = jax.nn.sigmoid((jnp.einsum('bsnc,ncd->bsnd', xb, w_r).reshape(B, S, D_RNN) + b_r).astype(jnp.float32))
    i = jax.nn.sigmoid((jnp.einsum('bsnc,ncd->bsnd', xb, w_i).reshape(B, S, D_RNN) + b_i).astype(jnp.float32))
    log_a = -LRU_C * r * jax.nn.softplus(-lam.astype(jnp.float32))
    a = jnp.exp(log_a)
    u = jnp.sqrt(-jnp.expm1(2.0 * log_a)) * (i * x.astype(jnp.float32))

    def combine(left, right):
        a_l, b_l = left
        a_r, b_r = right
        return a_l * a_r, a_r * b_l + b_r

    _, h = lax.associative_scan(combine, (a, u), axis=1)
    return h.astype(x.dtype)

def second_inputs(seed: int = 0) -> dict:
    key = jax.random.key(seed)
    ks = jax.random.split(key, 16)
    f32 = jnp.float32
    x = jax.random.normal(ks[0], (BATCH, SEQ, D_MODEL), f32)
    positions = jnp.broadcast_to(jnp.arange(SEQ, dtype=jnp.int32), (BATCH, SEQ))
    norm_g = 1.0 + 0.02 * jax.random.normal(ks[1], (DEPTH, D_MODEL), f32)
    w_in = jax.random.normal(ks[2], (DEPTH, D_MODEL, N_IN), f32) * D_MODEL ** -0.5
    conv_w = jax.random.normal(ks[3], (DEPTH, CONV_WIDTH_2, D_RNN), f32) * CONV_WIDTH_2 ** -0.5
    conv_b = 0.01 * jax.random.normal(ks[4], (DEPTH, D_RNN), f32)
    w_rg = jax.random.normal(ks[5], (DEPTH, RNN_BLOCKS, RNN_BLOCK_DIM, RNN_BLOCK_DIM), f32) * RNN_BLOCK_DIM ** -0.5
    b_rg = 0.01 * jax.random.normal(ks[6], (DEPTH, D_RNN), f32)
    w_ig = jax.random.normal(ks[7], (DEPTH, RNN_BLOCKS, RNN_BLOCK_DIM, RNN_BLOCK_DIM), f32) * RNN_BLOCK_DIM ** -0.5
    b_ig = 0.01 * jax.random.normal(ks[8], (DEPTH, D_RNN), f32)
    a0 = jax.random.uniform(ks[9], (DEPTH, D_RNN), f32, 0.9, 0.999)
    p = a0 ** (1.0 / LRU_C)
    lru_lambda = jnp.log(p) - jnp.log1p(-p)
    w_out_attn = jax.random.normal(ks[10], (DEPTH, ATTN_WIDTH_2, D_MODEL), f32) * ATTN_WIDTH_2 ** -0.5
    w_out_rnn = jax.random.normal(ks[11], (DEPTH, D_RNN, D_MODEL), f32) * D_RNN ** -0.5
    w_o = jax.random.normal(ks[12], (DEPTH, D_MODEL, D_MODEL), f32) * D_MODEL ** -0.5
    final_g = 1.0 + 0.02 * jax.random.normal(ks[13], (D_MODEL,), f32)
    return {"x": x, "positions": positions, "norm_g": norm_g, "w_in": w_in,
            "conv_w": conv_w, "conv_b": conv_b, "w_rg": w_rg, "b_rg": b_rg,
            "w_ig": w_ig, "b_ig": b_ig, "lru_lambda": lru_lambda,
            "w_out_attn": w_out_attn, "w_out_rnn": w_out_rnn, "w_o": w_o,
            "final_g": final_g}

def second_block(x, positions, norm_g, w_in, conv_w, conv_b, w_rg, b_rg, w_ig, b_ig,
              lru_lambda, w_out_attn, w_out_rnn, w_o, final_g):
    B, S, _ = x.shape
    offsets = np.cumsum(SPLIT_SIZES)[:-1].tolist()
    cos_a, sin_a = rope_tables_2(positions, HEAD_DIM_2)
    cos_i, sin_i = rope_tables_2(positions, IDX_DIM)
    for l in range(DEPTH):
        h = rmsnorm_2(x, norm_g[l])
        proj = h @ w_in[l]
        q, k, v, ga, iq, ik, iw, xr, gr, ma, mb = jnp.split(proj, offsets, axis=-1)
        q = apply_rope(q.reshape(B, S, N_HEADS, HEAD_DIM_2), cos_a, sin_a)
        k = apply_rope(k.reshape(B, S, N_HEADS, HEAD_DIM_2), cos_a, sin_a)
        v = v.reshape(B, S, N_HEADS, HEAD_DIM_2)
        iq = apply_rope(iq.reshape(B, S, IDX_HEADS, IDX_DIM), cos_i, sin_i)
        ik = apply_rope(ik, cos_i, sin_i)
        attn = dsa_attention(q, k, v, iq, ik, iw).reshape(B, S, ATTN_WIDTH_2)
        y_a = (attn * jax.nn.silu(ga)) @ w_out_attn[l]
        xr = causal_depthwise_conv(xr, conv_w[l], conv_b[l])
        hr = rg_lru(xr, w_rg[l], b_rg[l], w_ig[l], b_ig[l], lru_lambda[l])
        y_b = (hr * jax.nn.silu(gr)) @ w_out_rnn[l]
        merged = jax.nn.sigmoid(ma) * y_a + jax.nn.sigmoid(mb) * y_b
        x = x + merged @ w_o[l]
    return rmsnorm_2(x, final_g)


def setup_inputs(seed=0):
    out = dict(first_inputs(seed))
    for name, value in second_inputs(seed + 1).items():
        if name != "x":
            out[name + "_2"] = value
    return out


def reference(
    x, norm_mix, w_in, attn_sink, conv_w, norm_attn_out, norm_conv_out, w_out, norm_ffn,
    w_router_group, b_router_group, w_router_expert, b_router_expert, w_expert_gate,
    w_expert_up, w_expert_down, norm_final, positions_2, norm_g_2, w_in_2, conv_w_2, conv_b_2,
    w_rg_2, b_rg_2, w_ig_2, b_ig_2, lru_lambda_2, w_out_attn_2, w_out_rnn_2, w_o_2, final_g_2,
):
    x = first_block(
        x, norm_mix, w_in, attn_sink, conv_w, norm_attn_out, norm_conv_out, w_out, norm_ffn,
        w_router_group, b_router_group, w_router_expert, b_router_expert, w_expert_gate,
        w_expert_up, w_expert_down, norm_final,
    )
    return second_block(
        x, positions_2, norm_g_2, w_in_2, conv_w_2, conv_b_2, w_rg_2, b_rg_2, w_ig_2, b_ig_2,
        lru_lambda_2, w_out_attn_2, w_out_rnn_2, w_o_2, final_g_2,
    )


_drawn_inputs = setup_inputs


def setup_inputs(seed=0):
    import zlib

    import numpy as np

    out = dict(_drawn_inputs(seed))
    spreads = {}
    factors = {'attn_sink': 8.0,
     'norm_conv_out': 3.192,
     'b_router_group': 6.436,
     'b_router_expert': 4.127,
     'norm_g_2': 2.76,
     'conv_b_2': 3.291,
     'b_rg_2': 8.0,
     'b_ig_2': 8.0,
     'final_g_2': 2.78}
    for name, (base, spread) in spreads.items():
        noise = np.random.default_rng([zlib.crc32(name.encode()), seed]).standard_normal(out[name].shape)
        drawn = base * np.exp(spread * noise) if base else spread * noise
        out[name] = __import__('jax').numpy.asarray(drawn.astype(out[name].dtype))
    for name, factor in factors.items():
        out[name] = (out[name] * factor).astype(out[name].dtype)
    return out
```

```python
from contextlib import ExitStack

import numpy as np

import concourse.bass as bass
from concourse import mybir

F32 = mybir.dt.float32
I32 = mybir.dt.int32
ALU = mybir.AluOpType
ACT = mybir.ActivationFunctionType
AX = mybir.AxisListType

P = 128
SEQ = 256
NT = SEQ // P
D = 1024
KD = D // P
DEPTH = 2
EPS = 1e-6
NEG = -1e30
TAKEN = -3e38

HEADS = 8
HD1 = 64
KVH = 2
QW = HEADS * HD1
KVW = KVH * HD1
CW = D - QW
IN1 = QW + 2 * KVW + 3 * CW
ROT1 = 8
GROUPS = 4
PER_GROUP = 8
NE = GROUPS * PER_GROUP
DE = 512
FE = DE // P
SLOTS = 64
ROUNDS = SEQ // SLOTS
ROUTER_W = GROUPS + NE

HD2 = 128
AW2 = HEADS * HD2
IH = 16
ID = 64
TOPK = min(256, SEQ // 4)
RNN = 1408
RT = RNN // P
RB = 16
RBD = RNN // RB
LRU_C = 8.0
TAPS2 = 4
Q2, K2, V2, GA2, IQ2 = 0, 1024, 2048, 3072, 4096
IK2 = IQ2 + IH * ID
XR2 = IK2 + ID + IH
GR2 = XR2 + RNN
MA2 = GR2 + RNN
MB2 = MA2 + D
IN2 = MB2 + D

BETWEEN = 2 * DEPTH
SECOND = BETWEEN + 1
FINAL = SECOND + DEPTH

RING = 6
SLOT_F = 4096
BANKS = 8
MOE_BANKS = 4

BLOCK_PAIRS = [(j, i) for j in range(RT) for i in range(RT)
               if i * P < -(-(j + 1) * P // RBD) * RBD and (i + 1) * P > (j * P // RBD) * RBD]
NBP = len(BLOCK_PAIRS)

COLS = {}
_at = 0
for _name, _n in [("g_attn", 4), ("g_conv", 4), ("conv1", 12), ("conv2", TAPS2 * RT), ("conv2_b", RT),
                  ("b_rg", RT), ("b_ig", RT), ("lam", RT)]:
    COLS[_name] = (_at, _n)
    _at += _n
NCOLS = _at

NROPE1 = NT * (HEADS + KVH) * ROT1
INV2 = HD2 // 2 + ID // 2
TWO_PI_PARTS = (6.28125, 0.0019340515136718750, 1.2556659146999e-6)
ROUNDER = 12582912.0


def psum_tiles():
    names = []
    for layer in range(DEPTH):
        names += [("hT", 2 * layer, j) for j in range(4)]
        names += [("q", layer, t) for t in range(NT)] + [("kv", layer, t) for t in range(NT)]
        names += [(g, layer, j) for g in ("gb", "gc", "u") for j in range(2)]
        names += [("qkT", layer, j) for j in range(3)]
        names += [("S1", layer, 0)]
        for h in range(HEADS):
            names += [("S1", layer, h + 1)] if h + 1 < HEADS else []
            names += [("PT1", layer, h)]
            names += [("Y1", layer, h // 2)] if h % 2 == 0 else []
        names += [("ss", layer, 0)]
        names += [("out1", layer, i) for i in range(8)]
        names += [("hT", 2 * layer + 1, j) for j in range(4)]
        names += [("logits", layer, 0), ("rank", layer, 0)]
    for layer in range(DEPTH):
        names += [("hT", SECOND + layer, j) for j in range(4)]
        names += [("xr", layer, j) for j in range(6)]
        for c in range(15):
            names += [("rope", layer, c)] if c < 14 else []
            names += [("ropeT", layer, c - 2)] if c >= 2 else []
        names += [("ropeT", layer, 13)]
        names += [("v", layer, j) for j in range(4)]
        names += [("dots", layer, j) for j in range(12)]
        names += [("gates", layer, j) for j in range(RT)]
        names += [("gr", layer, j) for j in range(6)]
        names += [("S2", layer, 0)]
        for h in range(HEADS):
            names += [("ga", layer, h)]
            names += [("S2", layer, h + 1)] if h + 1 < HEADS else []
            names += [("PT2", layer, h), ("Y2", layer, h)]
        names += [("ma", layer, j) for j in range(8)]
        names += [("mb", layer, j) for j in range(8)]
        names += [("out2", layer, j) for j in range(4)]
    return {name: n for n, name in enumerate(names)}


TILE = psum_tiles()
assert len(TILE) == max(TILE.values()) + 1


class Steps:

    def __init__(self, eng, own, base=None):
        self.eng, self.own, self.base, self.n, self.last = eng, own, base or {}, {}, None

    def value(self, sem):
        n = self.n.get(sem.name, 0)
        return self.base[sem.name] + n if sem.name in self.base else n

    def __call__(self, ins, sem=None):
        sem = sem or self.own
        ins.then_inc(sem, 1)
        self.n[sem.name] = self.n.get(sem.name, 0) + 1
        self.last = (sem, self.value(sem))

    def marks(self, ins, sem, value):
        ins.then_inc(sem, 1)
        self.last = (sem, value)

    def settle(self):
        if self.last is not None:
            self.eng.wait_ge(*self.last)


def program(nc, x_in, cols_in, rows_in, rope1_in, gains_in, router_in, w_in, w_out, w_gate, w_up, w_down,
            positions, w_in2, w_lru, w_oa, w_or, w_o, out, upto=99):
    with ExitStack() as ctx:
        def sem(name):
            return ctx.enter_context(nc.semaphore(name))

        ring = ctx.enter_context(nc.sbuf_tensor("ring", [P, RING, SLOT_F], F32))
        x = ctx.enter_context(nc.sbuf_tensor("x", [P, NT, D], F32))
        h = ctx.enter_context(nc.sbuf_tensor("h", [P, NT, D], F32))
        hT = ctx.enter_context(nc.sbuf_tensor("hT", [P, KD, SEQ], F32))

        ident = ctx.enter_context(nc.sbuf_tensor("ident", [P, P], F32))
        ones = ctx.enter_context(nc.sbuf_tensor("ones", [P, P], F32))
        zeros = ctx.enter_context(nc.sbuf_tensor("zeros", [P, P], F32))
        before = ctx.enter_context(nc.sbuf_tensor("before", [P, P], F32))
        iota_i = ctx.enter_context(nc.sbuf_tensor("iota_i", [P, SLOTS], I32))
        iota_f = ctx.enter_context(nc.sbuf_tensor("iota_f", [P, SLOTS], F32))
        cols = ctx.enter_context(nc.sbuf_tensor("cols", [P, DEPTH, NCOLS], F32))
        rows = ctx.enter_context(nc.sbuf_tensor("rows", [P, DEPTH * (ROUTER_W + HEADS) + INV2], F32))
        gain = ctx.enter_context(nc.sbuf_tensor("gain", [P, D], F32))
        ang = ctx.enter_context(nc.sbuf_tensor("ang", [P, NT, INV2], F32))
        cos2 = ctx.enter_context(nc.sbuf_tensor("cos2", [P, NT, INV2], F32))
        sin2 = ctx.enter_context(nc.sbuf_tensor("sin2", [P, NT, INV2], F32))
        pos_i = ctx.enter_context(nc.sbuf_tensor("pos_i", [P, NT], I32))
        pos_f = ctx.enter_context(nc.sbuf_tensor("pos_f", [P, NT], F32))
        decay = ctx.enter_context(nc.sbuf_tensor("decay", [P, DEPTH, RT], F32))
        lam_t = ctx.enter_context(nc.sbuf_tensor("lam_t", [P, 4, DEPTH, RT], F32))
        power = ctx.enter_context(nc.sbuf_tensor("power", [P, 4], F32))
        stat = ctx.enter_context(nc.sbuf_tensor("stat", [P, 64], F32))
        small = ctx.enter_context(nc.sbuf_tensor("small", [P, 15, NT, NE], F32))
        causal = ctx.enter_context(nc.sbuf_tensor("causal", [P, 3 * P], F32))
        top8 = ctx.enter_context(nc.sbuf_tensor("top8", [P, 16], F32))
        trips_i = ctx.enter_context(nc.sbuf_tensor("trips_i", [P, 2], I32))

        WORK = 18240
        work = ctx.enter_context(nc.sbuf_tensor("work", [P, WORK], F32))
        top = {}

        def carve(phase, *shape):
            n = int(np.prod(shape))
            at = top.get(phase, 0)
            top[phase] = at + n
            assert top[phase] <= WORK, (phase, top[phase])
            v = work[:, at:at + n]
            if len(shape) == 2:
                v = v.rearrange("p (a b) -> p a b", a=shape[0])
            if len(shape) == 3:
                v = v.rearrange("p (a b c) -> p a b c", a=shape[0], b=shape[1])
            return v

        window = carve("keep1", NT, SEQ)
        cos1 = carve("keep1", NROPE1)
        sin1 = carve("keep1", NROPE1)
        w_router = carve("keep1", KD, P)
        top["mix1"] = top["moe"] = top["keep1"]
        qkv = carve("mix1", NT, QW + 2 * KVW)
        kswap = carve("mix1", NT, KVW)
        rt1 = carve("mix1", 4, NROPE1)
        qT1 = carve("mix1", HEADS // 2, SEQ)
        kT1 = carve("mix1", 2, SEQ)
        gb = carve("mix1", 4, SEQ)
        gc = carve("mix1", 4, SEQ)
        cu = carve("mix1", 4, SEQ + 2)
        yc = carve("mix1", 4, SEQ)
        yc_t = carve("mix1", SEQ)
        yT = carve("mix1", KD, SEQ)
        sq = carve("mix1", KD, SEQ)
        s1 = carve("mix1", 2, NT, SEQ)
        pT1 = carve("mix1", 2, NT, SEQ)
        xg = carve("moe", KD, PER_GROUP * SLOTS)
        pick = carve("moe", NT, PER_GROUP, SLOTS)
        wpick = carve("moe", NT, PER_GROUP, SLOTS)
        comb = carve("moe", 2, SEQ)
        silu_g = carve("moe", 2, DE)
        hid = carve("moe", 2, DE)
        hidT = carve("moe", 2, FE * P)
        ysb = carve("moe", 2, D)
        xr = carve("b2", RT, SEQ + TAPS2 - 1)
        xc = carve("b2", RT, SEQ)
        ra = carve("b2", RT, SEQ)
        ui = carve("b2", RT, SEQ)
        qT = carve("b2", HEADS, SEQ)
        kT = carve("b2", HEADS, SEQ)
        roped_at = top["b2"]
        roped = carve("b2", 4, 512)
        bias2 = carve("b2", 3 * P)
        iw = carve("b2", NT, IH)
        top["idx"] = roped_at
        relu = carve("idx", 2, 512)
        wk = carve("idx", 2, 3 * P)
        top["att"] = 0
        s2 = carve("att", 2, 3 * P)
        pT2 = carve("att", 2, 3 * P)
        sga = carve("att", 2, SEQ)
        assert top["att"] <= RT * (SEQ + 3)
        tanh_a = xr.rearrange("p a b -> p (a b)")[:, 0:RT * SEQ].rearrange("p (a b) -> p a b", a=RT)
        merged = xc.rearrange("p a b -> p (a b)")[:, 0:KD * SEQ].rearrange("p (a b) -> p a b", a=KD)
        ra_words, ui_words = (z.rearrange("p a b -> p (a b)") for z in (ra, ui))
        iqT = ra_words[:, 0:IH // 2 * SEQ].rearrange("p (a b) -> p a b", a=IH // 2)
        ikT = ra_words[:, IH // 2 * SEQ:(IH // 2 + 1) * SEQ]
        ropetmp = ui_words[:, 0:1024].rearrange("p (a b) -> p a b", a=2)
        vv = h

        banks = [ctx.enter_context(nc.psum_tensor(f"bank{b}", [P, 512], F32)) for b in range(BANKS)]
        psum_full = [sem(f"psum_full_{b}") for b in range(BANKS)]
        psum_read = [sem(f"psum_read_{b}") for b in range(BANKS)]

        x_loaded = sem("x_loaded")
        consts_loaded = sem("consts_loaded")
        gain_loaded = sem("gain_loaded")
        router_loaded = sem("router_loaded")
        masks_ready = sem("masks_ready")
        own_dve = sem("dve_steps")
        own_act = sem("act_steps")
        own_pool = sem("pool_steps")
        sumsq_ready = sem("sumsq_ready")
        mean_ready = sem("mean_ready")
        rstd_ready = sem("rstd_ready")
        h_ready = sem("h_ready")
        roped1 = sem("roped1")
        conv_out = sem("conv_out")
        conv_sq = sem("conv_sq")
        negmax = sem("negmax")
        exps = sem("exps")
        probs = sem("probs")
        route_exp_in = sem("route_exp_in")
        route_exp_out = sem("route_exp_out")
        assign_ready = sem("assign_ready")
        trips_ready = sem("trips_ready")
        angles_ready = sem("angles_ready")
        tables2_ready = sem("tables2_ready")
        lam_in = sem("lam_in")
        lam_exp = sem("lam_exp")
        decay_ready = sem("decay_ready")
        out_stored = sem("out_stored")
        SEGS = ["mix0", "moe0", "mix1", "moe1", "b2"]
        w_loaded = {s: [sem(f"w_loaded_{s}_{k}") for k in range(RING)] for s in SEGS}
        moe = [{n: sem(f"moe{l}_{n}") for n in ["picked", "full4", "full5", "full6", "full7", "read4", "read5",
                                                "read6", "read7", "silu", "scattered", "dve", "act", "x_ready"]}
               for l in range(DEPTH)]
        roped2 = sem("roped2")
        conv2_done = sem("conv2_done")
        tanh_ready = sem("tanh_ready")
        tanh_used = sem("tanh_used")
        root_ready = sem("root_ready")
        hidden_ready = sem("hidden_ready")
        relu_done = sem("relu_done")
        negmax2 = sem("negmax2")
        exps2 = sem("exps2")
        probs2 = sem("probs2")
        silu_gr = sem("silu_gr")
        sig_ready = sem("sig_ready")
        merged_ready = sem("merged_ready")

        def bank(name):
            return banks[TILE[name] % BANKS]

        def uses(name):
            return TILE[name] // BANKS + 1

        def full(eng, name):
            eng.wait_ge(psum_full[TILE[name] % BANKS], uses(name))

        def emptied(eng, name):
            eng.wait_ge(psum_read[TILE[name] % BANKS], uses(name))

        def col(layer, name, k, rows_=slice(0, P)):
            a, n = COLS[name]
            return cols[rows_, layer, a + k:a + k + 1]

        SINK0 = DEPTH * ROUTER_W
        INV0 = SINK0 + DEPTH * HEADS

        def mixer_piece(j):
            return (j + RING - 1) % RING

        def mixer_count(j):
            return 32 if j == RING else 16

        MIX_PIECES = [("in", 0, 512), ("in", QW, 2 * KVW), ("in", QW + 2 * KVW, CW), ("in", QW + 2 * KVW + CW, CW),
                      ("in", QW + 2 * KVW + 2 * CW, CW), ("out", 0, 512), ("out", 512, 512)]
        MIX_LAST = [("q", 1), ("kv", 1), ("gb", 1), ("gc", 1), ("u", 1), ("out1", 3), ("out1", 7)]
        B2_PIECES = ([("in", XR2, 512), ("in", XR2 + 512, 512), ("in", XR2 + 1024, 384)]
                     + [("in", Q2, 512), ("in", Q2 + 512, 512), ("in", K2, 512), ("in", K2 + 512, 512)]
                     + [("in", IQ2, 512), ("in", IQ2 + 512, 512), ("in", IK2, 128)]
                     + [("in", V2, 512), ("in", V2 + 512, 512)]
                     + [("lru", 0, NBP * P), ("lru", 1, NBP * P)]
                     + [("in", GR2, 512), ("in", GR2 + 512, 512), ("in", GR2 + 1024, 384)]
                     + [("in", GA2, 512), ("in", GA2 + 512, 512)]
                     + [("in", MA2, 512), ("oa", 0, 512), ("in", MA2 + 512, 512), ("oa", 512, 512)]
                     + [("in", MB2, 512), ("or", 0, 256), ("or", 256, 256)]
                     + [("in", MB2 + 512, 512), ("or", 512, 256), ("or", 768, 256)]
                     + [("o", 0, 512), ("o", 512, 512)])
        NB2 = len(B2_PIECES)
        B2_LAST = ([("xr", 1), ("xr", 3), ("xr", 5)] + [("rope", c) for c in (1, 3, 5, 7, 9, 11, 13)]
                   + [("v", 1), ("v", 3)] + [("gates", RT - 1)] * 2 + [("gr", 1), ("gr", 3), ("gr", 5), ("ga", 3), ("ga", 7)]
                   + [("ma", 3), ("ma", 3), ("ma", 7), ("ma", 7), ("mb", 3), ("mb", 1), ("mb", 3), ("mb", 7), ("mb", 5),
                      ("mb", 7), ("out2", 1), ("out2", 3)])
        PXR, PROPE, PV, PLRU, PGR, PGA, PMA, PMB, PO = 0, 3, 10, 12, 14, 17, 19, 23, 29

        def piece(slot, k, n):
            return ring[:, slot, 0:k * n].rearrange("p (k n) -> p k n", k=k)

        MOE_TILES = 8 + 6 * 4
        PER_BANK = MOE_TILES // MOE_BANKS

        def pair_last(p, idx):
            return 8 + 6 * p + (1, 1, 2, 2, 5, 5)[idx]

        block = ctx.enter_context(nc.Block())

        @block.sync
        def _(sp):
            sp.dma_start(x[:], x_in.rearrange("(t p) d -> p t d", p=P)).then_inc(x_loaded, 16)

            def left_by_experts(layer, slot):
                m = pair_last(3, slot)
                sp.wait_ge(moe[layer][f"full{4 + m % 4}"], last_turn * PER_BANK + (m // 4 + 1))

            def mixer(layer):
                for j, (kind, c0, n) in enumerate(MIX_PIECES):
                    slot = mixer_piece(j)
                    if j == RING:
                        full(sp, ("q", layer, 1))
                    elif layer > 0:
                        left_by_experts(layer - 1, slot)
                    src = (w_in if kind == "in" else w_out)[layer].rearrange("(k p) n -> p k n", p=P)
                    sp.dma_start(piece(slot, KD, n), src[:, :, c0:c0 + n]).then_inc(w_loaded[f"mix{layer}"][slot], 16)

            def expert_piece(layer, e0, p, idx):
                e = e0 + (2 * p + (idx % 2 if idx >= 4 else idx // 2))
                if idx >= 4:
                    src = w_down[layer].rearrange("e (k p) n -> e p k n", p=P)
                    dst = piece(idx, FE, D)
                else:
                    src = (w_gate if idx % 2 == 0 else w_up)[layer].rearrange("e (k p) n -> e p k n", p=P)
                    dst = piece(idx, KD, DE)
                sp.dma_start(dst, src[e]).then_inc(w_loaded[f"moe{layer}"][idx], 16)

            def experts(layer):
                for p in range(4):
                    for idx in range(6):
                        if p == 0:
                            nm, last = MIX_LAST[idx + 1]
                            full(sp, (nm, layer, last))
                        else:
                            m = pair_last(p - 1, idx)
                            sp.wait_ge(moe[layer][f"full{4 + m % 4}"], m // 4 + 1)
                        expert_piece(layer, 0, p, idx)
                sp.wait_ge(trips_ready, layer + 1)
                last = sp.value_load(trips_i[0:1, 1:2], min_val=GROUPS - 1, max_val=GROUPS * ROUNDS - 1)
                with sp.Fori(0, last) as i:
                    g = ((i + 1) % GROUPS) * PER_GROUP
                    for p in range(4):
                        for idx in range(6):
                            m = pair_last((p - 1) % 4, idx)
                            sp.wait_ge(moe[layer][f"full{4 + m % 4}"],
                                       i * PER_BANK + (m // 4 + 1 + (PER_BANK if p > 0 else 0)))
                            expert_piece(layer, g, p, idx)
                return last

            last_turn = None
            for layer in range(DEPTH):
                mixer(layer)
                last_turn = experts(layer)
            for layer in range(DEPTH):
                for j, (kind, c0, n) in enumerate(B2_PIECES):
                    at = layer * NB2 + j
                    slot = at % RING
                    if at < RING:
                        left_by_experts(DEPTH - 1, slot)
                    else:
                        nm, last = B2_LAST[(at - RING) % NB2]
                        full(sp, (nm, (at - RING) // NB2, last))
                    if kind == "lru":
                        dst, src = ring[:, slot, 0:n], w_lru[layer, c0]
                    elif kind == "or":
                        dst = piece(slot, RT, n)
                        src = w_or[layer].rearrange("(k p) n -> p k n", p=P)[:, :, c0:c0 + n]
                    else:
                        w = {"in": w_in2, "oa": w_oa, "o": w_o}[kind]
                        dst = piece(slot, KD, n)
                        src = w[layer].rearrange("(k p) n -> p k n", p=P)[:, :, c0:c0 + n]
                    sp.dma_start(dst, src).then_inc(w_loaded["b2"][slot], 16)
            sp.wait_ge(h_ready, 2 * FINAL + 2)
            sp.dma_start(out.rearrange("(t p) d -> p t d", p=P), h[:]).then_inc(out_stored, 16)
            sp.wait_ge(out_stored, 16)

        @block.gpsimd
        def _(pool):
            S = Steps(pool, own_pool)
            pool.dma_start(cols[:], cols_in).then_inc(consts_loaded, 16)
            pool.dma_start(rows[:], rows_in).then_inc(consts_loaded, 16)
            pool.dma_start(cos1, rope1_in[:, 0]).then_inc(consts_loaded, 16)
            pool.dma_start(sin1, rope1_in[:, 1]).then_inc(consts_loaded, 16)
            pool.dma_start(pos_i[:], positions).then_inc(consts_loaded, 16)
            S(pool.memset(ident[:], 0.0))
            S(pool.memset(ones[:], 1.0))
            S(pool.memset(zeros[:], 0.0))
            S(pool.memset(power[:], -0.5))
            S(pool.memset(window, 0.0))
            S(pool.memset(w_router, 0.0))
            S.settle()
            S(pool.affine_select(out=ident[:], in_=ident[:], compare_op=ALU.not_equal, fill=1.0, base=0,
                                 pattern=[[-1, P]], channel_multiplier=1))
            S(pool.affine_select(out=before[:], in_=ones[:], compare_op=ALU.is_gt, fill=0.0, base=0,
                                 pattern=[[1, P]], channel_multiplier=-1))
            S(pool.affine_select(out=window, in_=window, compare_op=ALU.is_ge, fill=NEG, base=P,
                                 pattern=[[P, NT], [-1, SEQ]], channel_multiplier=1))
            S.settle()
            S(pool.affine_select(out=window, in_=window, compare_op=ALU.is_ge, fill=NEG, base=P,
                                 pattern=[[-P, NT], [1, SEQ]], channel_multiplier=-1))
            S(pool.iota(iota_i[:], [[1, SLOTS]], base=0, channel_multiplier=0))
            S.settle()
            pool.tensor_copy(iota_f[:], iota_i[:]).then_inc(masks_ready, 1)
            pool.dma_start(w_router[:, :, 0:ROUTER_W],
                           router_in[0].rearrange("(k p) n -> p k n", p=P)).then_inc(router_loaded, 16)

            def inverse_root(src, dst, n, stage=None):
                if stage is not None:
                    pool.wait_ge(mean_ready, stage + 1)
                pool.tensor_tensor(dst, src, power[:, 0:n], ALU.pow).then_inc(rstd_ready, 1)

            for layer in range(DEPTH):
                inverse_root(stat[:, 2:4], stat[:, 4:6], 2, 2 * layer)
                emptied(pool, ("u", layer, 1))
                pool.wait_ge(consts_loaded, 80)
                for f in range(4):
                    if f == 0:
                        emptied(pool, ("gb", layer, 1))
                    S(pool.tensor_scalar(yc[:, f], cu[:, f, 0:SEQ], col(layer, "conv1", f), None, ALU.mult))
                    for tap in (1, 2):
                        S.settle()
                        S(pool.tensor_scalar(yc_t, cu[:, f, tap:tap + SEQ], col(layer, "conv1", 4 * tap + f), None,
                                             ALU.mult))
                        S.settle()
                        S(pool.tensor_tensor(yc[:, f], yc[:, f], yc_t, ALU.add))
                    S.settle()
                    S(pool.tensor_tensor(yc[:, f], yc[:, f], gb[:, f], ALU.mult), conv_out)
                emptied(pool, ("ss", layer, 0))
                inverse_root(stat[:, 8:12], stat[:, 12:16], 4)
                inverse_root(stat[:, 2:4], stat[:, 4:6], 2, 2 * layer + 1)
                if layer + 1 < DEPTH:
                    full(pool, ("rank", layer, 0))
                    pool.dma_start(w_router[:, :, 0:ROUTER_W],
                                   router_in[layer + 1].rearrange("(k p) n -> p k n", p=P)).then_inc(router_loaded, 16)
            for stage in range(BETWEEN, FINAL + 1):
                inverse_root(stat[:, 2:4], stat[:, 4:6], 2, stage)

        @block.scalar
        def _(act):
            S = Steps(act, own_act)

            def load_gain(stage):
                if stage > 0:
                    act.wait_ge(h_ready, 2 * stage)
                act.dma_start(gain[:], gains_in[stage]).then_inc(gain_loaded, 16)

            def squares(stage):
                for t in range(NT):
                    S.settle()
                    S(act.activation(h[:, t], x[:, t], ACT.Square, accum_out=stat[:, t:t + 1]),
                      sumsq_ready if t == NT - 1 else None)

            def even_hT(stage):
                for j in (0, 2):
                    full(act, ("hT", stage, j))
                    act.copy(hT[:, 2 * j:2 * j + 2].rearrange("p a b -> p (a b)"), bank(("hT", stage, j))[:]
                             ).then_inc(psum_read[TILE[("hT", stage, j)] % BANKS], 1)

            def empty(name, dst, src, func=ACT.Copy, **kw):
                full(act, name)
                act.activation(dst, src, func, **kw).then_inc(psum_read[TILE[name] % BANKS], 1)

            load_gain(0)
            act.wait_ge(x_loaded, 16)
            squares(0)
            act.wait_ge(consts_loaded, 80)
            act.wait_ge(angles_ready, 1)
            S(act.activation(sin2[:], sin2[:], ACT.Sin))
            S(act.activation(cos2[:], cos2[:], ACT.Sin), tables2_ready)
            act.wait_ge(lam_in, 1)
            act.activation(lam_t[:, 1], lam_t[:, 0], ACT.Exp, scale=-1.0).then_inc(lam_exp, 1)

            for layer in range(DEPTH):
                if layer > 0:
                    act.wait_ge(moe[layer - 1]["x_ready"], 1)
                    squares(2 * layer)
                even_hT(2 * layer)
                load_gain(2 * layer + 1)
                for t in range(NT):
                    empty(("q", layer, t), qkv[:, t, 0:QW], bank(("q", layer, t))[:])
                for t in range(NT):
                    empty(("kv", layer, t), qkv[:, t, QW:], bank(("kv", layer, t))[:, 0:2 * KVW])
                for nm, dst in (("gb", gb), ("gc", gc)):
                    for j in range(2):
                        empty((nm, layer, j), dst[:, 2 * j:2 * j + 2].rearrange("p a b -> p (a b)"),
                              bank((nm, layer, j))[:])
                for j in range(2):
                    empty(("qkT", layer, j), qT1[:, 2 * j:2 * j + 2].rearrange("p a b -> p (a b)"),
                          bank(("qkT", layer, j))[:])
                empty(("qkT", layer, 2), kT1.rearrange("p a b -> p (a b)"), bank(("qkT", layer, 2))[:])

                def exponentials(hh):
                    act.wait_ge(negmax, layer * HEADS + hh + 1)
                    st = stat[:, 16 + 8 * (hh % 2):24 + 8 * (hh % 2)]
                    for qb in range(NT):
                        S(act.activation(s1[:, hh % 2, qb], s1[:, hh % 2, qb], ACT.Exp, bias=st[:, 2 + qb:3 + qb],
                                         accum_out=st[:, 4 + qb:5 + qb]))
                    S(act.activation(st[:, 6:8], st[:, 2:4], ACT.Exp,
                                     bias=rows[:, SINK0 + layer * HEADS + hh:SINK0 + layer * HEADS + hh + 1]), exps)

                exponentials(0)
                for hh in range(HEADS):
                    if hh + 1 < HEADS:
                        exponentials(hh + 1)
                    empty(("PT1", layer, hh), pT1[:, hh % 2].rearrange("p a b -> p (a b)"),
                          bank(("PT1", layer, hh))[:])
                    if hh % 2 == 1:
                        j = hh // 2
                        full(act, ("Y1", layer, j))
                        S(act.activation(sq[:, j], bank(("Y1", layer, j))[:, 0:SEQ], ACT.Square))
                        empty(("Y1", layer, j), yT[:, j], bank(("Y1", layer, j))[:, 0:SEQ], ACT.Copy,
                              scale=col(layer, "g_attn", j))
                for f in range(4):
                    act.wait_ge(conv_out, 4 * layer + f + 1)
                    S(act.activation(sq[:, 4 + f], yc[:, f], ACT.Square))
                    S(act.activation(yT[:, 4 + f], yc[:, f], ACT.Copy, scale=col(layer, "g_conv", f)), conv_sq)

                emptied(act, ("out1", layer, 7))
                squares(2 * layer + 1)
                even_hT(2 * layer + 1)
                load_gain(2 * layer + 2)
                act.wait_ge(route_exp_in, 2 * layer + 1)
                act.activation(small[:, 3, :, 0:GROUPS], small[:, 2, :, 0:GROUPS], ACT.Exp).then_inc(route_exp_out, 1)
                act.wait_ge(route_exp_in, 2 * layer + 2)
                act.activation(stat[:, 40:42], stat[:, 38:40], ACT.Exp).then_inc(route_exp_out, 1)
                act.wait_ge(trips_ready, layer + 1)
                n = act.value_load(trips_i[0:1, 0:1], min_val=GROUPS, max_val=GROUPS * ROUNDS)
                M = moe[layer]
                with act.Fori(0, n) as i:
                    def m_full(m):
                        act.wait_ge(M[f"full{4 + m % 4}"], i * PER_BANK + (m // 4 + 1))

                    def m_bank(m):
                        return banks[4 + m % 4]

                    for k in range(0, KD, 2):
                        m_full(k)
                        act.copy(xg[:, k], m_bank(k)[:]).then_inc(M[f"read{4 + k % 4}"], 1)
                    for p in range(4):
                        b = p % 2
                        for side in range(2):
                            m = 8 + 6 * p + 1 + side
                            up, gate = (slice(0, 64), slice(64, P)) if side == 0 else (slice(64, P), slice(0, 64))
                            m_full(m)
                            act.activation(silu_g[up, b], m_bank(m)[gate, :], ACT.Silu).then_inc(M["silu"], 1)
                        m = 8 + 6 * p + 3
                        m_full(m)
                        act.copy(hidT[:, b], m_bank(m)[:]).then_inc(M[f"read{4 + m % 4}"], 1)
                        m = 8 + 6 * p + 4
                        m_full(m)
                        act.copy(ysb[:, b, 0:512], m_bank(m)[:]).then_inc(M[f"read{4 + m % 4}"], 1)

            act.wait_ge(moe[DEPTH - 1]["x_ready"], 1)
            squares(BETWEEN)
            load_gain(SECOND)
            for layer in range(DEPTH):
                stage = SECOND + layer
                if layer == 0:
                    act.wait_ge(h_ready, 2 * SECOND)
                else:
                    emptied(act, ("out2", layer - 1, 3))
                squares(stage)
                even_hT(stage)
                load_gain(stage + 1)
                for j in range(6):
                    w = min(2, RT - 2 * j)
                    empty(("xr", layer, j), xr[:, 2 * j:2 * j + w, TAPS2 - 1:],
                          bank(("xr", layer, j))[:, 0:w * SEQ].rearrange("p (a b) -> p a b", a=w))
                for c in range(14):
                    name = ("ropeT", layer, c)
                    if c < 12:
                        dst = (qT, kT, iqT)[c // 4]
                        pc, t = (c % 4) // 2, c % 2
                        empty(name, dst[:, 4 * pc:4 * pc + 4, t * P:(t + 1) * P],
                              bank(name)[:].rearrange("p (a b) -> p a b", a=4))
                    else:
                        t = c - 12
                        empty(name, ikT[:, t * P:(t + 1) * P], bank(name)[:, 0:P])
                for j in range(4):
                    pc, t = j // 2, j % 2
                    empty(("v", layer, j), vv[:, t, pc * 512:(pc + 1) * 512], bank(("v", layer, j))[:])
                for j in range(12):
                    full(act, ("dots", layer, j))
                    if layer * 12 + j >= 2:
                        act.wait_ge(relu_done, layer * 12 + j - 1)
                    empty(("dots", layer, j), relu[:, j % 2], bank(("dots", layer, j))[:], ACT.Relu)
                act.wait_ge(roped2, 14 * (layer + 1))
                for j in range(RT):
                    full(act, ("gates", layer, j))
                    S(act.activation(ra[:, j], bank(("gates", layer, j))[:, 0:SEQ], ACT.Sigmoid,
                                     bias=col(layer, "b_rg", j)))
                    empty(("gates", layer, j), ui[:, j], bank(("gates", layer, j))[:, SEQ:2 * SEQ], ACT.Sigmoid,
                          bias=col(layer, "b_ig", j))
                S.settle()
                act.wait_ge(decay_ready, 1)
                act.wait_ge(conv2_done, layer + 1)
                for j in range(RT):
                    S(act.activation(tanh_a[:, j], ra[:, j], ACT.Tanh, scale=decay[:, layer, j:j + 1]),
                      tanh_ready if j == RT - 1 else None)
                act.wait_ge(relu_done, 12 * (layer + 1))
                act.wait_ge(tanh_used, layer + 1)
                S(act.activation(tanh_a, tanh_a, ACT.Sqrt), root_ready)
                for j in range(6):
                    w = min(2, RT - 2 * j)
                    name = ("gr", layer, j)
                    full(act, name)
                    if j >= 2:
                        emptied(act, ("gr", layer, j - 2))
                    S(act.activation(roped[:, j % 2, 0:w * SEQ], bank(name)[:, 0:w * SEQ], ACT.Silu), silu_gr)

                def exponentials2(hh):
                    act.wait_ge(negmax2, layer * HEADS + hh + 1)
                    st = stat[:, 16 + 8 * (hh % 2):24 + 8 * (hh % 2)]
                    b = hh % 2
                    S(act.activation(s2[:, b, 0:P], s2[:, b, 0:P], ACT.Exp, bias=st[:, 2:3], accum_out=st[:, 4:5]))
                    S(act.activation(s2[:, b, P:], s2[:, b, P:], ACT.Exp, bias=st[:, 3:4], accum_out=st[:, 5:6]), exps2)

                exponentials2(0)
                for hh in range(HEADS):
                    if hh >= 2:
                        emptied(act, ("Y2", layer, hh - 2))
                    empty(("ga", layer, hh), sga[:, hh % 2], bank(("ga", layer, hh))[:, 0:SEQ], ACT.Silu)
                    if hh + 1 < HEADS:
                        exponentials2(hh + 1)
                    empty(("PT2", layer, hh), pT2[:, hh % 2], bank(("PT2", layer, hh))[:, 0:3 * P])
                for nm in ("ma", "mb"):
                    for j in range(8):
                        full(act, (nm, layer, j))
                        if (nm, j) not in (("ma", 0), ("ma", 1)):
                            emptied(act, (nm, layer, j - 2) if j >= 2 else ("ma", layer, 6 + j))
                        S(act.activation(s2.rearrange("p a b -> p (a b)")[:, (j % 2) * SEQ:(j % 2 + 1) * SEQ],
                                         bank((nm, layer, j))[:, 0:SEQ], ACT.Sigmoid), sig_ready)
            emptied(act, ("out2", DEPTH - 1, 3))
            squares(FINAL)

        @block.vector
        def _(dve):
            S = Steps(dve, own_dve)

            def normalise(stage, dst=h):
                k = {0: 1, 1: 3, 2: 4, 3: 6}.get(stage, stage + 3)
                dve.wait_ge(sumsq_ready, stage + 1)
                dve.tensor_scalar(stat[:, 2:4], stat[:, 0:2], 1.0 / D, EPS, ALU.mult, ALU.add).then_inc(mean_ready, 1)
                dve.wait_ge(rstd_ready, k)
                dve.wait_ge(gain_loaded, 16 * (stage + 1))
                for t in range(NT):
                    S(dve.scalar_tensor_tensor(out=dst[:, t], in0=x[:, t], scalar=stat[:, 4 + t:5 + t], in1=gain[:],
                                               op0=ALU.mult, op1=ALU.mult), h_ready)

            def odd_hT(stage):
                for j in (1, 3):
                    name = ("hT", stage, j)
                    full(dve, name)
                    dve.tensor_copy(hT[:, 2 * j:2 * j + 2].rearrange("p a b -> p (a b)"), bank(name)[:]
                                    ).then_inc(psum_read[TILE[name] % BANKS], 1)

            dve.wait_ge(consts_loaded, 80)
            dve.wait_ge(x_loaded, 16)
            normalise(0)
            S(dve.tensor_copy(pos_f[:], pos_i[:]))
            S.settle()
            for t in range(NT):
                S(dve.tensor_scalar(ang[:, t], rows[:, INV0:INV0 + INV2], pos_f[:, t:t + 1], None, ALU.mult))
            S.settle()
            S(dve.tensor_scalar(cos2[:], ang[:], float(1.0 / (2 * np.pi)), ROUNDER, ALU.mult, ALU.add))
            S.settle()
            S(dve.tensor_scalar(cos2[:], cos2[:], ROUNDER, None, ALU.subtract))
            for part in TWO_PI_PARTS:
                S.settle()
                S(dve.scalar_tensor_tensor(out=ang[:], in0=cos2[:], scalar=-part, in1=ang[:],
                                           op0=ALU.mult, op1=ALU.add))
            S.settle()
            S(dve.tensor_scalar(sin2[:], ang[:], 3.1415925, -3.1415925, ALU.min, ALU.max))
            S.settle()
            S(dve.scalar_tensor_tensor(out=cos2[:], in0=sin2[:], scalar=-1.0, in1=sin2[:], op0=ALU.mult, op1=ALU.max))
            S.settle()
            S(dve.tensor_scalar(cos2[:], cos2[:], -1.0, float(np.pi / 2), ALU.mult, ALU.add), angles_ready)
            lam = cols[:, :, COLS["lam"][0]:COLS["lam"][0] + RT]
            S(dve.tensor_scalar(lam_t[:, 3], lam, -1.0, None, ALU.mult))
            S.settle()
            dve.tensor_tensor(lam_t[:, 0], lam, lam_t[:, 3], ALU.max).then_inc(lam_in, 1)
            dve.wait_ge(lam_exp, 1)
            S(dve.tensor_scalar(lam_t[:, 2], lam_t[:, 1], 2.0, None, ALU.add))
            S.settle()
            S(dve.reciprocal(lam_t[:, 2], lam_t[:, 2]))
            S.settle()
            S(dve.tensor_tensor(lam_t[:, 1], lam_t[:, 1], lam_t[:, 2], ALU.mult))
            S.settle()
            S(dve.tensor_tensor(lam_t[:, 2], lam_t[:, 1], lam_t[:, 1], ALU.mult))
            S.settle()
            S(dve.tensor_scalar(lam_t[:, 0], lam_t[:, 2], 2.0 / 17, None, ALU.mult))
            for n in (15, 13, 11, 9, 7, 5, 3):
                S.settle()
                S(dve.scalar_tensor_tensor(out=lam_t[:, 0], in0=lam_t[:, 0], scalar=2.0 / n, in1=lam_t[:, 2],
                                           op0=ALU.add, op1=ALU.mult))
            S.settle()
            S(dve.scalar_tensor_tensor(out=lam_t[:, 0], in0=lam_t[:, 0], scalar=2.0, in1=lam_t[:, 1],
                                       op0=ALU.add, op1=ALU.mult))
            S.settle()
            S(dve.scalar_tensor_tensor(out=lam_t[:, 3], in0=lam_t[:, 3], scalar=0.0, in1=lam_t[:, 0],
                                       op0=ALU.max, op1=ALU.add))
            S.settle()
            S(dve.tensor_scalar(decay[:], lam_t[:, 3], LRU_C / 2, None, ALU.mult), decay_ready)
            dve.wait_ge(masks_ready, 1)

            def first_mixer(layer):
                stage = 2 * layer
                if layer > 0:
                    normalise(stage)
                odd_hT(stage)
                for t in range(NT):
                    emptied(dve, ("q", layer, t))
                    emptied(dve, ("kv", layer, t))
                heads = [qkv[:, t, 0:QW + KVW].rearrange("p (h d) -> p h d", d=HD1) for t in range(NT)]
                tab = [[z.rearrange("p (t h d) -> p t h d", t=NT, d=ROT1)[:, t] for t in range(NT)] for z in (cos1, sin1)]
                tmp = [[rt1[:, z].rearrange("p (t h d) -> p t h d", t=NT, d=ROT1)[:, t] for t in range(NT)]
                       for z in range(4)]
                for t in range(NT):
                    a, b = heads[t][:, :, 0:ROT1], heads[t][:, :, ROT1:2 * ROT1]
                    S(dve.tensor_tensor(tmp[0][t], a, tab[0][t], ALU.mult))
                    S(dve.tensor_tensor(tmp[1][t], b, tab[1][t], ALU.mult))
                    S(dve.tensor_tensor(tmp[2][t], b, tab[0][t], ALU.mult))
                    S(dve.tensor_tensor(tmp[3][t], a, tab[1][t], ALU.mult))
                S.settle()
                for t in range(NT):
                    a, b = heads[t][:, :, 0:ROT1], heads[t][:, :, ROT1:2 * ROT1]
                    S(dve.tensor_tensor(a, tmp[0][t], tmp[1][t], ALU.subtract))
                    S(dve.tensor_tensor(b, tmp[2][t], tmp[3][t], ALU.add))
                S.settle()
                S(dve.tensor_copy(kswap[:, :, 0:HD1], qkv[:, :, QW + HD1:QW + KVW]))
                S(dve.tensor_copy(kswap[:, :, HD1:], qkv[:, :, QW:QW + HD1]), roped1)
                S(dve.memset(cu[:, :, 0:1], 0.0))
                S(dve.memset(cu[:, :, SEQ + 1:], 0.0))
                for j in range(2):
                    name = ("u", layer, j)
                    emptied(dve, ("gc", layer, j))
                    full(dve, name)
                    S.settle()
                    S.marks(dve.tensor_tensor(cu[:, 2 * j:2 * j + 2, 1:SEQ + 1],
                                              bank(name)[:].rearrange("p (a b) -> p a b", a=2),
                                              gc[:, 2 * j:2 * j + 2], ALU.mult),
                            psum_read[TILE[name] % BANKS], uses(name))
                sink = rows[:, SINK0 + layer * HEADS:SINK0 + (layer + 1) * HEADS]

                def logits(hh):
                    name = ("S1", layer, hh)
                    st = stat[:, 16 + 8 * (hh % 2):24 + 8 * (hh % 2)]
                    full(dve, name)
                    if hh >= 2:
                        full(dve, ("PT1", layer, hh - 2))
                    S.marks(dve.scalar_tensor_tensor(out=s1[:, hh % 2], in0=bank(name)[:].rearrange("p (a b) -> p a b", a=2),
                                                     scalar=HD1 ** -0.5, in1=window, op0=ALU.mult, op1=ALU.add),
                            psum_read[TILE[name] % BANKS], uses(name))
                    S.settle()
                    S(dve.tensor_reduce(st[:, 0:2], s1[:, hh % 2], AX.X, ALU.max))
                    S.settle()
                    S(dve.tensor_scalar(st[:, 2:4], st[:, 0:2], sink[:, hh:hh + 1], -1.0, ALU.max, ALU.mult), negmax)

                def weights(hh):
                    st = stat[:, 16 + 8 * (hh % 2):24 + 8 * (hh % 2)]
                    dve.wait_ge(exps, layer * HEADS + hh + 1)
                    S(dve.tensor_tensor(st[:, 4:6], st[:, 4:6], st[:, 6:8], ALU.add))
                    S.settle()
                    S(dve.reciprocal(st[:, 4:6], st[:, 4:6]))
                    S.settle()
                    for qb in range(NT):
                        S(dve.tensor_scalar(s1[:, hh % 2, qb], s1[:, hh % 2, qb], st[:, 4 + qb:5 + qb], None, ALU.mult),
                          probs if qb == NT - 1 else None)

                logits(0)
                for hh in range(HEADS):
                    if hh + 1 < HEADS:
                        logits(hh + 1)
                    weights(hh)
                name = ("ss", layer, 0)
                full(dve, name)
                S.marks(dve.tensor_scalar(stat[:, 8:12], bank(name)[:].rearrange("p (a b) -> p a b", b=P)[:, :, 0],
                                          1.0 / CW, EPS, ALU.mult, ALU.add), psum_read[TILE[name] % BANKS], uses(name))
                dve.wait_ge(rstd_ready, 3 * layer + 2)
                for i in range(8):
                    hf, part, t = i // 4, (i // 2) % 2, i % 2
                    name = ("out1", layer, i)
                    full(dve, name)
                    S.settle()
                    xs = x[:, t, hf * 512:(hf + 1) * 512]
                    S.marks(dve.scalar_tensor_tensor(out=xs, in0=bank(name)[:], scalar=stat[:, 12 + 2 * part + t:13 + 2 * part + t],
                                                     in1=xs, op0=ALU.mult, op1=ALU.add),
                            psum_read[TILE[name] % BANKS], uses(name))
                S.settle()

            def pick_first(dst, src, mx, idx, wide, far):
                n = src.shape[-1]
                S(dve.tensor_tensor(dst, src, mx.unsqueeze(2).to_broadcast([P, NT, n]), ALU.is_equal))
                S.settle()
                S(dve.scalar_tensor_tensor(out=wide, in0=dst, scalar=-far, in1=idx, op0=ALU.mult, op1=ALU.add))
                S.settle()
                S(dve.tensor_reduce(stat[:, 42:44], wide, AX.X, ALU.min))
                S.settle()
                S(dve.tensor_tensor(dst, wide, stat[:, 42:44].unsqueeze(2).to_broadcast([P, NT, n]), ALU.is_equal))
                S.settle()

            def router(layer):
                name = ("logits", layer, 0)
                full(dve, name)
                lg = bank(name)[:, 0:2 * P].rearrange("p (t n) -> p t n", t=NT)
                bias = rows[:, layer * ROUTER_W:(layer + 1) * ROUTER_W]
                idx = iota_f[:, 0:NE]
                for t in range(NT):
                    S(dve.tensor_tensor(small[:, 0, t, 0:GROUPS], lg[:, t, 0:GROUPS], bias[:, 0:GROUPS], ALU.add))
                S(dve.tensor_tensor(small[:, 1, 0], lg[:, 0, GROUPS:ROUTER_W], bias[:, GROUPS:], ALU.add))
                S.marks(dve.tensor_tensor(small[:, 1, 1], lg[:, 1, GROUPS:ROUTER_W], bias[:, GROUPS:], ALU.add),
                        psum_read[TILE[name] % BANKS], uses(name))
                S.settle()
                gl = small[:, 0, :, 0:GROUPS]
                gmax = stat[:, 32:34]
                S(dve.tensor_reduce(gmax, gl, AX.X, ALU.max))
                S.settle()
                S(dve.tensor_tensor(small[:, 2, :, 0:GROUPS], gl, gmax.unsqueeze(2).to_broadcast([P, NT, GROUPS]),
                                    ALU.subtract), route_exp_in)
                oh = small[:, 4, :, 0:GROUPS]
                idx_g = idx[:, 0:GROUPS].unsqueeze(1).to_broadcast([P, NT, GROUPS])
                pick_first(oh, gl, gmax, idx_g, small[:, 5, :, 0:GROUPS], 64.0)
                S(dve.tensor_scalar(oh, oh, -NEG, NEG, ALU.mult, ALU.add))
                S.settle()
                for t in range(NT):
                    S(dve.tensor_tensor(small[:, 6, t].rearrange("p (g e) -> p g e", g=GROUPS),
                                        small[:, 1, t].rearrange("p (g e) -> p g e", g=GROUPS),
                                        small[:, 4, t, 0:GROUPS].unsqueeze(2).to_broadcast([P, GROUPS, PER_GROUP]), ALU.add))
                S.settle()
                idx_e = idx.unsqueeze(1).to_broadcast([P, NT, NE])
                m1, m2 = stat[:, 34:36], stat[:, 36:38]
                S(dve.tensor_reduce(m1, small[:, 6], AX.X, ALU.max))
                S.settle()
                pick_first(small[:, 7], small[:, 6], m1, idx_e, small[:, 5], 64.0)
                S(dve.scalar_tensor_tensor(out=small[:, 8], in0=small[:, 7], scalar=TAKEN, in1=small[:, 6],
                                           op0=ALU.mult, op1=ALU.add))
                S.settle()
                S(dve.tensor_reduce(m2, small[:, 8], AX.X, ALU.max))
                S.settle()
                pick_first(small[:, 9], small[:, 8], m2, idx_e, small[:, 5], 64.0)
                S(dve.tensor_tensor(small[:, 10], small[:, 7], small[:, 9], ALU.add), assign_ready)
                S(dve.tensor_tensor(stat[:, 38:40], m2, m1, ALU.subtract), route_exp_in)
                dve.wait_ge(route_exp_out, 2 * layer + 2)
                S(dve.tensor_reduce(stat[:, 44:46], small[:, 3, :, 0:GROUPS], AX.X, ALU.add))
                S(dve.tensor_scalar(stat[:, 46:48], stat[:, 40:42], 1.0, None, ALU.add))
                S.settle()
                S(dve.tensor_tensor(stat[:, 46:48], stat[:, 46:48], stat[:, 44:46], ALU.mult))
                S.settle()
                S(dve.reciprocal(stat[:, 46:48], stat[:, 46:48]))
                S.settle()
                S(dve.tensor_tensor(stat[:, 48:50], stat[:, 46:48], stat[:, 40:42], ALU.mult))
                S.settle()
                for t in range(NT):
                    S(dve.tensor_scalar(small[:, 11, t], small[:, 7, t], stat[:, 46 + t:47 + t], None, ALU.mult))
                S.settle()
                for t in range(NT):
                    S(dve.scalar_tensor_tensor(out=small[:, 12, t], in0=small[:, 9, t], scalar=stat[:, 48 + t:49 + t],
                                               in1=small[:, 11, t], op0=ALU.mult, op1=ALU.add))
                name = ("rank", layer, 0)
                full(dve, name)
                rk = bank(name)[:, 0:3 * NE].rearrange("p (a n) -> p a n", a=3)
                S(dve.scalar_tensor_tensor(out=small[:, 13], in0=rk[:, 0:NT], scalar=1.0, in1=small[:, 10],
                                           op0=ALU.add, op1=ALU.mult))
                S.settle()
                S(dve.tensor_scalar(small[:, 14], small[:, 13], -1.0, None, ALU.add))
                S.marks(dve.tensor_reduce(stat[:, 50:51], rk[:, 2], AX.X, ALU.max),
                        psum_read[TILE[name] % BANKS], uses(name))
                S.settle()
                for r in range(1, ROUNDS):
                    S(dve.tensor_scalar(stat[:, 50 + r:51 + r], stat[:, 50:51], float(SLOTS * r), float(GROUPS),
                                        ALU.is_gt, ALU.mult))
                S.settle()
                S(dve.tensor_reduce(stat[:, 54:55], stat[:, 51:50 + ROUNDS], AX.X, ALU.add))
                S.settle()
                S(dve.tensor_scalar(trips_i[:, 1:2], stat[:, 54:55], float(GROUPS - 1), None, ALU.add))
                S(dve.tensor_scalar(trips_i[:, 0:1], stat[:, 54:55], float(GROUPS), None, ALU.add), trips_ready)
                S.settle()

            def experts(layer):
                M = moe[layer]

                def picks(T, g):
                    slots = small[:, 14, :, bass.ds(g, PER_GROUP)]
                    gates = small[:, 12, :, bass.ds(g, PER_GROUP)]
                    for t in range(NT):
                        T(dve.tensor_tensor(pick[:, t], iota_f[:].unsqueeze(1).to_broadcast([P, PER_GROUP, SLOTS]),
                                            slots[:, t].unsqueeze(2).to_broadcast([P, PER_GROUP, SLOTS]), ALU.is_equal))
                    T.settle()
                    for t in range(NT):
                        T(dve.tensor_tensor(wpick[:, t], pick[:, t],
                                            gates[:, t].unsqueeze(2).to_broadcast([P, PER_GROUP, SLOTS]), ALU.mult))
                    T(dve.tensor_scalar(slots, slots, -float(SLOTS), None, ALU.add), M["picked"])
                    T.settle()

                picks(S, 0)
                n = dve.value_load(trips_i[0:1, 0:1], min_val=GROUPS, max_val=GROUPS * ROUNDS)
                STEPS = 4
                with dve.Fori(0, n) as i:
                    T = Steps(dve, M["dve"], {M["dve"].name: i * STEPS, M["picked"].name: i + 1})

                    def m_full(m):
                        dve.wait_ge(M[f"full{4 + m % 4}"], i * PER_BANK + (m // 4 + 1))

                    def m_bank(m):
                        return banks[4 + m % 4]

                    for k in range(1, KD, 2):
                        m_full(k)
                        dve.tensor_copy(xg[:, k], m_bank(k)[:]).then_inc(M[f"read{4 + k % 4}"], 1)
                    for p in range(4):
                        b = p % 2
                        m = 8 + 6 * p
                        m_full(m)
                        dve.tensor_copy(comb[:, b], m_bank(m)[:, 0:SEQ]).then_inc(M[f"read{4 + m % 4}"], 1)
                        for side in range(2):
                            m = 8 + 6 * p + 1 + side
                            up = slice(0, 64) if side == 0 else slice(64, P)
                            dve.wait_ge(M["silu"], i * 8 + (2 * p + side + 1))
                            dve.tensor_tensor(hid[up, b], silu_g[up, b], m_bank(m)[up, :], ALU.mult
                                              ).then_inc(M[f"read{4 + m % 4}"], 1)
                        if p == 3:
                            picks(T, ((i + 1) % GROUPS) * PER_GROUP)
                        m = 8 + 6 * p + 5
                        m_full(m)
                        dve.tensor_copy(ysb[:, b, 512:], m_bank(m)[:]).then_inc(M[f"read{4 + m % 4}"], 1)
                    assert T.n[M["dve"].name] == STEPS
                dve.wait_ge(M["scattered"], n)
                for t in range(NT):
                    for hf in range(2):
                        xs = x[:, t, hf * 512:(hf + 1) * 512]
                        last = dve.tensor_tensor(xs, banks[2 * t + hf][:], xs, ALU.add)
                        S(last, M["x_ready"] if (t, hf) == (NT - 1, 1) else None)
                S.settle()

            def second(layer):
                stage = SECOND + layer
                if layer == 0:
                    dve.wait_ge(tables2_ready, 1)
                normalise(stage)
                S(dve.memset(xr[:, :, 0:TAPS2 - 1], 0.0))
                odd_hT(stage)
                for j in range(RT):
                    emptied(dve, ("xr", layer, j // 2))
                    if j == 0:
                        S.settle()
                    S(dve.tensor_scalar(xc[:, j], xr[:, j, 0:SEQ], col(layer, "conv2", j), col(layer, "conv2_b", j),
                                        ALU.mult, ALU.add))
                    for tap in range(1, TAPS2):
                        S.settle()
                        S(dve.scalar_tensor_tensor(out=xc[:, j], in0=xr[:, j, tap:tap + SEQ],
                                                   scalar=col(layer, "conv2", tap * RT + j), in1=xc[:, j],
                                                   op0=ALU.mult, op1=ALU.add),
                          conv2_done if (j, tap) == (RT - 1, TAPS2 - 1) else None)
                for c in range(14):
                    name = ("rope", layer, c)
                    t = c % 2
                    full(dve, name)
                    if c >= 4:
                        full(dve, ("ropeT", layer, c - 4))
                    half = HD2 // 2 if c < 8 else ID // 2
                    t0 = 0 if c < 8 else HD2 // 2
                    nh = 512 // (2 * half) if c < 12 else 1
                    src = bank(name)[:, 0:nh * 2 * half].rearrange("p (h s d) -> p h s d", h=nh, s=2)
                    dst = roped[:, c % 4, 0:nh * 2 * half].rearrange("p (h s d) -> p h s d", h=nh, s=2)
                    tmp = ropetmp[:, c % 2, 0:nh * 2 * half].rearrange("p (h s d) -> p h s d", h=nh, s=2)
                    cs = cos2[:, t, t0:t0 + half].unsqueeze(1).to_broadcast([P, nh, half])
                    sn = sin2[:, t, t0:t0 + half].unsqueeze(1).to_broadcast([P, nh, half])
                    for s in range(2):
                        S(dve.tensor_tensor(dst[:, :, s], src[:, :, s], cs, ALU.mult))
                        S(dve.tensor_tensor(tmp[:, :, s], src[:, :, 1 - s], sn, ALU.mult))
                    if c >= 12:
                        S(dve.tensor_scalar(iw[:, t], bank(name)[:, ID:ID + IH], IH ** -0.5 * ID ** -0.5, None, ALU.mult))
                    S.settle()
                    S.marks(dve.tensor_tensor(dst[:, :, 0], dst[:, :, 0], tmp[:, :, 0], ALU.subtract),
                            psum_read[TILE[name] % BANKS], uses(name))
                    S(dve.tensor_tensor(dst[:, :, 1], dst[:, :, 1], tmp[:, :, 1], ALU.add), roped2 if c < 12 else None)
                    if c >= 12:
                        S.settle()
                        S(dve.tensor_copy(roped[:, c % 4, ID:2 * ID], roped[:, c % 4, 0:ID]), roped2)
                for j in range(12):
                    emptied(dve, ("dots", layer, j))
                    for piece_ in range(4 if j < 4 else 2):
                        if j < 4:
                            hd = 8 * (j // 2) + 2 * piece_ + j % 2
                            acc, src, qb = wk[:, 0, 0:P], relu[:, j % 2, piece_ * P:(piece_ + 1) * P], 0
                        else:
                            jj = j - 4
                            hd = 4 * (jj // 2) + 2 * piece_ + jj % 2
                            acc, src, qb = wk[:, 0, P:], relu[:, j % 2, piece_ * SEQ:(piece_ + 1) * SEQ], 1
                        lastp = piece_ == (3 if j < 4 else 1)
                        S.settle()
                        if hd == 0:
                            ins = dve.tensor_scalar(acc, src, iw[:, qb, hd:hd + 1], None, ALU.mult)
                        else:
                            ins = dve.scalar_tensor_tensor(out=acc, in0=src, scalar=iw[:, qb, hd:hd + 1], in1=acc,
                                                           op0=ALU.mult, op1=ALU.add)
                        S(ins, relu_done if lastp else None)
                S.settle()
                S(dve.tensor_tensor(wk[:, 0], wk[:, 0], causal[:], ALU.add))
                S.settle()
                for r in range(TOPK // 8):
                    a, b = r % 2, (r + 1) % 2
                    for sl in (slice(0, P), slice(P, 3 * P)):
                        o = 0 if sl.start == 0 else 8
                        S(dve.max(top8[:, o:o + 8], wk[:, a, sl]))
                    S.settle()
                    for sl in (slice(0, P), slice(P, 3 * P)):
                        o = 0 if sl.start == 0 else 8
                        S(dve.match_replace(wk[:, b, sl], top8[:, o:o + 8], wk[:, a, sl], TAKEN))
                    S.settle()
                S(dve.tensor_scalar(wk[:, 1], wk[:, 0], TAKEN, -NEG, ALU.is_equal, ALU.mult))
                S.settle()
                S(dve.scalar_tensor_tensor(out=bias2, in0=wk[:, 1], scalar=NEG, in1=causal[:], op0=ALU.add, op1=ALU.add))
                S.settle()
                emptied(dve, ("gates", layer, RT - 1))
                S(dve.tensor_tensor(ui, ui, xc, ALU.mult))
                S.settle()
                dve.wait_ge(tanh_ready, layer + 1)
                S(dve.tensor_scalar(xc, tanh_a, 1.0, None, ALU.add), tanh_used)
                S.settle()
                S(dve.reciprocal(xc, xc))
                S.settle()
                S(dve.tensor_scalar(ra, xc, 2.0, -1.0, ALU.mult, ALU.add))
                S(dve.scalar_tensor_tensor(out=ui, in0=xc, scalar=2.0, in1=ui, op0=ALU.mult, op1=ALU.mult))
                S.settle()
                dve.wait_ge(root_ready, layer + 1)
                S(dve.tensor_tensor(ui, ui, tanh_a, ALU.mult))
                S.settle()
                for j in range(RT):
                    S(dve.tensor_tensor_scan(xc[:, j], ra[:, j], ui[:, j], 0.0, ALU.mult, ALU.add),
                      hidden_ready if j == RT - 1 else None)
                S.settle()
                for j in range(6):
                    w = min(2, RT - 2 * j)
                    name = ("gr", layer, j)
                    dve.wait_ge(silu_gr, layer * 6 + j + 1)
                    S.marks(dve.tensor_tensor(ui[:, 2 * j:2 * j + w], xc[:, 2 * j:2 * j + w],
                                              roped[:, j % 2, 0:w * SEQ].rearrange("p (a b) -> p a b", a=w), ALU.mult),
                            psum_read[TILE[name] % BANKS], uses(name))
                S.settle()

                def logits(hh):
                    name = ("S2", layer, hh)
                    st = stat[:, 16 + 8 * (hh % 2):24 + 8 * (hh % 2)]
                    b = hh % 2
                    full(dve, name)
                    if hh >= 2:
                        full(dve, ("PT2", layer, hh - 2))
                    S.marks(dve.scalar_tensor_tensor(out=s2[:, b], in0=bank(name)[:, 0:3 * P], scalar=HD2 ** -0.5,
                                                     in1=bias2, op0=ALU.mult, op1=ALU.add),
                            psum_read[TILE[name] % BANKS], uses(name))
                    S.settle()
                    S(dve.tensor_reduce(st[:, 0:1], s2[:, b, 0:P], AX.X, ALU.max))
                    S(dve.tensor_reduce(st[:, 1:2], s2[:, b, P:], AX.X, ALU.max))
                    S.settle()
                    S(dve.tensor_scalar(st[:, 2:4], st[:, 0:2], -1.0, None, ALU.mult), negmax2)

                def weights(hh):
                    st = stat[:, 16 + 8 * (hh % 2):24 + 8 * (hh % 2)]
                    b = hh % 2
                    dve.wait_ge(exps2, layer * HEADS + hh + 1)
                    S(dve.reciprocal(st[:, 4:6], st[:, 4:6]))
                    S.settle()
                    S(dve.tensor_scalar(s2[:, b, 0:P], s2[:, b, 0:P], st[:, 4:5], None, ALU.mult))
                    S(dve.tensor_scalar(s2[:, b, P:], s2[:, b, P:], st[:, 5:6], None, ALU.mult), probs2)

                def gate(hh):
                    name = ("Y2", layer, hh)
                    emptied(dve, ("ga", layer, hh))
                    full(dve, name)
                    S.marks(dve.tensor_tensor(qT[:, hh], sga[:, hh % 2], bank(name)[:, 0:SEQ], ALU.mult),
                            psum_read[TILE[name] % BANKS], uses(name))

                logits(0)
                for hh in range(HEADS):
                    if hh + 1 < HEADS:
                        logits(hh + 1)
                    weights(hh)
                    gate(hh)
                sig = [s2.rearrange("p a b -> p (a b)")[:, b * SEQ:(b + 1) * SEQ] for b in range(2)]
                for j in range(8):
                    name = ("ma", layer, j)
                    dve.wait_ge(sig_ready, layer * 16 + j + 1)
                    S.marks(dve.tensor_tensor(merged[:, j], sig[j % 2], bank(name)[:, SEQ:], ALU.mult),
                            psum_read[TILE[name] % BANKS], uses(name))
                for j in range(8):
                    name = ("mb", layer, j)
                    dve.wait_ge(sig_ready, layer * 16 + 8 + j + 1)
                    S.settle()
                    S.marks(dve.tensor_tensor(pT2[:, 0, 0:SEQ], sig[j % 2], bank(name)[:, SEQ:], ALU.mult),
                            psum_read[TILE[name] % BANKS], uses(name))
                    S.settle()
                    S(dve.tensor_tensor(merged[:, j], merged[:, j], pT2[:, 0, 0:SEQ], ALU.add), merged_ready)
                for i in range(4):
                    name = ("out2", layer, i)
                    pc, t = i // 2, i % 2
                    full(dve, name)
                    xs = x[:, t, pc * 512:(pc + 1) * 512]
                    S.marks(dve.tensor_tensor(xs, bank(name)[:], xs, ALU.add), psum_read[TILE[name] % BANKS], uses(name))
                S.settle()

            for layer in range(DEPTH):
                first_mixer(layer)
                normalise(2 * layer + 1)
                odd_hT(2 * layer + 1)
                router(layer)
                experts(layer)
            S(dve.tensor_scalar(causal[:, 0:P], before[:], NEG, None, ALU.mult))
            S(dve.memset(causal[:, P:2 * P], 0.0))
            S(dve.tensor_scalar(causal[:, 2 * P:], before[:], NEG, None, ALU.mult))
            normalise(BETWEEN, x)
            S.settle()
            for layer in range(DEPTH):
                second(layer)
            normalise(FINAL)

        @block.tensor
        def _(pe):
            def claim(name):
                if TILE[name] >= BANKS:
                    pe.wait_ge(psum_read[TILE[name] % BANKS], uses(name) - 1)

            def done(mm, name):
                mm.then_inc(psum_full[TILE[name] % BANKS], 1)

            def turn_h(stage):
                pe.wait_ge(h_ready, 2 * stage + 2)
                for j in range(4):
                    name = ("hT", stage, j)
                    claim(name)
                    for k in range(2):
                        for t in range(NT):
                            f = 2 * j + k
                            mm = pe.transpose(bank(name)[:, k * SEQ + t * P:k * SEQ + (t + 1) * P],
                                              h[:, t, f * P:(f + 1) * P], ident[:])
                    done(mm, name)
                for j in range(4):
                    emptied(pe, ("hT", stage, j))

            def by_token(name, w, n, t):
                claim(name)
                for k in range(KD):
                    mm = pe.matmul(bank(name)[:, 0:n], hT[:, k, t * P:(t + 1) * P], w[:, k, 0:n],
                                   start=(k == 0), stop=(k == KD - 1))
                done(mm, name)

            def by_feature(dst, w, f, rhs=None, nk=KD):
                rhs = hT if rhs is None else rhs
                for k in range(nk):
                    mm = pe.matmul(dst, w[:, k, f * P:(f + 1) * P], rhs[:, k], start=(k == 0), stop=(k == nk - 1))
                return mm

            pe.wait_ge(masks_ready, 1)

            for layer in range(DEPTH):
                seg = f"mix{layer}"

                def arrive(j):
                    pe.wait_ge(w_loaded[seg][mixer_piece(j)], mixer_count(j))
                    return piece(mixer_piece(j), KD, MIX_PIECES[j][2])

                turn_h(2 * layer)
                w = arrive(0)
                for t in range(NT):
                    by_token(("q", layer, t), w, 512, t)
                w = arrive(1)
                for t in range(NT):
                    by_token(("kv", layer, t), w, 2 * KVW, t)
                for g, nm in enumerate(("gb", "gc", "u")):
                    w = arrive(2 + g)
                    for j in range(2):
                        name = (nm, layer, j)
                        claim(name)
                        for f in range(2):
                            mm = by_feature(bank(name)[:, f * SEQ:(f + 1) * SEQ], w, 2 * j + f)
                        done(mm, name)
                pe.wait_ge(roped1, layer + 1)
                for j in range(3):
                    name = ("qkT", layer, j)
                    claim(name)
                    for k in range(2):
                        for t in range(NT):
                            src = (qkv[:, t, (2 * j + k) * P:(2 * j + k + 1) * P] if j < 2 else
                                   (qkv[:, t, QW:QW + KVW] if k == 0 else kswap[:, t]))
                            mm = pe.transpose(bank(name)[:, k * SEQ + t * P:k * SEQ + (t + 1) * P], src, ident[:])
                    done(mm, name)
                for j in range(3):
                    emptied(pe, ("qkT", layer, j))

                def scores(hh):
                    name = ("S1", layer, hh)
                    claim(name)
                    r = slice(64 * (hh % 2), 64 * (hh % 2) + 64)
                    kk = kT1[r, 0 if hh % 2 == hh // 4 else 1]
                    for qb in range(NT):
                        mm = pe.matmul(bank(name)[:, qb * SEQ:(qb + 1) * SEQ], qT1[r, hh // 2, qb * P:(qb + 1) * P], kk,
                                       start=True, stop=True)
                    done(mm, name)

                scores(0)
                for hh in range(HEADS):
                    if hh + 1 < HEADS:
                        scores(hh + 1)
                    name = ("PT1", layer, hh)
                    claim(name)
                    pe.wait_ge(probs, layer * HEADS + hh + 1)
                    for kb in range(NT):
                        for qb in range(NT):
                            mm = pe.transpose(bank(name)[:, kb * SEQ + qb * P:kb * SEQ + (qb + 1) * P],
                                              s1[:, hh % 2, qb, kb * P:(kb + 1) * P], ident[:])
                    done(mm, name)
                    emptied(pe, name)
                    yn = ("Y1", layer, hh // 2)
                    if hh % 2 == 0:
                        claim(yn)
                    r = slice(64 * (hh % 2), 64 * (hh % 2) + 64)
                    v0 = QW + KVW + (hh // 4) * HD1
                    for kb in range(NT):
                        mm = pe.matmul(bank(yn)[r, 0:SEQ], qkv[:, kb, v0:v0 + HD1], pT1[:, hh % 2, kb],
                                       start=(kb == 0), stop=(kb == NT - 1))
                    if hh % 2 == 1:
                        done(mm, yn)
                for j in range(4):
                    emptied(pe, ("Y1", layer, j))
                pe.wait_ge(conv_sq, 4 * layer + 4)
                name = ("ss", layer, 0)
                claim(name)
                for part in range(2):
                    for t in range(NT):
                        o = (2 * part + t) * P
                        for j in range(4):
                            mm = pe.matmul(bank(name)[:, o:o + P], sq[:, 4 * part + j, t * P:(t + 1) * P], ones[:],
                                           start=(j == 0), stop=(j == 3))
                done(mm, name)
                for i in range(8):
                    hf, part, t = i // 4, (i // 2) % 2, i % 2
                    name = ("out1", layer, i)
                    if i % 4 == 0:
                        w = arrive(5 + hf)
                    claim(name)
                    for j in range(4):
                        mm = pe.matmul(bank(name)[:], yT[:, 4 * part + j, t * P:(t + 1) * P], w[:, 4 * part + j],
                                       start=(j == 0), stop=(j == 3))
                    done(mm, name)

                turn_h(2 * layer + 1)
                pe.wait_ge(router_loaded, 16 * (layer + 1))
                name = ("logits", layer, 0)
                claim(name)
                for t in range(NT):
                    for k in range(KD):
                        mm = pe.matmul(bank(name)[:, t * P:(t + 1) * P], hT[:, k, t * P:(t + 1) * P], w_router[:, k],
                                       start=(k == 0), stop=(k == KD - 1))
                done(mm, name)
                pe.wait_ge(assign_ready, layer + 1)
                name = ("rank", layer, 0)
                claim(name)
                A = small[:, 10]
                pe.matmul(bank(name)[:, 0:NE], before[:], A[:, 0], start=True, stop=True)
                pe.matmul(bank(name)[:, NE:2 * NE], before[:], A[:, 1], start=True, stop=False)
                pe.matmul(bank(name)[:, NE:2 * NE], ones[:], A[:, 0], start=False, stop=True)
                pe.matmul(bank(name)[:, 2 * NE:3 * NE], ones[:], A[:, 0], start=True, stop=False)
                mm = pe.matmul(bank(name)[:, 2 * NE:3 * NE], ones[:], A[:, 1], start=False, stop=True)
                done(mm, name)

                M = moe[layer]
                seg = f"moe{layer}"
                last_static = max(v for k, v in TILE.items() if k == name)
                for b in range(BANKS):
                    n_b = last_static // BANKS + (1 if b <= last_static % BANKS else 0)
                    pe.wait_ge(psum_read[b], n_b)
                for b in range(4):
                    pe.matmul(banks[b][:], zeros[:], x[:, 0, 0:512], start=True, stop=True, skip_group_check=True)
                pe.wait_ge(trips_ready, layer + 1)
                n = pe.value_load(trips_i[0:1, 0:1], min_val=GROUPS, max_val=GROUPS * ROUNDS)
                with pe.Fori(0, n) as i:
                    def m_claim(m):
                        if m >= MOE_BANKS:
                            pe.wait_ge(M[f"read{4 + m % 4}"], i * PER_BANK + m // 4)

                    def m_emptied(m):
                        pe.wait_ge(M[f"read{4 + m % 4}"], i * PER_BANK + (m // 4 + 1))

                    def m_bank(m):
                        return banks[4 + m % 4]

                    def m_done(mm, m):
                        mm.then_inc(M[f"full{4 + m % 4}"], 1)

                    def loaded(idx, p):
                        pe.wait_ge(w_loaded[seg][idx], (i * 4 + (p + 1)) * 16)

                    pe.wait_ge(M["picked"], i + 1)
                    for k in range(KD):
                        m_claim(k)
                        for t in range(NT):
                            mm = pe.matmul(m_bank(k)[:], h[:, t, k * P:(k + 1) * P],
                                           pick[:, t].rearrange("p a b -> p (a b)"), start=(t == 0), stop=(t == NT - 1))
                        m_done(mm, k)

                    def scatter(p):
                        b = p % 2
                        for m in (0, 4, 5):
                            m_emptied(8 + 6 * p + m)
                        for t in range(NT):
                            for hf in range(2):
                                mm = pe.matmul(banks[2 * t + hf][:], comb[:, b, t * P:(t + 1) * P],
                                               ysb[:, b, hf * 512:(hf + 1) * 512], start=False, stop=True,
                                               skip_group_check=True)
                        return mm

                    for p in range(4):
                        b = p % 2
                        m0 = 8 + 6 * p
                        m_claim(m0)
                        for t in range(NT):
                            mm = pe.transpose(m_bank(m0)[:, t * P:(t + 1) * P],
                                              wpick[:, t, 2 * p:2 * p + 2].rearrange("p a b -> p (a b)"), ident[:])
                        m_done(mm, m0)
                        if p == 0:
                            for k in range(KD - 4, KD):
                                m_emptied(k)
                        for side in range(2):
                            m = m0 + 1 + side
                            up, gate = (slice(0, 64), slice(64, P)) if side == 0 else (slice(64, P), slice(0, 64))
                            e = 2 * p + side
                            wg, wu = piece(2 * side, KD, DE), piece(2 * side + 1, KD, DE)
                            loaded(2 * side, p)
                            loaded(2 * side + 1, p)
                            m_claim(m)
                            for k in range(KD):
                                lhs = xg[:, k, e * SLOTS:(e + 1) * SLOTS]
                                pe.matmul(m_bank(m)[gate, :], lhs, wg[:, k], start=(k == 0), stop=(k == KD - 1),
                                          skip_group_check=True)
                                mu = pe.matmul(m_bank(m)[up, :], lhs, wu[:, k], start=(k == 0), stop=(k == KD - 1),
                                               skip_group_check=True)
                            m_done(mu, m)
                        if p > 0:
                            scatter(p - 1)
                        m = m0 + 3
                        m_claim(m)
                        m_emptied(m0 + 1)
                        m_emptied(m0 + 2)
                        for f in range(FE):
                            mm = pe.transpose(m_bank(m)[:, f * P:(f + 1) * P], hid[:, b, f * P:(f + 1) * P], ident[:])
                        m_done(mm, m)
                        m_claim(m0 + 4)
                        m_claim(m0 + 5)
                        loaded(4, p)
                        loaded(5, p)
                        m_emptied(m)
                        wd = [piece(4, FE, D), piece(5, FE, D)]
                        for f in range(FE):
                            for hf in range(2):
                                for side in range(2):
                                    r = slice(64 * side, 64 * side + 64)
                                    mm = pe.matmul(m_bank(m0 + 4 + hf)[r, :],
                                                   hidT[:, b, f * P + 64 * side:f * P + 64 * side + 64],
                                                   wd[side][:, f, hf * 512:(hf + 1) * 512],
                                                   start=(f == 0), stop=(f == FE - 1), skip_group_check=True)
                                    if f == FE - 1 and side == 1:
                                        m_done(mm, m0 + 4 + hf)
                    scatter(3).then_inc(M["scattered"], 1)

            pe.wait_ge(moe[DEPTH - 1]["x_ready"], 1)
            for layer in range(DEPTH):
                def arrive2(j):
                    at = layer * NB2 + j
                    kind, _, n = B2_PIECES[j]
                    pe.wait_ge(w_loaded["b2"][at % RING], 16 * (at // RING + 1))
                    if kind == "lru":
                        return ring[:, at % RING, 0:n].rearrange("p (b n) -> p b n", n=P)
                    return piece(at % RING, RT if kind == "or" else KD, n)

                turn_h(SECOND + layer)

                def rnn_inputs(nm, p0):
                    for j in range(6):
                        if j % 2 == 0:
                            w_ = arrive2(p0 + j // 2)
                        name = (nm, layer, j)
                        claim(name)
                        for f in range(min(2, RT - 2 * j)):
                            mm = by_feature(bank(name)[:, f * SEQ:(f + 1) * SEQ], w_, 2 * (j % 2) + f)
                        done(mm, name)

                rnn_inputs("xr", PXR)

                def turn_rope(c):
                    name = ("ropeT", layer, c)
                    claim(name)
                    pe.wait_ge(roped2, 14 * layer + c + 1)
                    for k in range(4 if c < 12 else 1):
                        mm = pe.transpose(bank(name)[:, k * P:(k + 1) * P], roped[:, c % 4, k * P:(k + 1) * P], ident[:])
                    done(mm, name)

                for c in range(15):
                    if c < 14:
                        name = ("rope", layer, c)
                        if c % 2 == 0:
                            w = arrive2(PROPE + c // 2)
                        by_token(name, w, 512 if c < 12 else P, c % 2)
                    if c >= 2:
                        turn_rope(c - 2)
                turn_rope(13)

                for j in range(4):
                    name = ("v", layer, j)
                    if j % 2 == 0:
                        w = arrive2(PV + j // 2)
                    by_token(name, w, 512, j % 2)
                for c in range(8, 14):
                    emptied(pe, ("ropeT", layer, c))
                for j in range(0, 12, 2):
                    names = [("dots", layer, j), ("dots", layer, j + 1)]
                    for n_ in names:
                        claim(n_)
                    cnt, w_ = (4, P) if j < 4 else (2, SEQ)
                    for k in range(cnt):
                        for odd in range(2):
                            if j < 4:
                                hd, qb = 8 * (j // 2) + 2 * k + odd, 0
                            else:
                                hd, qb = 4 * ((j - 4) // 2) + 2 * k + odd, 1
                            r = slice(64 * odd, 64 * odd + 64)
                            mm = pe.matmul(bank(names[odd])[:, k * w_:(k + 1) * w_], iqT[r, hd // 2, qb * P:(qb + 1) * P],
                                           ikT[r, 0:w_], start=True, stop=True)
                            if k == cnt - 1:
                                done(mm, names[odd])
                wr, wi = arrive2(PLRU), arrive2(PLRU + 1)
                pe.wait_ge(conv2_done, layer + 1)
                for j in range(RT):
                    name = ("gates", layer, j)
                    claim(name)
                    mine = [(n, i) for n, (jj, i) in enumerate(BLOCK_PAIRS) if jj == j]
                    for g, wg_ in enumerate((wr, wi)):
                        for n, i in mine:
                            mm = pe.matmul(bank(name)[:, g * SEQ:(g + 1) * SEQ], wg_[:, n], xc[:, i],
                                           start=(n == mine[0][0]), stop=(n == mine[-1][0]))
                    done(mm, name)
                rnn_inputs("gr", PGR)

                def scores2(hh):
                    name = ("S2", layer, hh)
                    claim(name)
                    pe.matmul(bank(name)[:, 0:P], qT[:, hh, 0:P], kT[:, hh, 0:P], start=True, stop=True)
                    mm = pe.matmul(bank(name)[:, P:3 * P], qT[:, hh, P:], kT[:, hh], start=True, stop=True)
                    done(mm, name)

                for c in range(8):
                    emptied(pe, ("ropeT", layer, c))
                for j in range(4):
                    emptied(pe, ("v", layer, j))
                scores2(0)
                for hh in range(HEADS):
                    name = ("ga", layer, hh)
                    if hh % 4 == 0:
                        w = arrive2(PGA + hh // 4)
                    claim(name)
                    done(by_feature(bank(name)[:, 0:SEQ], w, hh % 4), name)
                    if hh + 1 < HEADS:
                        scores2(hh + 1)
                    name = ("PT2", layer, hh)
                    claim(name)
                    pe.wait_ge(probs2, layer * HEADS + hh + 1)
                    b = hh % 2
                    pe.transpose(bank(name)[:, 0:P], s2[:, b, 0:P], ident[:])
                    pe.transpose(bank(name)[:, P:2 * P], s2[:, b, P:2 * P], ident[:])
                    done(pe.transpose(bank(name)[:, 2 * P:3 * P], s2[:, b, 2 * P:], ident[:]), name)
                    emptied(pe, name)
                    yn = ("Y2", layer, hh)
                    claim(yn)
                    hs = slice(hh * HD2, (hh + 1) * HD2)
                    pe.matmul(bank(yn)[:, 0:SEQ], vv[:, 0, hs], pT2[:, b, 0:SEQ], start=True, stop=False)
                    done(pe.matmul(bank(yn)[:, P:SEQ], vv[:, 1, hs], pT2[:, b, 2 * P:], start=False, stop=True), yn)
                for hh in range(HEADS):
                    emptied(pe, ("Y2", layer, hh))
                for pc in range(2):
                    wm, wa = arrive2(PMA + 2 * pc), arrive2(PMA + 2 * pc + 1)
                    for f in range(4):
                        name = ("ma", layer, 4 * pc + f)
                        claim(name)
                        by_feature(bank(name)[:, 0:SEQ], wm, f)
                        done(by_feature(bank(name)[:, SEQ:], wa, f, qT), name)
                for j in range(6):
                    emptied(pe, ("gr", layer, j))
                for pc in range(2):
                    wm = arrive2(PMB + 3 * pc)
                    for f in range(4):
                        if f % 2 == 0:
                            wb = arrive2(PMB + 3 * pc + 1 + f // 2)
                        name = ("mb", layer, 4 * pc + f)
                        claim(name)
                        by_feature(bank(name)[:, 0:SEQ], wm, f)
                        done(by_feature(bank(name)[:, SEQ:], wb, f % 2, ui, RT), name)
                pe.wait_ge(merged_ready, 8 * (layer + 1))
                for i in range(4):
                    name = ("out2", layer, i)
                    pc, t = i // 2, i % 2
                    if t == 0:
                        w = arrive2(PO + pc)
                    claim(name)
                    for k in range(KD):
                        mm = pe.matmul(bank(name)[:], merged[:, k, t * P:(t + 1) * P], w[:, k], start=(k == 0),
                                       stop=(k == KD - 1))
                    done(mm, name)


def _columns(v):
    return v.reshape(-1, P).T


def _block_diagonal(w):
    whole = np.zeros((RNN, RNN), w.dtype)
    for b in range(RB):
        whole[b * RBD:(b + 1) * RBD, b * RBD:(b + 1) * RBD] = w[b]
    return np.concatenate([whole[i * P:(i + 1) * P, j * P:(j + 1) * P] for j, i in BLOCK_PAIRS], axis=1)


def kernel(**inputs):
    import concourse.bacc as bacc
    from concourse.bass_utils import run_bass_kernel_spmd

    a = {k: np.asarray(v) for k, v in inputs.items()}
    f = np.float32
    cols = np.stack([np.concatenate(
        [_columns(a["norm_attn_out"][l]), _columns(a["norm_conv_out"][l]), _columns(a["conv_w"][l].reshape(-1)),
         _columns(a["conv_w_2"][l].reshape(-1)), _columns(a["conv_b_2"][l]), _columns(a["b_rg_2"][l]),
         _columns(a["b_ig_2"][l]), _columns(a["lru_lambda_2"][l])], axis=1) for l in range(DEPTH)], axis=1)

    def inverse_frequencies(theta, dim):
        return (f(theta) ** (-np.arange(0, dim, 2, dtype=f) / f(dim))).astype(f)

    inv2 = np.concatenate([inverse_frequencies(10000.0, HD2), inverse_frequencies(10000.0, ID)])
    rows = np.concatenate(
        [np.concatenate([a["b_router_group"][l], a["b_router_expert"][l]]) for l in range(DEPTH)]
        + [a["attn_sink"][l] for l in range(DEPTH)] + [inv2])
    rows = np.broadcast_to(rows, (P, rows.size))
    angle = np.arange(SEQ, dtype=f)[:, None] * inverse_frequencies(500000.0, 2 * ROT1)
    rope1 = np.stack([np.broadcast_to(g(angle).reshape(NT, P, 1, ROT1), (NT, P, HEADS + KVH, ROT1))
                      .transpose(1, 0, 2, 3).reshape(P, -1) for g in (np.cos, np.sin)], axis=1)
    gains = np.stack([a["norm_mix"][0], a["norm_ffn"][0], a["norm_mix"][1], a["norm_ffn"][1],
                      a["norm_final"], a["norm_g_2"][0], a["norm_g_2"][1], a["final_g_2"]])
    gains = np.broadcast_to(gains[:, None], (gains.shape[0], P, D))
    router = np.concatenate([a["w_router_group"], a["w_router_expert"]], axis=2)
    lru = np.stack([np.stack([_block_diagonal(a[n][l]) for n in ("w_rg_2", "w_ig_2")]) for l in range(DEPTH)])
    arrays = {
        "x_in": a["x"].reshape(SEQ, D), "cols_in": cols, "rows_in": rows, "rope1_in": rope1, "gains_in": gains,
        "router_in": router, "w_in": a["w_in"], "w_out": a["w_out"], "w_gate": a["w_expert_gate"],
        "w_up": a["w_expert_up"], "w_down": a["w_expert_down"], "positions": a["positions_2"].reshape(NT, P).T,
        "w_in2": a["w_in_2"], "w_lru": lru, "w_oa": a["w_out_attn_2"], "w_or": a["w_out_rnn_2"], "w_o": a["w_o_2"],
    }
    arrays = {k: np.ascontiguousarray(v) for k, v in arrays.items()}
    nc = bacc.Bacc("TRN2", target_bir_lowering=False, num_devices=1)
    args = {k: nc.dram_tensor(f"{k}_dram", v.shape, mybir.dt.from_np(v.dtype), kind="ExternalInput").ap()
            for k, v in arrays.items()}
    out = nc.dram_tensor("out_dram", (SEQ, D), F32, kind="ExternalOutput").ap()
    program(nc, *args.values(), out)
    r = run_bass_kernel_spmd(nc, [{f"{k}_dram": v for k, v in arrays.items()}], core_ids=[0])
    return r.results[0]["out_dram"].reshape(1, SEQ, D)
```

```python
from contextlib import ExitStack

import numpy as np

import concourse.bass as bass
from concourse import mybir

F32 = mybir.dt.float32
I32 = mybir.dt.int32
ALU = mybir.AluOpType
ACT = mybir.ActivationFunctionType
AX = mybir.AxisListType

P = 128
SEQ = 256
NT = SEQ // P
D = 1024
KD = D // P
DEPTH = 2
EPS = 1e-6
NEG = -1e30
TAKEN = -3e38

HEADS = 8
HD1 = 64
KVH = 2
QW = HEADS * HD1
KVW = KVH * HD1
CW = D - QW
IN1 = QW + 2 * KVW + 3 * CW
ROT1 = 8
GROUPS = 4
PER_GROUP = 8
NE = GROUPS * PER_GROUP
DE = 512
FE = DE // P
SLOTS = 64
ROUNDS = SEQ // SLOTS
ROUTER_W = GROUPS + NE

HD2 = 128
AW2 = HEADS * HD2
IH = 16
ID = 64
TOPK = min(256, SEQ // 4)
RNN = 1408
RT = RNN // P
RB = 16
RBD = RNN // RB
LRU_C = 8.0
TAPS2 = 4
Q2, K2, V2, GA2, IQ2 = 0, 1024, 2048, 3072, 4096
IK2 = IQ2 + IH * ID
XR2 = IK2 + ID + IH
GR2 = XR2 + RNN
MA2 = GR2 + RNN
MB2 = MA2 + D
IN2 = MB2 + D

BETWEEN = 2 * DEPTH
SECOND = BETWEEN + 1
FINAL = SECOND + DEPTH

RING = 6
EXTRA = 2
SLOT_F = 4096
BANKS = 8
IDLE_START, IDLE_EXPERTS, IDLE_MIXER, IDLE_BETWEEN, IDLE_ROUTER, IDLE_PICKS = 16, 18, 12, 26, 22, 9
MOE_BANKS = 4

BLOCK_PAIRS = [(j, i) for j in range(RT) for i in range(RT)
               if i * P < -(-(j + 1) * P // RBD) * RBD and (i + 1) * P > (j * P // RBD) * RBD]
NBP = len(BLOCK_PAIRS)

COLS = {}
_at = 0
for _name, _n in [("g_attn", 4), ("g_conv", 4), ("conv1", 12), ("conv2", TAPS2 * RT), ("conv2_b", RT),
                  ("b_rg", RT), ("b_ig", RT), ("lam", RT)]:
    COLS[_name] = (_at, _n)
    _at += _n
NCOLS = _at

NROPE1 = NT * (HEADS + KVH) * ROT1
INV2 = HD2 // 2 + ID // 2
TWO_PI_PARTS = (6.28125, 0.0019340515136718750, 1.2556659146999e-6)
ROUNDER = 12582912.0


BESIDE_HEAD = [[("u", 1), ("gc", 2)], [("u", 2)], [("gc", 3)], [("u", 3), ("gb", 0)], [("gb", 1), ("gb", 2)], [("gb", 3)],
               [("out1", 0)], [("out1", 1)]]
OUT1 = [(0, 0, 1), (0, 1, 1), (0, 0, 0), (0, 1, 0), (1, 0, 1), (1, 0, 0), (1, 1, 1), (1, 1, 0)]


def psum_tiles():
    names = []
    for layer in range(DEPTH):
        names += [("hT", 2 * layer, j) for j in range(4)]
        names += [("q", layer, t) for t in range(NT)] + [("kv", layer, t) for t in range(NT)]
        names += [("gc", layer, j) for j in range(2)]
        names += [("qkT", layer, j) for j in range(3)]
        names += [("S1", layer, 0), ("u", layer, 0)]
        for h in range(HEADS):
            names += [("S1", layer, h + 1)] if h + 1 < HEADS else []
            names += [("PT1", layer, h)]
            names += [(g, layer, j) for g, j in BESIDE_HEAD[h]]
            names += [("Y1", layer, h // 2)] if h % 2 == 0 else []
        names += [("ss", layer, 0)]
        names += [("out1", layer, i) for i in range(2, 8)]
        names += [("hT", 2 * layer + 1, j) for j in range(4)]
        names += [("logits", layer, 0), ("rank", layer, 0), ("gather", layer, 0), ("gather", layer, 1)]
    for layer in range(DEPTH):
        names += [("hT", SECOND + layer, j) for j in range(4)]
        names += [("xr", layer, j) for j in range(6)]
        for c in range(15):
            names += [("rope", layer, c)] if c < 14 else []
            names += [("ropeT", layer, c - 2)] if c >= 2 else []
        names += [("ropeT", layer, 13)]
        names += [("v", layer, j) for j in range(4)]
        names += [("dots", layer, j) for j in range(12)]
        names += [("gates", layer, j) for j in range(RT)]
        names += [("gr", layer, j) for j in range(6)]
        names += [("S2", layer, 0), ("ga", layer, 0)]
        for h in range(HEADS):
            names += [("S2", layer, h + 1)] if h + 1 < HEADS else []
            names += [("PT2", layer, h)]
            names += [("ga", layer, h + 1)] if h + 1 < HEADS else []
            names += [("Y2", layer, h)]
        names += [("mb", layer, j) for j in range(8)]
        names += [("ma", layer, j) for j in range(8)]
        names += [("out2", layer, j) for j in range(4)]
    return {name: n for n, name in enumerate(names)}


TILE = psum_tiles()
assert len(TILE) == max(TILE.values()) + 1


class Steps:

    def __init__(self, eng, own, base=None):
        self.eng, self.own, self.base, self.n, self.last = eng, own, base or {}, {}, None

    def value(self, sem):
        n = self.n.get(sem.name, 0)
        return self.base[sem.name] + n if sem.name in self.base else n

    def __call__(self, ins, sem=None):
        sem = sem or self.own
        ins.then_inc(sem, 1)
        self.n[sem.name] = self.n.get(sem.name, 0) + 1
        self.last = (sem, self.value(sem))

    def marks(self, ins, sem, value):
        ins.then_inc(sem, 1)
        self.last = (sem, value)

    def settle(self):
        if self.last is not None:
            self.eng.wait_ge(*self.last)


def program(nc, x_in, cols_in, rows_in, rope1_in, gains_in, router_in, w_in, w_out, w_gate, w_up, w_down,
            positions, w_in2, w_lru, w_oa, w_or, w_o, out, upto=99):
    with ExitStack() as ctx:
        def sem(name):
            return ctx.enter_context(nc.semaphore(name))

        ring = ctx.enter_context(nc.sbuf_tensor("ring", [P, RING, SLOT_F], F32))
        x = ctx.enter_context(nc.sbuf_tensor("x", [P, NT, D], F32))
        h = ctx.enter_context(nc.sbuf_tensor("h", [P, NT, D], F32))
        hT = ctx.enter_context(nc.sbuf_tensor("hT", [P, KD, SEQ], F32))

        ident = ctx.enter_context(nc.sbuf_tensor("ident", [P, P], F32))
        ones = ctx.enter_context(nc.sbuf_tensor("ones", [P, P], F32))
        zeros = ctx.enter_context(nc.sbuf_tensor("zeros", [P, P], F32))
        before = ctx.enter_context(nc.sbuf_tensor("before", [P, P], F32))
        iota_i = ctx.enter_context(nc.sbuf_tensor("iota_i", [P, SLOTS], I32))
        iota_f = ctx.enter_context(nc.sbuf_tensor("iota_f", [P, SLOTS], F32))
        cols = ctx.enter_context(nc.sbuf_tensor("cols", [P, DEPTH, NCOLS], F32))
        rows = ctx.enter_context(nc.sbuf_tensor("rows", [P, DEPTH * (ROUTER_W + HEADS) + INV2], F32))
        gain = ctx.enter_context(nc.sbuf_tensor("gain", [P, D], F32))
        ang = ctx.enter_context(nc.sbuf_tensor("ang", [P, NT, INV2], F32))
        cos2 = ctx.enter_context(nc.sbuf_tensor("cos2", [P, NT, INV2], F32))
        sin2 = ctx.enter_context(nc.sbuf_tensor("sin2", [P, NT, INV2], F32))
        pos_i = ctx.enter_context(nc.sbuf_tensor("pos_i", [P, NT], I32))
        pos_f = ctx.enter_context(nc.sbuf_tensor("pos_f", [P, NT], F32))
        decay = ctx.enter_context(nc.sbuf_tensor("decay", [P, DEPTH, RT], F32))
        lam_t = ctx.enter_context(nc.sbuf_tensor("lam_t", [P, 4, DEPTH, RT], F32))
        power = ctx.enter_context(nc.sbuf_tensor("power", [P, 4], F32))
        stat = ctx.enter_context(nc.sbuf_tensor("stat", [P, 64], F32))
        small = ctx.enter_context(nc.sbuf_tensor("small", [P, 15, NT, NE], F32))
        causal = ctx.enter_context(nc.sbuf_tensor("causal", [P, 3 * P], F32))
        top8 = ctx.enter_context(nc.sbuf_tensor("top8", [P, 16], F32))
        trips_i = ctx.enter_context(nc.sbuf_tensor("trips_i", [P, 2], I32))

        WORK = 18240
        work = ctx.enter_context(nc.sbuf_tensor("work", [P, WORK], F32))
        top = {}

        def carve(phase, *shape):
            n = int(np.prod(shape))
            at = top.get(phase, 0)
            top[phase] = at + n
            assert top[phase] <= WORK, (phase, top[phase])
            v = work[:, at:at + n]
            if len(shape) == 2:
                v = v.rearrange("p (a b) -> p a b", a=shape[0])
            if len(shape) == 3:
                v = v.rearrange("p (a b c) -> p a b c", a=shape[0], b=shape[1])
            return v

        window = carve("keep1", NT, SEQ)
        cos1 = carve("keep1", NROPE1)
        sin1 = carve("keep1", NROPE1)
        w_router = carve("keep1", KD, P)
        top["mix1"] = top["moe"] = top["keep1"]
        qkv = carve("mix1", NT, QW + 2 * KVW)
        kswap = carve("mix1", NT, KVW)
        rt1 = carve("mix1", 4, NROPE1)
        qT1 = carve("mix1", HEADS // 2, SEQ)
        kT1 = carve("mix1", 2, SEQ)
        gb = carve("mix1", 4, SEQ)
        gc = carve("mix1", 4, SEQ)
        cu = carve("mix1", 4, SEQ + 2)
        yc = carve("mix1", 4, SEQ)
        yc_t = carve("mix1", SEQ)
        yT = carve("mix1", KD, SEQ)
        sq = carve("mix1", KD, SEQ)
        s1 = carve("mix1", 2, NT, SEQ)
        pT1 = carve("mix1", 2, NT, SEQ)
        xg = carve("moe", 2 * KD, 2 * SLOTS)
        pick = carve("moe", NT, PER_GROUP, SLOTS)
        wpick = carve("moe", NT, PER_GROUP, SLOTS)
        comb = carve("moe", 2, SEQ)
        silu_g = carve("moe", 2, DE)
        hid = carve("moe", 2, DE)
        hidT = carve("moe", 2, FE * P)
        ysb = hT[:].rearrange("p a b -> p (a b)").rearrange("p (a b) -> p a b", a=2)
        extra = work[:, WORK - EXTRA * SLOT_F:].rearrange("p (a b) -> p a b", a=EXTRA)

        assert top["moe"] <= WORK - EXTRA * SLOT_F
        gain_second = w_router.rearrange("p a b -> p (a b)")

        def gathered(b, half):
            return xg[:, b * KD + half * KD // 2:b * KD + (half + 1) * KD // 2].rearrange("p a b -> p (a b)")

        xr = carve("b2", RT, SEQ + TAPS2 - 1)
        xc = carve("b2", RT, SEQ)
        ra = carve("b2", RT, SEQ)
        ui = carve("b2", RT, SEQ)
        qT = carve("b2", HEADS, SEQ)
        kT = carve("b2", HEADS, SEQ)
        roped_at = top["b2"]
        roped = carve("b2", 4, 512)
        bias2 = carve("b2", 3 * P)
        iw = carve("b2", NT, IH)
        top["idx"] = roped_at
        relu = carve("idx", 2, 512)
        wk = carve("idx", 2, 3 * P)
        top["att"] = 0
        s2 = carve("att", 2, 3 * P)
        pT2 = carve("att", 2, 3 * P)
        assert top["att"] <= RT * (SEQ + 3)
        tanh_a = xr.rearrange("p a b -> p (a b)")[:, 0:RT * SEQ].rearrange("p (a b) -> p a b", a=RT)
        merged = xc.rearrange("p a b -> p (a b)")[:, 0:KD * SEQ].rearrange("p (a b) -> p a b", a=KD)
        ra_words, ui_words = (z.rearrange("p a b -> p (a b)") for z in (ra, ui))
        iqT = ra_words[:, 0:IH // 2 * SEQ].rearrange("p (a b) -> p a b", a=IH // 2)
        ga_all = iqT
        ikT = ra_words[:, IH // 2 * SEQ:(IH // 2 + 1) * SEQ]
        ropetmp = ui_words[:, 0:1024].rearrange("p (a b) -> p a b", a=2)
        vv = h

        banks = [ctx.enter_context(nc.psum_tensor(f"bank{b}", [P, 512], F32)) for b in range(BANKS)]
        psum_full = [sem(f"psum_full_{b}") for b in range(BANKS)]
        psum_read = [sem(f"psum_read_{b}") for b in range(BANKS)]

        x_loaded = [sem(f"x_loaded_{t}") for t in range(NT)]
        rope1_loaded = sem("rope1_loaded")
        consts_loaded = sem("consts_loaded")
        gain_loaded = sem("gain_loaded")
        gain_second_loaded = sem("gain_second_loaded")
        router_loaded = sem("router_loaded")
        masks_ready = sem("masks_ready")
        own_dve = sem("dve_steps")
        own_act = sem("act_steps")
        own_pool = sem("pool_steps")
        sumsq_ready = sem("sumsq_ready")
        mean_ready = sem("mean_ready")
        rstd_ready = sem("rstd_ready")
        h_ready = sem("h_ready")
        roped1 = sem("roped1")
        conv_out = sem("conv_out")
        conv_sq = sem("conv_sq")
        negmax = sem("negmax")
        exps = sem("exps")
        probs = sem("probs")
        route_exp_in = sem("route_exp_in")
        route_exp_out = sem("route_exp_out")
        assign_ready = sem("assign_ready")
        trips_ready = sem("trips_ready")
        angles_ready = sem("angles_ready")
        tables2_ready = sem("tables2_ready")
        lam_in = sem("lam_in")
        lam_exp = sem("lam_exp")
        decay_ready = sem("decay_ready")
        out_stored = sem("out_stored")
        SEGS = ["mix0", "moe0", "mix1", "moe1", "b2"]
        w_loaded = {s: [sem(f"w_loaded_{s}_{k}") for k in range(RING + EXTRA)] for s in SEGS}
        moe = [{n: sem(f"moe{l}_{n}") for n in ["picked", "wpicked", "full4", "full5", "full6", "full7", "read4", "read5",
                                                "read6", "read7", "silu", "scattered", "dve", "act", "x_ready"]}
               for l in range(DEPTH)]
        roped2 = sem("roped2")
        conv2_done = sem("conv2_done")
        tanh_ready = sem("tanh_ready")
        tanh_used = sem("tanh_used")
        root_ready = sem("root_ready")
        hidden_ready = sem("hidden_ready")
        relu_done = sem("relu_done")
        negmax2 = sem("negmax2")
        exps2 = sem("exps2")
        probs2 = sem("probs2")
        silu_gr = sem("silu_gr")
        silu_ga = sem("silu_ga")
        attn_gated = sem("attn_gated")
        sig_ready = sem("sig_ready")
        merged_ready = sem("merged_ready")

        def bank(name):
            return banks[TILE[name] % BANKS]

        def uses(name):
            return TILE[name] // BANKS + 1

        def full(eng, name):
            eng.wait_ge(psum_full[TILE[name] % BANKS], uses(name))

        def emptied(eng, name):
            eng.wait_ge(psum_read[TILE[name] % BANKS], uses(name))

        def col(layer, name, k, rows_=slice(0, P)):
            a, n = COLS[name]
            return cols[rows_, layer, a + k:a + k + 1]

        SINK0 = DEPTH * ROUTER_W
        INV0 = SINK0 + DEPTH * HEADS

        def mixer_piece(j):
            return (j + RING - 1) % RING

        def mixer_count(j):
            return 32 if j == RING else 16

        MIX_PIECES = [("in", 0, QW), ("in", QW, 2 * KVW), ("in", QW + 2 * KVW + CW, CW),
                      ("in", QW + 2 * KVW + 2 * CW, CW), ("in", QW + 2 * KVW, CW), ("out", 0, 512), ("out", 512, 512)]
        MIX_LAST = [("q", 1), ("kv", 1), ("gc", 3), ("u", 3), ("gb", 3), ("out1", 3), ("out1", 7)]
        B2_PIECES = ([("in", XR2, 512), ("in", XR2 + 512, 512), ("in", XR2 + 1024, 384)]
                     + [("in", Q2, 512), ("in", Q2 + 512, 512), ("in", K2, 512), ("in", K2 + 512, 512)]
                     + [("in", IQ2, 512), ("in", IQ2 + 512, 512), ("in", IK2, 128)]
                     + [("in", V2, 512), ("in", V2 + 512, 512)]
                     + [("lru", 0, NBP * P), ("lru", 1, NBP * P)]
                     + [("in", GR2, 512), ("in", GR2 + 512, 512), ("in", GR2 + 1024, 384)]
                     + [("in", GA2, 512), ("in", GA2 + 512, 512)]
                     + [("in", MB2, 512), ("or", 0, 256), ("or", 256, 256)]
                     + [("in", MB2 + 512, 512), ("or", 512, 256), ("or", 768, 256)]
                     + [("in", MA2, 512), ("oa", 0, 512), ("in", MA2 + 512, 512), ("oa", 512, 512)]
                     + [("o", 0, 512), ("o", 512, 512)])
        NB2 = len(B2_PIECES)
        B2_LAST = ([("xr", 1), ("xr", 3), ("xr", 5)] + [("rope", c) for c in (1, 3, 5, 7, 9, 11, 13)]
                   + [("v", 1), ("v", 3)] + [("gates", RT - 1)] * 2 + [("gr", 1), ("gr", 3), ("gr", 5), ("ga", 3), ("ga", 7)]
                   + [("mb", 3), ("mb", 1), ("mb", 3), ("mb", 7), ("mb", 5), ("mb", 7),
                      ("ma", 3), ("ma", 3), ("ma", 7), ("ma", 7), ("out2", 1), ("out2", 3)])
        PXR, PROPE, PV, PLRU, PGR, PGA, PMB, PMA, PO = 0, 3, 10, 12, 14, 17, 19, 25, 29

        def piece(slot, k, n):
            words = ring[:, slot, 0:k * n] if slot < RING else extra[:, slot - RING, 0:k * n]
            return words.rearrange("p (k n) -> p k n", k=k)

        T_COMB, T_GU, T_NEXT, T_HID, T_OUT, PAIR_TILES = 0, 1, 3, 5, 6, 8
        MOE_TILES = 4 * PAIR_TILES
        PER_BANK = MOE_TILES // MOE_BANKS

        PER_PAIR = 6
        TURN = 4 * PER_PAIR
        MOE_RING = RING + EXTRA
        ROUND_TRIPS = TURN // MOE_RING
        assert TURN % MOE_RING == 0

        def piece_last(n):
            pair, idx = n // PER_PAIR, n % PER_PAIR
            return PAIR_TILES * pair + (T_GU, T_GU, T_GU + 1, T_GU + 1, T_OUT + 1, T_OUT + 1)[idx]

        block = ctx.enter_context(nc.Block())

        @block.sync
        def _(sp):
            for t in range(NT):
                sp.dma_start(x[:, t], x_in[t * P:(t + 1) * P]).then_inc(x_loaded[t], 16)
            for dst, src in ((rows[:], rows_in), (cols[:], cols_in), (pos_i[:], positions)):
                sp.dma_start(dst, src).then_inc(consts_loaded, 16)

            def left_by_experts(layer, slot):
                m = piece_last(TURN - MOE_RING + slot)
                sp.wait_ge(moe[layer][f"full{4 + m % 4}"], last_turn * PER_BANK + (m // 4 + 1))

            def mixer(layer):
                for j, (kind, c0, n) in enumerate(MIX_PIECES):
                    slot = mixer_piece(j)
                    if j == RING:
                        full(sp, ("q", layer, 1))
                    elif layer > 0:
                        left_by_experts(layer - 1, slot)
                    src = (w_in if kind == "in" else w_out)[layer].rearrange("(k p) n -> p k n", p=P)
                    sp.dma_start(piece(slot, KD, n), src[:, :, c0:c0 + n]).then_inc(w_loaded[f"mix{layer}"][slot], 16)

            def expert_piece(layer, e0, n):
                p, idx, slot = n // PER_PAIR, n % PER_PAIR, n % MOE_RING
                e = e0 + (2 * p + (idx % 2 if idx >= 4 else idx // 2))
                if idx >= 4:
                    src = w_down[layer].rearrange("e (k p) n -> e p k n", p=P)
                    dst = piece(slot, FE, D)
                else:
                    src = (w_gate if idx % 2 == 0 else w_up)[layer].rearrange("e (k p) n -> e p k n", p=P)
                    dst = piece(slot, KD, DE)
                sp.dma_start(dst, src[e]).then_inc(w_loaded[f"moe{layer}"][slot], 16)

            def experts(layer):
                for n in range(TURN):
                    if n < RING:
                        nm, last_tile = MIX_LAST[n + 1]
                        full(sp, (nm, layer, last_tile))
                    elif n < MOE_RING:
                        emptied(sp, ("out1", layer, 7))
                    else:
                        m = piece_last(n - MOE_RING)
                        sp.wait_ge(moe[layer][f"full{4 + m % 4}"], m // 4 + 1)
                    expert_piece(layer, 0, n)
                sp.wait_ge(trips_ready, layer + 1)
                last = sp.value_load(trips_i[0:1, 1:2], min_val=GROUPS - 1, max_val=GROUPS * ROUNDS - 1)
                with sp.Fori(0, last) as i:
                    g = ((i + 1) % GROUPS) * PER_GROUP
                    for n in range(TURN):
                        m = piece_last((n - MOE_RING) % TURN)
                        sp.wait_ge(moe[layer][f"full{4 + m % 4}"],
                                   i * PER_BANK + (m // 4 + 1 + (PER_BANK if n >= MOE_RING else 0)))
                        expert_piece(layer, g, n)
                return last

            last_turn = None
            for layer in range(DEPTH):
                mixer(layer)
                last_turn = experts(layer)
            for layer in range(DEPTH):
                for j, (kind, c0, n) in enumerate(B2_PIECES):
                    at = layer * NB2 + j
                    slot = at % RING
                    if at < RING:
                        left_by_experts(DEPTH - 1, slot)
                    else:
                        nm, last = B2_LAST[(at - RING) % NB2]
                        full(sp, (nm, (at - RING) // NB2, last))
                    if kind == "lru":
                        dst, src = ring[:, slot, 0:n], w_lru[layer, c0]
                    elif kind == "or":
                        dst = piece(slot, RT, n)
                        src = w_or[layer].rearrange("(k p) n -> p k n", p=P)[:, :, c0:c0 + n]
                    else:
                        w = {"in": w_in2, "oa": w_oa, "o": w_o}[kind]
                        dst = piece(slot, KD, n)
                        src = w[layer].rearrange("(k p) n -> p k n", p=P)[:, :, c0:c0 + n]
                    sp.dma_start(dst, src).then_inc(w_loaded["b2"][slot], 16)
            for t in range(NT):
                sp.wait_ge(h_ready, NT * FINAL + t + 1)
                sp.dma_start(out[t * P:(t + 1) * P], h[:, t]).then_inc(out_stored, 16)
            sp.wait_ge(out_stored, 16 * NT)

        @block.gpsimd
        def _(pool):
            S = Steps(pool, own_pool)
            S(pool.memset(ident[:], 0.0))
            S(pool.memset(ones[:], 1.0))
            S(pool.memset(zeros[:], 0.0))
            S(pool.memset(power[:], -0.5))
            S(pool.memset(window, 0.0))
            S(pool.memset(w_router, 0.0))
            S.settle()
            S(pool.affine_select(out=ident[:], in_=ident[:], compare_op=ALU.not_equal, fill=1.0, base=0,
                                 pattern=[[-1, P]], channel_multiplier=1))
            S(pool.affine_select(out=before[:], in_=ones[:], compare_op=ALU.is_gt, fill=0.0, base=0,
                                 pattern=[[1, P]], channel_multiplier=-1))
            S(pool.affine_select(out=window, in_=window, compare_op=ALU.is_ge, fill=NEG, base=P,
                                 pattern=[[P, NT], [-1, SEQ]], channel_multiplier=1))
            S.settle()
            S(pool.affine_select(out=window, in_=window, compare_op=ALU.is_ge, fill=NEG, base=P,
                                 pattern=[[-P, NT], [1, SEQ]], channel_multiplier=-1))
            S(pool.iota(iota_i[:], [[1, SLOTS]], base=0, channel_multiplier=0))
            S.settle()
            pool.tensor_copy(iota_f[:], iota_i[:]).then_inc(masks_ready, 1)
            pool.dma_start(w_router[:, :, 0:ROUTER_W],
                           router_in[0].rearrange("(k p) n -> p k n", p=P)).then_inc(router_loaded, 16)

            def inverse_root(src, dst, n):
                pool.tensor_tensor(dst, src, power[:, 0:n], ALU.pow).then_inc(rstd_ready, 1)

            def inverse_rms(stage):
                for t in range(NT):
                    pool.wait_ge(mean_ready, NT * stage + t + 1)
                    inverse_root(stat[:, 2 + t:3 + t], stat[:, 4 + t:5 + t], 1)

            for layer in range(DEPTH):
                inverse_rms(2 * layer)
                pool.wait_ge(consts_loaded, 48)
                for f in range(4):
                    emptied(pool, ("u", layer, f))
                    S.settle()
                    S(pool.tensor_scalar(yc[:, f], cu[:, f, 0:SEQ], col(layer, "conv1", f), None, ALU.mult))
                    for tap in (1, 2):
                        S.settle()
                        S(pool.tensor_scalar(yc_t, cu[:, f, tap:tap + SEQ], col(layer, "conv1", 4 * tap + f), None,
                                             ALU.mult))
                        S.settle()
                        S(pool.tensor_tensor(yc[:, f], yc[:, f], yc_t, ALU.add))
                S.settle()
                for f in range(4):
                    emptied(pool, ("gb", layer, f))
                    S(pool.tensor_tensor(yc[:, f], yc[:, f], gb[:, f], ALU.mult), conv_out)
                emptied(pool, ("ss", layer, 0))
                inverse_root(stat[:, 8:12], stat[:, 12:16], 4)
                inverse_rms(2 * layer + 1)
                if layer + 1 < DEPTH:
                    full(pool, ("rank", layer, 0))
                    pool.dma_start(w_router[:, :, 0:ROUTER_W],
                                   router_in[layer + 1].rearrange("(k p) n -> p k n", p=P)).then_inc(router_loaded, 16)
            for stage in range(BETWEEN, FINAL + 1):
                inverse_rms(stage)

        @block.scalar
        def _(act):
            S = Steps(act, own_act)

            def load_gain(stage):
                if stage > 0:
                    act.wait_ge(h_ready, 2 * stage)
                act.dma_start(gain[:], gains_in[stage]).then_inc(gain_loaded, 16)

            def square(stage, t):
                S(act.activation(h[:, t], x[:, t], ACT.Square, accum_out=stat[:, t:t + 1]), sumsq_ready)

            def even_hT(stage):
                for j in (0, 2):
                    full(act, ("hT", stage, j))
                    act.copy(hT[:, 2 * j:2 * j + 2].rearrange("p a b -> p (a b)"), bank(("hT", stage, j))[:]
                             ).then_inc(psum_read[TILE[("hT", stage, j)] % BANKS], 1)

            def empty(name, dst, src, func=ACT.Copy, **kw):
                full(act, name)
                act.activation(dst, src, func, **kw).then_inc(psum_read[TILE[name] % BANKS], 1)

            load_gain(0)
            act.dma_start(cos1, rope1_in[:, 0]).then_inc(rope1_loaded, 16)
            act.dma_start(sin1, rope1_in[:, 1]).then_inc(rope1_loaded, 16)
            for t in range(NT):
                act.wait_ge(x_loaded[t], 16)
                square(0, t)

            def second_block_tables():
                act.wait_ge(consts_loaded, 48)
                act.wait_ge(lam_in, 1)
                act.activation(lam_t[:, 1], lam_t[:, 0], ACT.Exp, scale=-1.0).then_inc(lam_exp, 1)
                act.wait_ge(angles_ready, 1)
                S(act.activation(sin2[:], sin2[:], ACT.Sin))
                S(act.activation(cos2[:], cos2[:], ACT.Sin), tables2_ready)

            for layer in range(DEPTH):
                if layer > 0:
                    for t in range(NT):
                        act.wait_ge(moe[layer - 1]["x_ready"], t + 1)
                        square(2 * layer, t)
                even_hT(2 * layer)
                load_gain(2 * layer + 1)
                if layer == 0:
                    second_block_tables()
                for t in range(NT):
                    empty(("q", layer, t), qkv[:, t, 0:QW], bank(("q", layer, t))[:])
                for t in range(NT):
                    empty(("kv", layer, t), qkv[:, t, QW:], bank(("kv", layer, t))[:, 0:2 * KVW])

                def gate_tile(nm, j):
                    if nm in ("gc", "gb"):
                        empty((nm, layer, j), (gc if nm == "gc" else gb)[:, j], bank((nm, layer, j))[:, 0:SEQ])

                gate_tile("gc", 0)
                gate_tile("gc", 1)
                for j in range(2):
                    empty(("qkT", layer, j), qT1[:, 2 * j:2 * j + 2].rearrange("p a b -> p (a b)"),
                          bank(("qkT", layer, j))[:])
                empty(("qkT", layer, 2), kT1.rearrange("p a b -> p (a b)"), bank(("qkT", layer, 2))[:])

                def exponentials(hh):
                    act.wait_ge(negmax, layer * HEADS + hh + 1)
                    st = stat[:, 16 + 8 * (hh % 2):24 + 8 * (hh % 2)]
                    for qb in range(NT):
                        S(act.activation(s1[:, hh % 2, qb], s1[:, hh % 2, qb], ACT.Exp, bias=st[:, 2 + qb:3 + qb],
                                         accum_out=st[:, 4 + qb:5 + qb]))
                    S(act.activation(st[:, 6:8], st[:, 2:4], ACT.Exp,
                                     bias=rows[:, SINK0 + layer * HEADS + hh:SINK0 + layer * HEADS + hh + 1]), exps)

                def convolved(f):
                    act.wait_ge(conv_out, 4 * layer + f + 1)
                    S(act.activation(sq[:, 4 + f], yc[:, f], ACT.Square))
                    S(act.activation(yT[:, 4 + f], yc[:, f], ACT.Copy, scale=col(layer, "g_conv", f)), conv_sq)

                exponentials(0)
                for hh in range(HEADS):
                    if hh == 6:
                        convolved(3)
                    empty(("PT1", layer, hh), pT1[:, hh % 2].rearrange("p a b -> p (a b)"),
                          bank(("PT1", layer, hh))[:])
                    if hh + 1 < HEADS:
                        exponentials(hh + 1)
                    for nm, j in BESIDE_HEAD[hh]:
                        gate_tile(nm, j)
                    if hh == 5:
                        for f in range(3):
                            convolved(f)
                    if hh % 2 == 1:
                        j = hh // 2
                        full(act, ("Y1", layer, j))
                        S(act.activation(sq[:, j], bank(("Y1", layer, j))[:, 0:SEQ], ACT.Square))
                        empty(("Y1", layer, j), yT[:, j], bank(("Y1", layer, j))[:, 0:SEQ], ACT.Copy,
                              scale=col(layer, "g_attn", j))

                for t in range(NT):
                    emptied(act, ("out1", layer, 5 + 2 * t))
                    square(2 * layer + 1, t)
                even_hT(2 * layer + 1)
                load_gain(2 * layer + 2)
                act.wait_ge(route_exp_in, 2 * layer + 1)
                act.activation(small[:, 3, :, 0:GROUPS], small[:, 2, :, 0:GROUPS], ACT.Exp).then_inc(route_exp_out, 1)
                act.wait_ge(route_exp_in, 2 * layer + 2)
                act.activation(stat[:, 40:42], stat[:, 38:40], ACT.Exp).then_inc(route_exp_out, 1)
                if layer == DEPTH - 1:
                    full(act, ("rank", layer, 0))
                    act.dma_start(gain_second, gains_in[SECOND]).then_inc(gain_second_loaded, 16)
                empty(("gather", layer, 0), gathered(0, 0), bank(("gather", layer, 0))[:])
                act.wait_ge(trips_ready, layer + 1)
                n = act.value_load(trips_i[0:1, 0:1], min_val=GROUPS, max_val=GROUPS * ROUNDS)
                M = moe[layer]
                with act.Fori(0, n) as i:
                    def m_full(m):
                        act.wait_ge(M[f"full{4 + m % 4}"], i * PER_BANK + (m // 4 + 1))

                    def m_bank(m):
                        return banks[4 + m % 4]

                    for p in range(4):
                        b = p % 2
                        m0 = PAIR_TILES * p
                        for side in range(2):
                            m = m0 + T_GU + side
                            up, gate = (slice(0, 64), slice(64, P)) if side == 0 else (slice(64, P), slice(0, 64))
                            m_full(m)
                            act.activation(silu_g[up, b], m_bank(m)[gate, :], ACT.Silu).then_inc(M["silu"], 1)
                        m = m0 + T_NEXT
                        m_full(m)
                        act.copy(gathered(1 - b, 0), m_bank(m)[:]).then_inc(M[f"read{4 + m % 4}"], 1)
                        m = m0 + T_HID
                        m_full(m)
                        act.copy(hidT[:, b], m_bank(m)[:]).then_inc(M[f"read{4 + m % 4}"], 1)
                        m = m0 + T_OUT
                        m_full(m)
                        act.copy(ysb[:, b, 0:512], m_bank(m)[:]).then_inc(M[f"read{4 + m % 4}"], 1)

            for t in range(NT):
                act.wait_ge(moe[DEPTH - 1]["x_ready"], t + 1)
                square(BETWEEN, t)
            for layer in range(DEPTH):
                stage = SECOND + layer
                for t in range(NT):
                    if layer == 0:
                        act.wait_ge(h_ready, NT * BETWEEN + t + 1)
                    else:
                        emptied(act, ("out2", layer - 1, 2 + t))
                    square(stage, t)
                even_hT(stage)
                load_gain(stage + 1)
                for j in range(6):
                    w = min(2, RT - 2 * j)
                    empty(("xr", layer, j), xr[:, 2 * j:2 * j + w, TAPS2 - 1:],
                          bank(("xr", layer, j))[:, 0:w * SEQ].rearrange("p (a b) -> p a b", a=w))
                for c in range(14):
                    name = ("ropeT", layer, c)
                    if c < 12:
                        dst = (qT, kT, iqT)[c // 4]
                        pc, t = (c % 4) // 2, c % 2
                        empty(name, dst[:, 4 * pc:4 * pc + 4, t * P:(t + 1) * P],
                              bank(name)[:].rearrange("p (a b) -> p a b", a=4))
                    else:
                        t = c - 12
                        empty(name, ikT[:, t * P:(t + 1) * P], bank(name)[:, 0:P])
                for j in range(4):
                    pc, t = j // 2, j % 2
                    empty(("v", layer, j), vv[:, t, pc * 512:(pc + 1) * 512], bank(("v", layer, j))[:])
                for j in range(12):
                    full(act, ("dots", layer, j))
                    if layer * 12 + j >= 2:
                        act.wait_ge(relu_done, layer * 12 + j - 1)
                    empty(("dots", layer, j), relu[:, j % 2], bank(("dots", layer, j))[:], ACT.Relu)
                act.wait_ge(roped2, 14 * (layer + 1))
                for j in range(RT):
                    full(act, ("gates", layer, j))
                    S(act.activation(ra[:, j], bank(("gates", layer, j))[:, 0:SEQ], ACT.Sigmoid,
                                     bias=col(layer, "b_rg", j)))
                    empty(("gates", layer, j), ui[:, j], bank(("gates", layer, j))[:, SEQ:2 * SEQ], ACT.Sigmoid,
                          bias=col(layer, "b_ig", j))
                S.settle()
                act.wait_ge(decay_ready, 1)
                act.wait_ge(conv2_done, layer + 1)
                for j in range(RT):
                    S(act.activation(tanh_a[:, j], ra[:, j], ACT.Tanh, scale=decay[:, layer, j:j + 1]),
                      tanh_ready if j == RT - 1 else None)
                act.wait_ge(relu_done, 12 * (layer + 1))
                act.wait_ge(tanh_used, layer + 1)
                S(act.activation(tanh_a, tanh_a, ACT.Sqrt), root_ready)
                for j in range(6):
                    w = min(2, RT - 2 * j)
                    name = ("gr", layer, j)
                    full(act, name)
                    if j >= 2:
                        emptied(act, ("gr", layer, j - 2))
                    S(act.activation(roped[:, j % 2, 0:w * SEQ], bank(name)[:, 0:w * SEQ], ACT.Silu), silu_gr)

                def exponentials2(hh):
                    act.wait_ge(negmax2, layer * HEADS + hh + 1)
                    st = stat[:, 16 + 8 * (hh % 2):24 + 8 * (hh % 2)]
                    b = hh % 2
                    S(act.activation(s2[:, b, 0:P], s2[:, b, 0:P], ACT.Exp, bias=st[:, 2:3], accum_out=st[:, 4:5]))
                    S(act.activation(s2[:, b, P:], s2[:, b, P:], ACT.Exp, bias=st[:, 3:4], accum_out=st[:, 5:6]), exps2)

                act.wait_ge(hidden_ready, layer + 1)
                def gate(hh):
                    empty(("ga", layer, hh), ga_all[:, hh], bank(("ga", layer, hh))[:, 0:SEQ])

                exponentials2(0)
                gate(0)
                for hh in range(HEADS):
                    empty(("PT2", layer, hh), pT2[:, hh % 2], bank(("PT2", layer, hh))[:, 0:3 * P])
                    if hh + 1 < HEADS:
                        exponentials2(hh + 1)
                        gate(hh + 1)
                emptied(act, ("ga", layer, HEADS - 1))
                for half in range(2):
                    g = ga_all[:, 4 * half:4 * half + 4]
                    S(act.activation(g, g, ACT.Silu), silu_ga)
                for nm in ("mb", "ma"):
                    for j in range(8):
                        full(act, (nm, layer, j))
                        if (nm, j) not in (("mb", 0), ("mb", 1)):
                            emptied(act, (nm, layer, j - 2) if j >= 2 else ("mb", layer, 6 + j))
                        S(act.activation(s2.rearrange("p a b -> p (a b)")[:, (j % 2) * SEQ:(j % 2 + 1) * SEQ],
                                         bank((nm, layer, j))[:, 0:SEQ], ACT.Sigmoid), sig_ready)
            for t in range(NT):
                emptied(act, ("out2", DEPTH - 1, 2 + t))
                square(FINAL, t)

        @block.vector
        def _(dve):
            S = Steps(dve, own_dve)

            def normalise(stage, t, dst=h):
                k = NT * stage + t + 1
                dve.wait_ge(sumsq_ready, k)
                dve.tensor_scalar(stat[:, 2 + t:3 + t], stat[:, t:t + 1], 1.0 / D, EPS, ALU.mult, ALU.add
                                  ).then_inc(mean_ready, 1)
                dve.wait_ge(rstd_ready, k + min((stage + 1) // 2, DEPTH))
                if stage == SECOND:
                    dve.wait_ge(gain_second_loaded, 16)
                else:
                    dve.wait_ge(gain_loaded, 16 * (stage + (stage < SECOND)))
                S(dve.scalar_tensor_tensor(out=dst[:, t], in0=x[:, t], scalar=stat[:, 4 + t:5 + t],
                                           in1=gain_second if stage == SECOND else gain[:],
                                           op0=ALU.mult, op1=ALU.mult), h_ready)

            def odd_hT(stage):
                for j in (1, 3):
                    name = ("hT", stage, j)
                    full(dve, name)
                    dve.tensor_copy(hT[:, 2 * j:2 * j + 2].rearrange("p a b -> p (a b)"), bank(name)[:]
                                    ).then_inc(psum_read[TILE[name] % BANKS], 1)

            for t in range(NT):
                dve.wait_ge(x_loaded[t], 16)
                normalise(0, t)
            dve.wait_ge(masks_ready, 1)

            def second_block_tables():
                dve.wait_ge(consts_loaded, 48)
                lam = cols[:, :, COLS["lam"][0]:COLS["lam"][0] + RT]
                S(dve.tensor_scalar(lam_t[:, 3], lam, -1.0, None, ALU.mult))
                S.settle()
                dve.tensor_tensor(lam_t[:, 0], lam, lam_t[:, 3], ALU.max).then_inc(lam_in, 1)
                S(dve.tensor_copy(pos_f[:], pos_i[:]))
                S.settle()
                for t in range(NT):
                    S(dve.tensor_scalar(ang[:, t], rows[:, INV0:INV0 + INV2], pos_f[:, t:t + 1], None, ALU.mult))
                S.settle()
                S(dve.tensor_scalar(cos2[:], ang[:], float(1.0 / (2 * np.pi)), ROUNDER, ALU.mult, ALU.add))
                S.settle()
                S(dve.tensor_scalar(cos2[:], cos2[:], ROUNDER, None, ALU.subtract))
                for part in TWO_PI_PARTS:
                    S.settle()
                    S(dve.scalar_tensor_tensor(out=ang[:], in0=cos2[:], scalar=-part, in1=ang[:],
                                               op0=ALU.mult, op1=ALU.add))
                S.settle()
                S(dve.tensor_scalar(sin2[:], ang[:], 3.1415925, -3.1415925, ALU.min, ALU.max))
                S.settle()
                S(dve.scalar_tensor_tensor(out=cos2[:], in0=sin2[:], scalar=-1.0, in1=sin2[:], op0=ALU.mult, op1=ALU.max))
                S.settle()
                S(dve.tensor_scalar(cos2[:], cos2[:], -1.0, float(np.pi / 2), ALU.mult, ALU.add), angles_ready)
                dve.wait_ge(lam_exp, 1)
                S(dve.tensor_scalar(lam_t[:, 2], lam_t[:, 1], 2.0, None, ALU.add))
                S.settle()
                S(dve.reciprocal(lam_t[:, 2], lam_t[:, 2]))
                S.settle()
                S(dve.tensor_tensor(lam_t[:, 1], lam_t[:, 1], lam_t[:, 2], ALU.mult))
                S.settle()
                S(dve.tensor_tensor(lam_t[:, 2], lam_t[:, 1], lam_t[:, 1], ALU.mult))
                S.settle()
                S(dve.tensor_scalar(lam_t[:, 0], lam_t[:, 2], 2.0 / 17, None, ALU.mult))
                for n in (15, 13, 11, 9, 7, 5, 3):
                    S.settle()
                    S(dve.scalar_tensor_tensor(out=lam_t[:, 0], in0=lam_t[:, 0], scalar=2.0 / n, in1=lam_t[:, 2],
                                               op0=ALU.add, op1=ALU.mult))
                S.settle()
                S(dve.scalar_tensor_tensor(out=lam_t[:, 0], in0=lam_t[:, 0], scalar=2.0, in1=lam_t[:, 1],
                                           op0=ALU.add, op1=ALU.mult))
                S.settle()
                S(dve.scalar_tensor_tensor(out=lam_t[:, 3], in0=lam_t[:, 3], scalar=0.0, in1=lam_t[:, 0],
                                           op0=ALU.max, op1=ALU.add))
                S.settle()
                S(dve.tensor_scalar(decay[:], lam_t[:, 3], LRU_C / 2, None, ALU.mult), decay_ready)

            def first_mixer(layer):
                stage = 2 * layer
                odd_hT(stage)
                if layer == 0:
                    second_block_tables()
                for t in range(NT):
                    emptied(dve, ("q", layer, t))
                    emptied(dve, ("kv", layer, t))
                dve.wait_ge(rope1_loaded, 32)
                heads = [qkv[:, t, 0:QW + KVW].rearrange("p (h d) -> p h d", d=HD1) for t in range(NT)]
                tab = [[z.rearrange("p (t h d) -> p t h d", t=NT, d=ROT1)[:, t] for t in range(NT)] for z in (cos1, sin1)]
                tmp = [[rt1[:, z].rearrange("p (t h d) -> p t h d", t=NT, d=ROT1)[:, t] for t in range(NT)]
                       for z in range(4)]
                for t in range(NT):
                    a, b = heads[t][:, :, 0:ROT1], heads[t][:, :, ROT1:2 * ROT1]
                    S(dve.tensor_tensor(tmp[0][t], a, tab[0][t], ALU.mult))
                    S(dve.tensor_tensor(tmp[1][t], b, tab[1][t], ALU.mult))
                    S(dve.tensor_tensor(tmp[2][t], b, tab[0][t], ALU.mult))
                    S(dve.tensor_tensor(tmp[3][t], a, tab[1][t], ALU.mult))
                S.settle()
                for t in range(NT):
                    a, b = heads[t][:, :, 0:ROT1], heads[t][:, :, ROT1:2 * ROT1]
                    S(dve.tensor_tensor(a, tmp[0][t], tmp[1][t], ALU.subtract))
                    S(dve.tensor_tensor(b, tmp[2][t], tmp[3][t], ALU.add))
                S.settle()
                S(dve.tensor_copy(kswap[:, :, 0:HD1], qkv[:, :, QW + HD1:QW + KVW]))
                S(dve.tensor_copy(kswap[:, :, HD1:], qkv[:, :, QW:QW + HD1]), roped1)
                S(dve.memset(cu[:, :, 0:1], 0.0))
                S(dve.memset(cu[:, :, SEQ + 1:], 0.0))

                def gated_input(j):
                    name = ("u", layer, j)
                    emptied(dve, ("gc", layer, j))
                    full(dve, name)
                    S.settle()
                    S.marks(dve.tensor_tensor(cu[:, j, 1:SEQ + 1], bank(name)[:, 0:SEQ], gc[:, j], ALU.mult),
                            psum_read[TILE[name] % BANKS], uses(name))

                sink = rows[:, SINK0 + layer * HEADS:SINK0 + (layer + 1) * HEADS]

                def logits(hh):
                    name = ("S1", layer, hh)
                    st = stat[:, 16 + 8 * (hh % 2):24 + 8 * (hh % 2)]
                    full(dve, name)
                    if hh >= 2:
                        full(dve, ("PT1", layer, hh - 2))
                    S.marks(dve.scalar_tensor_tensor(out=s1[:, hh % 2], in0=bank(name)[:].rearrange("p (a b) -> p a b", a=2),
                                                     scalar=HD1 ** -0.5, in1=window, op0=ALU.mult, op1=ALU.add),
                            psum_read[TILE[name] % BANKS], uses(name))
                    S.settle()
                    S(dve.tensor_reduce(st[:, 0:2], s1[:, hh % 2], AX.X, ALU.max))
                    S.settle()
                    S(dve.tensor_scalar(st[:, 2:4], st[:, 0:2], sink[:, hh:hh + 1], -1.0, ALU.max, ALU.mult), negmax)

                def weights(hh):
                    st = stat[:, 16 + 8 * (hh % 2):24 + 8 * (hh % 2)]
                    dve.wait_ge(exps, layer * HEADS + hh + 1)
                    S(dve.tensor_tensor(st[:, 4:6], st[:, 4:6], st[:, 6:8], ALU.add))
                    S.settle()
                    S(dve.reciprocal(st[:, 4:6], st[:, 4:6]))
                    S.settle()
                    for qb in range(NT):
                        S(dve.tensor_scalar(s1[:, hh % 2, qb], s1[:, hh % 2, qb], st[:, 4 + qb:5 + qb], None, ALU.mult),
                          probs if qb == NT - 1 else None)

                logits(0)
                weights(0)
                gated_input(0)
                for hh in range(HEADS):
                    if hh + 1 < HEADS:
                        logits(hh + 1)
                        weights(hh + 1)
                    for nm, j in BESIDE_HEAD[hh]:
                        if nm == "u":
                            gated_input(j)
                name = ("ss", layer, 0)
                full(dve, name)
                S.marks(dve.tensor_scalar(stat[:, 8:12], bank(name)[:].rearrange("p (a b) -> p a b", b=P)[:, :, 0],
                                          1.0 / CW, EPS, ALU.mult, ALU.add), psum_read[TILE[name] % BANKS], uses(name))
                dve.wait_ge(rstd_ready, 5 * layer + 3)
                for i in range(8):
                    hf, t, part = OUT1[i]
                    name = ("out1", layer, i)
                    full(dve, name)
                    S.settle()
                    xs = x[:, t, hf * 512:(hf + 1) * 512]
                    S.marks(dve.scalar_tensor_tensor(out=xs, in0=bank(name)[:], scalar=stat[:, 12 + 2 * part + t:13 + 2 * part + t],
                                                     in1=xs, op0=ALU.mult, op1=ALU.add),
                            psum_read[TILE[name] % BANKS], uses(name))
                    if i in (5, 7):
                        S.settle()
                        normalise(stage + 1, t)

            def pick_first(dst, src, mx, idx, wide, far):
                n = src.shape[-1]
                S(dve.tensor_tensor(dst, src, mx.unsqueeze(2).to_broadcast([P, NT, n]), ALU.is_equal))
                S.settle()
                S(dve.scalar_tensor_tensor(out=wide, in0=dst, scalar=-far, in1=idx, op0=ALU.mult, op1=ALU.add))
                S.settle()
                S(dve.tensor_reduce(stat[:, 42:44], wide, AX.X, ALU.min))
                S.settle()
                S(dve.tensor_tensor(dst, wide, stat[:, 42:44].unsqueeze(2).to_broadcast([P, NT, n]), ALU.is_equal))
                S.settle()

            def router(layer):
                name = ("logits", layer, 0)
                full(dve, name)
                lg = bank(name)[:, 0:2 * P].rearrange("p (t n) -> p t n", t=NT)
                bias = rows[:, layer * ROUTER_W:(layer + 1) * ROUTER_W]
                idx = iota_f[:, 0:NE]
                for t in range(NT):
                    S(dve.tensor_tensor(small[:, 0, t, 0:GROUPS], lg[:, t, 0:GROUPS], bias[:, 0:GROUPS], ALU.add))
                S(dve.tensor_tensor(small[:, 1, 0], lg[:, 0, GROUPS:ROUTER_W], bias[:, GROUPS:], ALU.add))
                S.marks(dve.tensor_tensor(small[:, 1, 1], lg[:, 1, GROUPS:ROUTER_W], bias[:, GROUPS:], ALU.add),
                        psum_read[TILE[name] % BANKS], uses(name))
                S.settle()
                gl = small[:, 0, :, 0:GROUPS]
                gmax = stat[:, 32:34]
                S(dve.tensor_reduce(gmax, gl, AX.X, ALU.max))
                S.settle()
                S(dve.tensor_tensor(small[:, 2, :, 0:GROUPS], gl, gmax.unsqueeze(2).to_broadcast([P, NT, GROUPS]),
                                    ALU.subtract), route_exp_in)
                oh = small[:, 4, :, 0:GROUPS]
                idx_g = idx[:, 0:GROUPS].unsqueeze(1).to_broadcast([P, NT, GROUPS])
                pick_first(oh, gl, gmax, idx_g, small[:, 5, :, 0:GROUPS], 64.0)
                S(dve.tensor_scalar(oh, oh, -NEG, NEG, ALU.mult, ALU.add))
                S.settle()
                for t in range(NT):
                    S(dve.tensor_tensor(small[:, 6, t].rearrange("p (g e) -> p g e", g=GROUPS),
                                        small[:, 1, t].rearrange("p (g e) -> p g e", g=GROUPS),
                                        small[:, 4, t, 0:GROUPS].unsqueeze(2).to_broadcast([P, GROUPS, PER_GROUP]), ALU.add))
                S.settle()
                idx_e = idx.unsqueeze(1).to_broadcast([P, NT, NE])
                m1, m2 = stat[:, 34:36], stat[:, 36:38]
                S(dve.tensor_reduce(m1, small[:, 6], AX.X, ALU.max))
                S.settle()
                pick_first(small[:, 7], small[:, 6], m1, idx_e, small[:, 5], 64.0)
                S(dve.scalar_tensor_tensor(out=small[:, 8], in0=small[:, 7], scalar=TAKEN, in1=small[:, 6],
                                           op0=ALU.mult, op1=ALU.add))
                S.settle()
                S(dve.tensor_reduce(m2, small[:, 8], AX.X, ALU.max))
                S.settle()
                pick_first(small[:, 9], small[:, 8], m2, idx_e, small[:, 5], 64.0)
                S(dve.tensor_tensor(small[:, 10], small[:, 7], small[:, 9], ALU.add), assign_ready)
                S(dve.tensor_tensor(stat[:, 38:40], m2, m1, ALU.subtract), route_exp_in)
                dve.wait_ge(route_exp_out, 2 * layer + 2)
                S(dve.tensor_reduce(stat[:, 44:46], small[:, 3, :, 0:GROUPS], AX.X, ALU.add))
                S(dve.tensor_scalar(stat[:, 46:48], stat[:, 40:42], 1.0, None, ALU.add))
                S.settle()
                S(dve.tensor_tensor(stat[:, 46:48], stat[:, 46:48], stat[:, 44:46], ALU.mult))
                S.settle()
                S(dve.reciprocal(stat[:, 46:48], stat[:, 46:48]))
                S.settle()
                S(dve.tensor_tensor(stat[:, 48:50], stat[:, 46:48], stat[:, 40:42], ALU.mult))
                S.settle()
                for t in range(NT):
                    S(dve.tensor_scalar(small[:, 11, t], small[:, 7, t], stat[:, 46 + t:47 + t], None, ALU.mult))
                S.settle()
                for t in range(NT):
                    S(dve.scalar_tensor_tensor(out=small[:, 12, t], in0=small[:, 9, t], scalar=stat[:, 48 + t:49 + t],
                                               in1=small[:, 11, t], op0=ALU.mult, op1=ALU.add))
                name = ("rank", layer, 0)
                full(dve, name)
                rk = bank(name)[:, 0:3 * NE].rearrange("p (a n) -> p a n", a=3)
                S(dve.scalar_tensor_tensor(out=small[:, 13], in0=rk[:, 0:NT], scalar=1.0, in1=small[:, 10],
                                           op0=ALU.add, op1=ALU.mult))
                S.settle()
                S(dve.tensor_scalar(small[:, 14], small[:, 13], -1.0, None, ALU.add))
                S.marks(dve.tensor_reduce(stat[:, 50:51], rk[:, 2], AX.X, ALU.max),
                        psum_read[TILE[name] % BANKS], uses(name))
                S.settle()

            def turns(layer):
                S.settle()
                for r in range(1, ROUNDS):
                    S(dve.tensor_scalar(stat[:, 50 + r:51 + r], stat[:, 50:51], float(SLOTS * r), float(GROUPS),
                                        ALU.is_gt, ALU.mult))
                S.settle()
                S(dve.tensor_reduce(stat[:, 54:55], stat[:, 51:50 + ROUNDS], AX.X, ALU.add))
                S.settle()
                S(dve.tensor_scalar(trips_i[:, 1:2], stat[:, 54:55], float(GROUPS - 1), None, ALU.add))
                S(dve.tensor_scalar(trips_i[:, 0:1], stat[:, 54:55], float(GROUPS), None, ALU.add), trips_ready)
                S.settle()

            def experts(layer):
                M = moe[layer]

                def picks(T, g):
                    slots = small[:, 14, :, bass.ds(g, PER_GROUP)]
                    for t in range(NT):
                        T(dve.tensor_tensor(pick[:, t], iota_f[:].unsqueeze(1).to_broadcast([P, PER_GROUP, SLOTS]),
                                            slots[:, t].unsqueeze(2).to_broadcast([P, PER_GROUP, SLOTS]), ALU.is_equal))
                    T.settle()
                    T(dve.tensor_scalar(slots, slots, -float(SLOTS), None, ALU.add), M["picked"])

                def weighted_picks(T, g):
                    gates = small[:, 12, :, bass.ds(g, PER_GROUP)]
                    T.settle()
                    for t in range(NT):
                        T(dve.tensor_tensor(wpick[:, t], pick[:, t],
                                            gates[:, t].unsqueeze(2).to_broadcast([P, PER_GROUP, SLOTS]), ALU.mult),
                          M["wpicked"] if t == NT - 1 else None)
                    T.settle()

                picks(S, 0)
                turns(layer)
                weighted_picks(S, 0)
                name = ("gather", layer, 1)
                full(dve, name)
                dve.tensor_copy(gathered(0, 1), bank(name)[:]).then_inc(psum_read[TILE[name] % BANKS], 1)
                n = dve.value_load(trips_i[0:1, 0:1], min_val=GROUPS, max_val=GROUPS * ROUNDS)
                STEPS = 3
                with dve.Fori(0, n) as i:
                    T = Steps(dve, M["dve"], {M["dve"].name: i * STEPS, M["picked"].name: i + 1,
                                              M["wpicked"].name: i + 1})
                    next_group = ((i + 1) % GROUPS) * PER_GROUP

                    def m_full(m):
                        dve.wait_ge(M[f"full{4 + m % 4}"], i * PER_BANK + (m // 4 + 1))

                    def m_bank(m):
                        return banks[4 + m % 4]

                    for p in range(4):
                        b = p % 2
                        m0 = PAIR_TILES * p
                        m = m0 + T_COMB
                        m_full(m)
                        dve.tensor_copy(comb[:, b], m_bank(m)[:, 0:SEQ]).then_inc(M[f"read{4 + m % 4}"], 1)
                        for side in range(2):
                            m = m0 + T_GU + side
                            up = slice(0, 64) if side == 0 else slice(64, P)
                            dve.wait_ge(M["silu"], i * 8 + (2 * p + side + 1))
                            dve.tensor_tensor(hid[up, b], silu_g[up, b], m_bank(m)[up, :], ALU.mult
                                              ).then_inc(M[f"read{4 + m % 4}"], 1)
                        if p == 3:
                            weighted_picks(T, next_group)
                        m = m0 + T_NEXT + 1
                        m_full(m)
                        dve.tensor_copy(gathered(1 - b, 1), m_bank(m)[:]).then_inc(M[f"read{4 + m % 4}"], 1)
                        if p == 2:
                            picks(T, next_group)
                        m = m0 + T_OUT + 1
                        m_full(m)
                        dve.tensor_copy(ysb[:, b, 512:], m_bank(m)[:]).then_inc(M[f"read{4 + m % 4}"], 1)
                    assert T.n[M["dve"].name] == STEPS
                dve.wait_ge(M["scattered"], n)
                for t in range(NT):
                    for hf in range(2):
                        xs = x[:, t, hf * 512:(hf + 1) * 512]
                        S(dve.tensor_tensor(xs, banks[2 * t + hf][:], xs, ALU.add), M["x_ready"] if hf else None)
                for t in range(NT):
                    normalise(2 * layer + 2, t, h if layer + 1 < DEPTH else x)

            def second(layer):
                stage = SECOND + layer
                if layer == 0:
                    dve.wait_ge(tables2_ready, 1)
                    S.settle()
                S(dve.memset(xr[:, :, 0:TAPS2 - 1], 0.0))
                odd_hT(stage)
                for j in range(RT):
                    emptied(dve, ("xr", layer, j // 2))
                    if j == 0:
                        S.settle()
                    S(dve.tensor_scalar(xc[:, j], xr[:, j, 0:SEQ], col(layer, "conv2", j), col(layer, "conv2_b", j),
                                        ALU.mult, ALU.add))
                    for tap in range(1, TAPS2):
                        S.settle()
                        S(dve.scalar_tensor_tensor(out=xc[:, j], in0=xr[:, j, tap:tap + SEQ],
                                                   scalar=col(layer, "conv2", tap * RT + j), in1=xc[:, j],
                                                   op0=ALU.mult, op1=ALU.add),
                          conv2_done if (j, tap) == (RT - 1, TAPS2 - 1) else None)
                for c in range(14):
                    name = ("rope", layer, c)
                    t = c % 2
                    full(dve, name)
                    if c >= 4:
                        full(dve, ("ropeT", layer, c - 4))
                    half = HD2 // 2 if c < 8 else ID // 2
                    t0 = 0 if c < 8 else HD2 // 2
                    nh = 512 // (2 * half) if c < 12 else 1
                    src = bank(name)[:, 0:nh * 2 * half].rearrange("p (h s d) -> p h s d", h=nh, s=2)
                    dst = roped[:, c % 4, 0:nh * 2 * half].rearrange("p (h s d) -> p h s d", h=nh, s=2)
                    tmp = ropetmp[:, c % 2, 0:nh * 2 * half].rearrange("p (h s d) -> p h s d", h=nh, s=2)
                    cs = cos2[:, t, t0:t0 + half].unsqueeze(1).to_broadcast([P, nh, half])
                    sn = sin2[:, t, t0:t0 + half].unsqueeze(1).to_broadcast([P, nh, half])
                    for s in range(2):
                        S(dve.tensor_tensor(dst[:, :, s], src[:, :, s], cs, ALU.mult))
                        S(dve.tensor_tensor(tmp[:, :, s], src[:, :, 1 - s], sn, ALU.mult))
                    if c >= 12:
                        S(dve.tensor_scalar(iw[:, t], bank(name)[:, ID:ID + IH], IH ** -0.5 * ID ** -0.5, None, ALU.mult))
                    S.settle()
                    S.marks(dve.tensor_tensor(dst[:, :, 0], dst[:, :, 0], tmp[:, :, 0], ALU.subtract),
                            psum_read[TILE[name] % BANKS], uses(name))
                    S(dve.tensor_tensor(dst[:, :, 1], dst[:, :, 1], tmp[:, :, 1], ALU.add), roped2 if c < 12 else None)
                    if c >= 12:
                        S.settle()
                        S(dve.tensor_copy(roped[:, c % 4, ID:2 * ID], roped[:, c % 4, 0:ID]), roped2)
                for j in range(12):
                    emptied(dve, ("dots", layer, j))
                    for piece_ in range(4 if j < 4 else 2):
                        if j < 4:
                            hd = 8 * (j // 2) + 2 * piece_ + j % 2
                            acc, src, qb = wk[:, 0, 0:P], relu[:, j % 2, piece_ * P:(piece_ + 1) * P], 0
                        else:
                            jj = j - 4
                            hd = 4 * (jj // 2) + 2 * piece_ + jj % 2
                            acc, src, qb = wk[:, 0, P:], relu[:, j % 2, piece_ * SEQ:(piece_ + 1) * SEQ], 1
                        lastp = piece_ == (3 if j < 4 else 1)
                        S.settle()
                        if hd == 0:
                            ins = dve.tensor_scalar(acc, src, iw[:, qb, hd:hd + 1], None, ALU.mult)
                        else:
                            ins = dve.scalar_tensor_tensor(out=acc, in0=src, scalar=iw[:, qb, hd:hd + 1], in1=acc,
                                                           op0=ALU.mult, op1=ALU.add)
                        S(ins, relu_done if lastp else None)
                S.settle()
                S(dve.tensor_tensor(wk[:, 0], wk[:, 0], causal[:], ALU.add))
                S.settle()
                for r in range(TOPK // 8):
                    a, b = r % 2, (r + 1) % 2
                    for sl in (slice(0, P), slice(P, 3 * P)):
                        o = 0 if sl.start == 0 else 8
                        S(dve.max(top8[:, o:o + 8], wk[:, a, sl]))
                    S.settle()
                    for sl in (slice(0, P), slice(P, 3 * P)):
                        o = 0 if sl.start == 0 else 8
                        S(dve.match_replace(wk[:, b, sl], top8[:, o:o + 8], wk[:, a, sl], TAKEN))
                    S.settle()
                S(dve.tensor_scalar(wk[:, 1], wk[:, 0], TAKEN, -NEG, ALU.is_equal, ALU.mult))
                S.settle()
                S(dve.scalar_tensor_tensor(out=bias2, in0=wk[:, 1], scalar=NEG, in1=causal[:], op0=ALU.add, op1=ALU.add))
                S.settle()
                emptied(dve, ("gates", layer, RT - 1))
                S(dve.tensor_tensor(ui, ui, xc, ALU.mult))
                S.settle()
                dve.wait_ge(tanh_ready, layer + 1)
                S(dve.tensor_scalar(xc, tanh_a, 1.0, None, ALU.add), tanh_used)
                S.settle()
                S(dve.reciprocal(xc, xc))
                S.settle()
                S(dve.tensor_scalar(ra, xc, 2.0, -1.0, ALU.mult, ALU.add))
                S(dve.scalar_tensor_tensor(out=ui, in0=xc, scalar=2.0, in1=ui, op0=ALU.mult, op1=ALU.mult))
                S.settle()
                dve.wait_ge(root_ready, layer + 1)
                S(dve.tensor_tensor(ui, ui, tanh_a, ALU.mult))
                S.settle()
                for j in range(RT):
                    S(dve.tensor_tensor_scan(xc[:, j], ra[:, j], ui[:, j], 0.0, ALU.mult, ALU.add),
                      hidden_ready if j == RT - 1 else None)
                S.settle()
                for j in range(6):
                    w = min(2, RT - 2 * j)
                    name = ("gr", layer, j)
                    dve.wait_ge(silu_gr, layer * 6 + j + 1)
                    S.marks(dve.tensor_tensor(ui[:, 2 * j:2 * j + w], xc[:, 2 * j:2 * j + w],
                                              roped[:, j % 2, 0:w * SEQ].rearrange("p (a b) -> p a b", a=w), ALU.mult),
                            psum_read[TILE[name] % BANKS], uses(name))
                S.settle()

                def logits(hh):
                    name = ("S2", layer, hh)
                    st = stat[:, 16 + 8 * (hh % 2):24 + 8 * (hh % 2)]
                    b = hh % 2
                    full(dve, name)
                    if hh >= 2:
                        full(dve, ("PT2", layer, hh - 2))
                    S.marks(dve.scalar_tensor_tensor(out=s2[:, b], in0=bank(name)[:, 0:3 * P], scalar=HD2 ** -0.5,
                                                     in1=bias2, op0=ALU.mult, op1=ALU.add),
                            psum_read[TILE[name] % BANKS], uses(name))
                    S.settle()
                    S(dve.tensor_reduce(st[:, 0:1], s2[:, b, 0:P], AX.X, ALU.max))
                    S(dve.tensor_reduce(st[:, 1:2], s2[:, b, P:], AX.X, ALU.max))
                    S.settle()
                    S(dve.tensor_scalar(st[:, 2:4], st[:, 0:2], -1.0, None, ALU.mult), negmax2)

                def weights(hh):
                    st = stat[:, 16 + 8 * (hh % 2):24 + 8 * (hh % 2)]
                    b = hh % 2
                    dve.wait_ge(exps2, layer * HEADS + hh + 1)
                    S(dve.reciprocal(st[:, 4:6], st[:, 4:6]))
                    S.settle()
                    S(dve.tensor_scalar(s2[:, b, 0:P], s2[:, b, 0:P], st[:, 4:5], None, ALU.mult))
                    S(dve.tensor_scalar(s2[:, b, P:], s2[:, b, P:], st[:, 5:6], None, ALU.mult), probs2)

                def attended(hh):
                    name = ("Y2", layer, hh)
                    full(dve, name)
                    S.marks(dve.tensor_copy(qT[:, hh], bank(name)[:, 0:SEQ]), psum_read[TILE[name] % BANKS], uses(name))

                logits(0)
                weights(0)
                for hh in range(HEADS):
                    if hh + 1 < HEADS:
                        logits(hh + 1)
                        weights(hh + 1)
                    attended(hh)
                S.settle()
                for half in range(2):
                    dve.wait_ge(silu_ga, 2 * layer + half + 1)
                    y = qT[:, 4 * half:4 * half + 4]
                    S(dve.tensor_tensor(y, y, ga_all[:, 4 * half:4 * half + 4], ALU.mult), attn_gated)
                sig = [s2.rearrange("p a b -> p (a b)")[:, b * SEQ:(b + 1) * SEQ] for b in range(2)]
                for j in range(8):
                    name = ("mb", layer, j)
                    dve.wait_ge(sig_ready, layer * 16 + j + 1)
                    S.marks(dve.tensor_tensor(merged[:, j], sig[j % 2], bank(name)[:, SEQ:], ALU.mult),
                            psum_read[TILE[name] % BANKS], uses(name))
                for j in range(8):
                    name = ("ma", layer, j)
                    dve.wait_ge(sig_ready, layer * 16 + 8 + j + 1)
                    S.settle()
                    S.marks(dve.tensor_tensor(pT2[:, 0, 0:SEQ], sig[j % 2], bank(name)[:, SEQ:], ALU.mult),
                            psum_read[TILE[name] % BANKS], uses(name))
                    S.settle()
                    S(dve.tensor_tensor(merged[:, j], merged[:, j], pT2[:, 0, 0:SEQ], ALU.add), merged_ready)
                for i in range(4):
                    name = ("out2", layer, i)
                    pc, t = i // 2, i % 2
                    full(dve, name)
                    xs = x[:, t, pc * 512:(pc + 1) * 512]
                    S.marks(dve.tensor_tensor(xs, bank(name)[:], xs, ALU.add), psum_read[TILE[name] % BANKS], uses(name))
                    if pc == 1:
                        S.settle()
                        normalise(stage + 1, t)

            for layer in range(DEPTH):
                first_mixer(layer)
                odd_hT(2 * layer + 1)
                router(layer)
                experts(layer)
            S(dve.tensor_scalar(causal[:, 0:P], before[:], NEG, None, ALU.mult))
            S(dve.memset(causal[:, P:2 * P], 0.0))
            S(dve.tensor_scalar(causal[:, 2 * P:], before[:], NEG, None, ALU.mult))
            S.settle()
            for t in range(NT):
                normalise(SECOND, t)
            for layer in range(DEPTH):
                second(layer)

        @block.tensor
        def _(pe):
            def claim(name):
                if TILE[name] >= BANKS:
                    pe.wait_ge(psum_read[TILE[name] % BANKS], uses(name) - 1)

            def done(mm, name):
                mm.then_inc(psum_full[TILE[name] % BANKS], 1)

            def keep_clock(name, n):
                claim(name)
                for _ in range(n):
                    pe.matmul(bank(name)[:, 0:P], zeros[:], ones[:], start=True, stop=True)

            def turn_h(stage, idle):
                after_experts = stage > 0 and stage % 2 == 0
                keep_clock(next(("hT", stage, j) for j in range(4)
                                if not after_experts or TILE[("hT", stage, j)] % BANKS >= MOE_BANKS), idle)
                for t in range(NT):
                    pe.wait_ge(h_ready, NT * stage + t + 1)
                    for j in range(4):
                        name = ("hT", stage, j)
                        if t == 0:
                            claim(name)
                        for k in range(2):
                            f = 2 * j + k
                            mm = pe.transpose(bank(name)[:, k * SEQ + t * P:k * SEQ + (t + 1) * P],
                                              h[:, t, f * P:(f + 1) * P], ident[:])
                        if t == NT - 1:
                            done(mm, name)
                for j in range(4):
                    emptied(pe, ("hT", stage, j))

            def by_token(name, w, n, t):
                claim(name)
                for k in range(KD):
                    mm = pe.matmul(bank(name)[:, 0:n], hT[:, k, t * P:(t + 1) * P], w[:, k, 0:n],
                                   start=(k == 0), stop=(k == KD - 1))
                done(mm, name)

            def by_feature(dst, w, f, rhs=None, nk=KD):
                rhs = hT if rhs is None else rhs
                for k in range(nk):
                    mm = pe.matmul(dst, w[:, k, f * P:(f + 1) * P], rhs[:, k], start=(k == 0), stop=(k == nk - 1))
                return mm

            def gather(dst, half, pair):
                for kk in range(KD // 2):
                    k = half * KD // 2 + kk
                    for t in range(NT):
                        mm = pe.matmul(dst[:, kk * P:(kk + 1) * P], h[:, t, k * P:(k + 1) * P],
                                       pick[:, t, 2 * pair:2 * pair + 2].rearrange("p a b -> p (a b)"),
                                       start=(t == 0), stop=(t == NT - 1))
                return mm

            pe.wait_ge(masks_ready, 1)

            for layer in range(DEPTH):
                seg = f"mix{layer}"

                def arrive(j):
                    pe.wait_ge(w_loaded[seg][mixer_piece(j)], mixer_count(j))
                    return piece(mixer_piece(j), KD, MIX_PIECES[j][2])

                turn_h(2 * layer, IDLE_START if layer == 0 else IDLE_EXPERTS)
                w = arrive(0)
                for t in range(NT):
                    by_token(("q", layer, t), w, 512, t)
                w = arrive(1)
                for t in range(NT):
                    by_token(("kv", layer, t), w, 2 * KVW, t)

                def gate_tile(nm, j):
                    w_ = arrive({"gc": 2, "u": 3, "gb": 4}[nm])
                    name = (nm, layer, j)
                    claim(name)
                    done(by_feature(bank(name)[:, 0:SEQ], w_, j), name)

                gate_tile("gc", 0)
                gate_tile("gc", 1)
                pe.wait_ge(roped1, layer + 1)
                for j in range(3):
                    name = ("qkT", layer, j)
                    claim(name)
                    for k in range(2):
                        for t in range(NT):
                            src = (qkv[:, t, (2 * j + k) * P:(2 * j + k + 1) * P] if j < 2 else
                                   (qkv[:, t, QW:QW + KVW] if k == 0 else kswap[:, t]))
                            mm = pe.transpose(bank(name)[:, k * SEQ + t * P:k * SEQ + (t + 1) * P], src, ident[:])
                    done(mm, name)
                for j in range(3):
                    emptied(pe, ("qkT", layer, j))

                def scores(hh):
                    name = ("S1", layer, hh)
                    claim(name)
                    r = slice(64 * (hh % 2), 64 * (hh % 2) + 64)
                    kk = kT1[r, 0 if hh % 2 == hh // 4 else 1]
                    for qb in range(NT):
                        mm = pe.matmul(bank(name)[:, qb * SEQ:(qb + 1) * SEQ], qT1[r, hh // 2, qb * P:(qb + 1) * P], kk,
                                       start=True, stop=True)
                    done(mm, name)

                def mixer_out(i):
                    hf, t, part = OUT1[i]
                    name = ("out1", layer, i)
                    w_ = arrive(5 + hf)
                    claim(name)
                    for j in range(4):
                        mm = pe.matmul(bank(name)[:], yT[:, 4 * part + j, t * P:(t + 1) * P], w_[:, 4 * part + j],
                                       start=(j == 0), stop=(j == 3))
                    done(mm, name)

                scores(0)
                gate_tile("u", 0)
                for hh in range(HEADS):
                    if hh + 1 < HEADS:
                        scores(hh + 1)
                    name = ("PT1", layer, hh)
                    claim(name)
                    pe.wait_ge(probs, layer * HEADS + hh + 1)
                    for kb in range(NT):
                        for qb in range(NT):
                            mm = pe.transpose(bank(name)[:, kb * SEQ + qb * P:kb * SEQ + (qb + 1) * P],
                                              s1[:, hh % 2, qb, kb * P:(kb + 1) * P], ident[:])
                    done(mm, name)
                    for nm, j in BESIDE_HEAD[hh]:
                        if nm == "out1":
                            pe.wait_ge(conv_sq, 4 * layer + 4)
                            mixer_out(j)
                        else:
                            gate_tile(nm, j)
                    emptied(pe, ("PT1", layer, hh))
                    yn = ("Y1", layer, hh // 2)
                    if hh % 2 == 0:
                        claim(yn)
                    r = slice(64 * (hh % 2), 64 * (hh % 2) + 64)
                    v0 = QW + KVW + (hh // 4) * HD1
                    for kb in range(NT):
                        mm = pe.matmul(bank(yn)[r, 0:SEQ], qkv[:, kb, v0:v0 + HD1], pT1[:, hh % 2, kb],
                                       start=(kb == 0), stop=(kb == NT - 1))
                    if hh % 2 == 1:
                        done(mm, yn)
                for j in range(4):
                    emptied(pe, ("Y1", layer, j))
                name = ("ss", layer, 0)
                claim(name)
                for part in range(2):
                    for t in range(NT):
                        o = (2 * part + t) * P
                        for j in range(4):
                            mm = pe.matmul(bank(name)[:, o:o + P], sq[:, 4 * part + j, t * P:(t + 1) * P], ones[:],
                                           start=(j == 0), stop=(j == 3))
                done(mm, name)
                for i in range(2, 8):
                    mixer_out(i)

                turn_h(2 * layer + 1, IDLE_MIXER)
                pe.wait_ge(router_loaded, 16 * (layer + 1))
                name = ("logits", layer, 0)
                claim(name)
                for t in range(NT):
                    for k in range(KD):
                        mm = pe.matmul(bank(name)[:, t * P:(t + 1) * P], hT[:, k, t * P:(t + 1) * P], w_router[:, k],
                                       start=(k == 0), stop=(k == KD - 1))
                done(mm, name)
                name = ("rank", layer, 0)
                keep_clock(name, IDLE_ROUTER)
                pe.wait_ge(assign_ready, layer + 1)
                A = small[:, 10]
                pe.matmul(bank(name)[:, 0:NE], before[:], A[:, 0], start=True, stop=True)
                pe.matmul(bank(name)[:, NE:2 * NE], before[:], A[:, 1], start=True, stop=False)
                pe.matmul(bank(name)[:, NE:2 * NE], ones[:], A[:, 0], start=False, stop=True)
                pe.matmul(bank(name)[:, 2 * NE:3 * NE], ones[:], A[:, 0], start=True, stop=False)
                mm = pe.matmul(bank(name)[:, 2 * NE:3 * NE], ones[:], A[:, 1], start=False, stop=True)
                done(mm, name)

                keep_clock(("gather", layer, 0), IDLE_PICKS)
                pe.wait_ge(moe[layer]["picked"], 1)
                for half in range(2):
                    name = ("gather", layer, half)
                    claim(name)
                    done(gather(bank(name), half, 0), name)
                M = moe[layer]
                seg = f"moe{layer}"
                last_static = TILE[("gather", layer, 1)]
                for b in range(BANKS):
                    n_b = last_static // BANKS + (1 if b <= last_static % BANKS else 0)
                    pe.wait_ge(psum_read[b], n_b)
                for b in range(4):
                    pe.matmul(banks[b][:], zeros[:], x[:, 0, 0:512], start=True, stop=True, skip_group_check=True)
                pe.wait_ge(trips_ready, layer + 1)
                n = pe.value_load(trips_i[0:1, 0:1], min_val=GROUPS, max_val=GROUPS * ROUNDS)
                with pe.Fori(0, n) as i:
                    def m_claim(m):
                        if m >= MOE_BANKS:
                            pe.wait_ge(M[f"read{4 + m % 4}"], i * PER_BANK + m // 4)

                    def m_emptied(m):
                        pe.wait_ge(M[f"read{4 + m % 4}"], i * PER_BANK + (m // 4 + 1))

                    def m_bank(m):
                        return banks[4 + m % 4]

                    def m_done(mm, m):
                        mm.then_inc(M[f"full{4 + m % 4}"], 1)

                    def weights_in(p, idx):
                        n = PER_PAIR * p + idx
                        pe.wait_ge(w_loaded[seg][n % MOE_RING], (i * ROUND_TRIPS + (n // MOE_RING + 1)) * 16)
                        return piece(n % MOE_RING, *((KD, DE) if idx < 4 else (FE, D)))

                    def scatter(p):
                        b = p % 2
                        for m in (T_COMB, T_OUT, T_OUT + 1):
                            m_emptied(PAIR_TILES * p + m)
                        for t in range(NT):
                            for hf in range(2):
                                mm = pe.matmul(banks[2 * t + hf][:], comb[:, b, t * P:(t + 1) * P],
                                               ysb[:, b, hf * 512:(hf + 1) * 512], start=False, stop=True,
                                               skip_group_check=True)
                        return mm

                    for p in range(4):
                        b = p % 2
                        m0 = PAIR_TILES * p
                        m_claim(m0)
                        if p == 0:
                            pe.wait_ge(M["wpicked"], i + 1)
                        for t in range(NT):
                            mm = pe.transpose(m_bank(m0)[:, t * P:(t + 1) * P],
                                              wpick[:, t, 2 * p:2 * p + 2].rearrange("p a b -> p (a b)"), ident[:])
                        m_done(mm, m0)
                        if p > 0:
                            m_emptied(m0 - PAIR_TILES + T_NEXT)
                            m_emptied(m0 - PAIR_TILES + T_NEXT + 1)
                        for side in range(2):
                            m = m0 + T_GU + side
                            up, gate = (slice(0, 64), slice(64, P)) if side == 0 else (slice(64, P), slice(0, 64))
                            wg, wu = weights_in(p, 2 * side), weights_in(p, 2 * side + 1)
                            m_claim(m)
                            for k in range(KD):
                                lhs = xg[:, b * KD + k, side * SLOTS:(side + 1) * SLOTS]
                                pe.matmul(m_bank(m)[gate, :], lhs, wg[:, k], start=(k == 0), stop=(k == KD - 1),
                                          skip_group_check=True)
                                mu = pe.matmul(m_bank(m)[up, :], lhs, wu[:, k], start=(k == 0), stop=(k == KD - 1),
                                               skip_group_check=True)
                            m_done(mu, m)
                        if p > 0:
                            scatter(p - 1)
                        if p == 3:
                            pe.wait_ge(M["picked"], i + 2)
                        for half in range(2):
                            m = m0 + T_NEXT + half
                            m_claim(m)
                            m_done(gather(m_bank(m), half, (p + 1) % 4), m)
                        m = m0 + T_HID
                        m_claim(m)
                        m_emptied(m0 + T_GU)
                        m_emptied(m0 + T_GU + 1)
                        for f in range(FE):
                            mm = pe.transpose(m_bank(m)[:, f * P:(f + 1) * P], hid[:, b, f * P:(f + 1) * P], ident[:])
                        m_done(mm, m)
                        m_claim(m0 + T_OUT)
                        m_claim(m0 + T_OUT + 1)
                        wd = [weights_in(p, 4), weights_in(p, 5)]
                        m_emptied(m)
                        for f in range(FE):
                            for hf in range(2):
                                for side in range(2):
                                    r = slice(64 * side, 64 * side + 64)
                                    mm = pe.matmul(m_bank(m0 + T_OUT + hf)[r, :],
                                                   hidT[:, b, f * P + 64 * side:f * P + 64 * side + 64],
                                                   wd[side][:, f, hf * 512:(hf + 1) * 512],
                                                   start=(f == 0), stop=(f == FE - 1), skip_group_check=True)
                                    if f == FE - 1 and side == 1:
                                        m_done(mm, m0 + T_OUT + hf)
                    scatter(3).then_inc(M["scattered"], 1)
                    for half in range(2):
                        m_emptied(PAIR_TILES * 3 + T_NEXT + half)

            for layer in range(DEPTH):
                def arrive2(j):
                    at = layer * NB2 + j
                    kind, _, n = B2_PIECES[j]
                    pe.wait_ge(w_loaded["b2"][at % RING], 16 * (at // RING + 1))
                    if kind == "lru":
                        return ring[:, at % RING, 0:n].rearrange("p (b n) -> p b n", n=P)
                    return piece(at % RING, RT if kind == "or" else KD, n)

                if layer == 0:
                    pe.wait_ge(moe[DEPTH - 1]["x_ready"], NT)
                turn_h(SECOND + layer, IDLE_BETWEEN if layer == 0 else IDLE_MIXER)

                def rnn_inputs(nm, p0):
                    for j in range(6):
                        if j % 2 == 0:
                            w_ = arrive2(p0 + j // 2)
                        name = (nm, layer, j)
                        claim(name)
                        for f in range(min(2, RT - 2 * j)):
                            mm = by_feature(bank(name)[:, f * SEQ:(f + 1) * SEQ], w_, 2 * (j % 2) + f)
                        done(mm, name)

                rnn_inputs("xr", PXR)

                def turn_rope(c):
                    name = ("ropeT", layer, c)
                    claim(name)
                    pe.wait_ge(roped2, 14 * layer + c + 1)
                    for k in range(4 if c < 12 else 1):
                        mm = pe.transpose(bank(name)[:, k * P:(k + 1) * P], roped[:, c % 4, k * P:(k + 1) * P], ident[:])
                    done(mm, name)

                for c in range(15):
                    if c < 14:
                        name = ("rope", layer, c)
                        if c % 2 == 0:
                            w = arrive2(PROPE + c // 2)
                        by_token(name, w, 512 if c < 12 else P, c % 2)
                    if c >= 2:
                        turn_rope(c - 2)
                turn_rope(13)

                for j in range(4):
                    name = ("v", layer, j)
                    if j % 2 == 0:
                        w = arrive2(PV + j // 2)
                    by_token(name, w, 512, j % 2)
                for c in range(8, 14):
                    emptied(pe, ("ropeT", layer, c))
                for j in range(0, 12, 2):
                    names = [("dots", layer, j), ("dots", layer, j + 1)]
                    for n_ in names:
                        claim(n_)
                    cnt, w_ = (4, P) if j < 4 else (2, SEQ)
                    for k in range(cnt):
                        for odd in range(2):
                            if j < 4:
                                hd, qb = 8 * (j // 2) + 2 * k + odd, 0
                            else:
                                hd, qb = 4 * ((j - 4) // 2) + 2 * k + odd, 1
                            r = slice(64 * odd, 64 * odd + 64)
                            mm = pe.matmul(bank(names[odd])[:, k * w_:(k + 1) * w_], iqT[r, hd // 2, qb * P:(qb + 1) * P],
                                           ikT[r, 0:w_], start=True, stop=True)
                            if k == cnt - 1:
                                done(mm, names[odd])
                wr, wi = arrive2(PLRU), arrive2(PLRU + 1)
                pe.wait_ge(conv2_done, layer + 1)
                for j in range(RT):
                    name = ("gates", layer, j)
                    claim(name)
                    mine = [(n, i) for n, (jj, i) in enumerate(BLOCK_PAIRS) if jj == j]
                    for g, wg_ in enumerate((wr, wi)):
                        for n, i in mine:
                            mm = pe.matmul(bank(name)[:, g * SEQ:(g + 1) * SEQ], wg_[:, n], xc[:, i],
                                           start=(n == mine[0][0]), stop=(n == mine[-1][0]))
                    done(mm, name)
                rnn_inputs("gr", PGR)

                def scores2(hh):
                    name = ("S2", layer, hh)
                    claim(name)
                    pe.matmul(bank(name)[:, 0:P], qT[:, hh, 0:P], kT[:, hh, 0:P], start=True, stop=True)
                    mm = pe.matmul(bank(name)[:, P:3 * P], qT[:, hh, P:], kT[:, hh], start=True, stop=True)
                    done(mm, name)

                for c in range(8):
                    emptied(pe, ("ropeT", layer, c))
                for j in range(4):
                    emptied(pe, ("v", layer, j))
                def gate(hh):
                    name = ("ga", layer, hh)
                    w_ = arrive2(PGA + hh // 4)
                    claim(name)
                    done(by_feature(bank(name)[:, 0:SEQ], w_, hh % 4), name)

                scores2(0)
                gate(0)
                for hh in range(HEADS):
                    if hh + 1 < HEADS:
                        scores2(hh + 1)
                    name = ("PT2", layer, hh)
                    claim(name)
                    pe.wait_ge(probs2, layer * HEADS + hh + 1)
                    b = hh % 2
                    pe.transpose(bank(name)[:, 0:P], s2[:, b, 0:P], ident[:])
                    pe.transpose(bank(name)[:, P:2 * P], s2[:, b, P:2 * P], ident[:])
                    done(pe.transpose(bank(name)[:, 2 * P:3 * P], s2[:, b, 2 * P:], ident[:]), name)
                    if hh + 1 < HEADS:
                        gate(hh + 1)
                    emptied(pe, name)
                    yn = ("Y2", layer, hh)
                    claim(yn)
                    hs = slice(hh * HD2, (hh + 1) * HD2)
                    pe.matmul(bank(yn)[:, 0:SEQ], vv[:, 0, hs], pT2[:, b, 0:SEQ], start=True, stop=False)
                    done(pe.matmul(bank(yn)[:, P:SEQ], vv[:, 1, hs], pT2[:, b, 2 * P:], start=False, stop=True), yn)
                for j in range(6):
                    emptied(pe, ("gr", layer, j))
                for pc in range(2):
                    wm = arrive2(PMB + 3 * pc)
                    for f in range(4):
                        if f % 2 == 0:
                            wb = arrive2(PMB + 3 * pc + 1 + f // 2)
                        name = ("mb", layer, 4 * pc + f)
                        claim(name)
                        by_feature(bank(name)[:, 0:SEQ], wm, f)
                        done(by_feature(bank(name)[:, SEQ:], wb, f % 2, ui, RT), name)
                pe.wait_ge(attn_gated, 2 * layer + 2)
                for pc in range(2):
                    wm, wa = arrive2(PMA + 2 * pc), arrive2(PMA + 2 * pc + 1)
                    for f in range(4):
                        name = ("ma", layer, 4 * pc + f)
                        claim(name)
                        by_feature(bank(name)[:, 0:SEQ], wm, f)
                        done(by_feature(bank(name)[:, SEQ:], wa, f, qT), name)
                pe.wait_ge(merged_ready, 8 * (layer + 1))
                for i in range(4):
                    name = ("out2", layer, i)
                    pc, t = i // 2, i % 2
                    if t == 0:
                        w = arrive2(PO + pc)
                    claim(name)
                    for k in range(KD):
                        mm = pe.matmul(bank(name)[:], merged[:, k, t * P:(t + 1) * P], w[:, k], start=(k == 0),
                                       stop=(k == KD - 1))
                    done(mm, name)


def _columns(v):
    return v.reshape(-1, P).T


def _block_diagonal(w):
    whole = np.zeros((RNN, RNN), w.dtype)
    for b in range(RB):
        whole[b * RBD:(b + 1) * RBD, b * RBD:(b + 1) * RBD] = w[b]
    return np.concatenate([whole[i * P:(i + 1) * P, j * P:(j + 1) * P] for j, i in BLOCK_PAIRS], axis=1)


def kernel(**inputs):
    import concourse.bacc as bacc
    from concourse.bass_utils import run_bass_kernel_spmd

    a = {k: np.asarray(v) for k, v in inputs.items()}
    f = np.float32
    cols = np.stack([np.concatenate(
        [_columns(a["norm_attn_out"][l]), _columns(a["norm_conv_out"][l]), _columns(a["conv_w"][l].reshape(-1)),
         _columns(a["conv_w_2"][l].reshape(-1)), _columns(a["conv_b_2"][l]), _columns(a["b_rg_2"][l]),
         _columns(a["b_ig_2"][l]), _columns(a["lru_lambda_2"][l])], axis=1) for l in range(DEPTH)], axis=1)

    def inverse_frequencies(theta, dim):
        return (f(theta) ** (-np.arange(0, dim, 2, dtype=f) / f(dim))).astype(f)

    inv2 = np.concatenate([inverse_frequencies(10000.0, HD2), inverse_frequencies(10000.0, ID)])
    rows = np.concatenate(
        [np.concatenate([a["b_router_group"][l], a["b_router_expert"][l]]) for l in range(DEPTH)]
        + [a["attn_sink"][l] for l in range(DEPTH)] + [inv2])
    rows = np.broadcast_to(rows, (P, rows.size))
    angle = np.arange(SEQ, dtype=f)[:, None] * inverse_frequencies(500000.0, 2 * ROT1)
    rope1 = np.stack([np.broadcast_to(g(angle).reshape(NT, P, 1, ROT1), (NT, P, HEADS + KVH, ROT1))
                      .transpose(1, 0, 2, 3).reshape(P, -1) for g in (np.cos, np.sin)], axis=1)
    gains = np.stack([a["norm_mix"][0], a["norm_ffn"][0], a["norm_mix"][1], a["norm_ffn"][1],
                      a["norm_final"], a["norm_g_2"][0], a["norm_g_2"][1], a["final_g_2"]])
    gains = np.broadcast_to(gains[:, None], (gains.shape[0], P, D))
    router = np.concatenate([a["w_router_group"], a["w_router_expert"]], axis=2)
    lru = np.stack([np.stack([_block_diagonal(a[n][l]) for n in ("w_rg_2", "w_ig_2")]) for l in range(DEPTH)])
    arrays = {
        "x_in": a["x"].reshape(SEQ, D), "cols_in": cols, "rows_in": rows, "rope1_in": rope1, "gains_in": gains,
        "router_in": router, "w_in": a["w_in"], "w_out": a["w_out"], "w_gate": a["w_expert_gate"],
        "w_up": a["w_expert_up"], "w_down": a["w_expert_down"], "positions": a["positions_2"].reshape(NT, P).T,
        "w_in2": a["w_in_2"], "w_lru": lru, "w_oa": a["w_out_attn_2"], "w_or": a["w_out_rnn_2"], "w_o": a["w_o_2"],
    }
    arrays = {k: np.ascontiguousarray(v) for k, v in arrays.items()}
    nc = bacc.Bacc("TRN2", target_bir_lowering=False, num_devices=1)
    args = {k: nc.dram_tensor(f"{k}_dram", v.shape, mybir.dt.from_np(v.dtype), kind="ExternalInput").ap()
            for k, v in arrays.items()}
    out = nc.dram_tensor("out_dram", (SEQ, D), F32, kind="ExternalOutput").ap()
    program(nc, *args.values(), out)
    r = run_bass_kernel_spmd(nc, [{f"{k}_dram": v for k, v in arrays.items()}], core_ids=[0])
    return r.results[0]["out_dram"].reshape(1, SEQ, D)
```

```python
from contextlib import ExitStack

import numpy as np

import concourse.bass as bass
from concourse import mybir

F32 = mybir.dt.float32
F32R = mybir.dt.float32r
I32 = mybir.dt.int32
ALU = mybir.AluOpType
ACT = mybir.ActivationFunctionType
AX = mybir.AxisListType

P = 128
SEQ = 256
NT = SEQ // P
D = 1024
KD = D // P
DEPTH = 2
EPS = 1e-6
NEG = -1e30
TAKEN = -3e38

HEADS = 8
HD1 = 64
KVH = 2
QW = HEADS * HD1
KVW = KVH * HD1
CW = D - QW
ROT1 = 8
GROUPS = 4
PER_GROUP = 8
NE = GROUPS * PER_GROUP
DE = 512
FE = DE // P
SLOTS = 64
ROUNDS = SEQ // SLOTS
ROUTER_W = GROUPS + NE

HD2 = 128
IH = 16
ID = 64
TOPK = min(256, SEQ // 4)
RNN = 1408
RT = RNN // P
RB = 16
RBD = RNN // RB
LRU_C = 8.0
TAPS2 = 4
Q2, K2, V2, GA2, IQ2 = 0, 1024, 2048, 3072, 4096
IK2 = IQ2 + IH * ID
XR2 = IK2 + ID + IH
GR2 = XR2 + RNN
MA2 = GR2 + RNN
MB2 = MA2 + D

BETWEEN = 2 * DEPTH
SECOND = BETWEEN + 1
FINAL = SECOND + DEPTH

RING = 6
RING2 = 4
CHUNKS = 4
EXTRA = 2
SLOT_F = 4096
BANKS = 8
IDLE_START, IDLE_EXPERTS, IDLE_MIXER, IDLE_BETWEEN, IDLE_ROUTER, IDLE_PICKS = 16, 16, 6, 36, 22, 9
MOE_BANKS = 4

BLOCK_PAIRS = [(j, i) for j in range(RT) for i in range(RT)
               if i * P < -(-(j + 1) * P // RBD) * RBD and (i + 1) * P > (j * P // RBD) * RBD]
NBP = len(BLOCK_PAIRS)

COLS = {}
_at = 0
for _name, _n in [("g_attn", 4), ("g_conv", 4), ("conv1", 12), ("conv2", TAPS2 * RT), ("conv2_b", RT),
                  ("b_rg", RT), ("b_ig", RT), ("lam", RT)]:
    COLS[_name] = (_at, _n)
    _at += _n
NCOLS = _at

NROPE1 = NT * (HEADS + KVH) * ROT1
INV2 = HD2 // 2 + ID // 2
TWO_PI_PARTS = (6.28125, 0.0019340515136718750, 1.2556659146999e-6)
ROUNDER = 12582912.0


BESIDE_HEAD = [[("u", 1), ("gc", 2)], [("u", 2)], [("gc", 3)], [("u", 3), ("gb", 0)], [("gb", 1), ("gb", 2)], [("gb", 3)],
               [("out1", 0)], [("out1", 1)]]
OUT1 = [(0, 0, 1), (0, 1, 1), (0, 0, 0), (0, 1, 0), (1, 0, 1), (1, 0, 0), (1, 1, 1), (1, 1, 0)]


def psum_tiles():
    names = []
    for layer in range(DEPTH):
        for t in range(NT):
            names += [("hT", 2 * layer, 2 * t), ("hT", 2 * layer, 2 * t + 1), ("q", layer, t)]
        names += [("kv", layer, t) for t in range(NT)]
        names += [("gc", layer, j) for j in range(2)]
        names += [("qkT", layer, j) for j in range(3)]
        names += [("S1", layer, 0), ("u", layer, 0)]
        for h in range(HEADS):
            names += [("S1", layer, h + 1)] if h + 1 < HEADS else []
            names += [("PT1", layer, h)]
            names += [(g, layer, j) for g, j in BESIDE_HEAD[h]]
            names += [("Y1", layer, h // 2)] if h % 2 == 0 else []
        names += [("ss", layer, 0)]
        names += [("out1", layer, i) for i in range(2, 8)]
        names += [("hT", 2 * layer + 1, 0), ("hT", 2 * layer + 1, 1), ("logits", layer, 0)]
        names += [("hT", 2 * layer + 1, 2), ("hT", 2 * layer + 1, 3), ("rank", layer, 0), ("gather", layer, 0), ("gather", layer, 1)]
    for layer in range(DEPTH):
        names += [("hT", SECOND + layer, 0), ("hT", SECOND + layer, 1)]
        names += [("rope", layer, 0), ("hT", SECOND + layer, 2), ("hT", SECOND + layer, 3), ("rope", layer, 1)]
        for c in range(2, 14, 2):
            names += [("rope", layer, c), ("rope", layer, c + 1), ("ropeT", layer, c - 2), ("ropeT", layer, c - 1)]
        names += [("ropeT", layer, 12), ("ropeT", layer, 13)]
        names += [("xr", layer, j) for j in range(RT)]
        names += [("v", layer, j) for j in range(4)]
        names += [("dots", layer, j) for j in range(12)]
        names += [("gates", layer, j) for j in range(RT)]
        names += [("gr", layer, j) for j in range(6)]
        names += [("S2", layer, 0), ("ga", layer, 0)]
        for h in range(HEADS):
            names += [("S2", layer, h + 1)] if h + 1 < HEADS else []
            names += [("PT2", layer, h)]
            names += [("ga", layer, h + 1)] if h + 1 < HEADS else []
            names += [("Y2", layer, h)]
        names += [("mb", layer, j) for j in range(8)]
        names += [("ma", layer, j) for j in range(8)]
        names += [("out2", layer, j) for j in range(4)]
    return {name: n for n, name in enumerate(names)}


TILE = psum_tiles()
assert len(TILE) == max(TILE.values()) + 1


class Steps:

    def __init__(self, eng, own, base=None):
        self.eng, self.own, self.base, self.n, self.last = eng, own, base or {}, {}, None

    def value(self, sem):
        n = self.n.get(sem.name, 0)
        return self.base[sem.name] + n if sem.name in self.base else n

    def __call__(self, ins, sem=None):
        sem = sem or self.own
        ins.then_inc(sem, 1)
        self.n[sem.name] = self.n.get(sem.name, 0) + 1
        self.last = (sem, self.value(sem))

    def marks(self, ins, sem, value):
        ins.then_inc(sem, 1)
        self.last = (sem, value)

    def settle(self):
        if self.last is not None:
            self.eng.wait_ge(*self.last)


def program(nc, x_in, cols_in, rows_in, rope1_in, gains_in, router_in, w_in, w_out, w_gate, w_up, w_down,
            positions, w_in2, w_lru, w_oa, w_or, w_o, out):
    with ExitStack() as ctx:
        def sem(name):
            return ctx.enter_context(nc.semaphore(name))

        ring = ctx.enter_context(nc.sbuf_tensor("ring", [P, RING2, SLOT_F], F32))
        x = ctx.enter_context(nc.sbuf_tensor("x", [P, NT, D], F32))
        h = ctx.enter_context(nc.sbuf_tensor("h", [P, NT, D], F32))
        hT = ctx.enter_context(nc.sbuf_tensor("hT", [P, KD, SEQ], F32))

        ident = ctx.enter_context(nc.sbuf_tensor("ident", [P, P], F32))
        ones = ctx.enter_context(nc.sbuf_tensor("ones", [P, P], F32))
        zeros = ctx.enter_context(nc.sbuf_tensor("zeros", [P, P], F32))
        before = ctx.enter_context(nc.sbuf_tensor("before", [P, P], F32))
        iota_i = ctx.enter_context(nc.sbuf_tensor("iota_i", [P, SLOTS], I32))
        iota_f = ctx.enter_context(nc.sbuf_tensor("iota_f", [P, SLOTS], F32))
        cols = ctx.enter_context(nc.sbuf_tensor("cols", [P, DEPTH, NCOLS], F32))
        rows = ctx.enter_context(nc.sbuf_tensor("rows", [P, DEPTH * (ROUTER_W + HEADS) + INV2], F32))
        gain = ctx.enter_context(nc.sbuf_tensor("gain", [P, D], F32))
        ang = ctx.enter_context(nc.sbuf_tensor("ang", [P, NT, INV2], F32))
        cos2 = ctx.enter_context(nc.sbuf_tensor("cos2", [P, NT, INV2], F32))
        sin2 = ctx.enter_context(nc.sbuf_tensor("sin2", [P, NT, INV2], F32))
        pos_i = ctx.enter_context(nc.sbuf_tensor("pos_i", [P, NT], I32))
        pos_f = ctx.enter_context(nc.sbuf_tensor("pos_f", [P, NT], F32))
        decay = ctx.enter_context(nc.sbuf_tensor("decay", [P, DEPTH, RT], F32))
        lam_t = ctx.enter_context(nc.sbuf_tensor("lam_t", [P, 4, DEPTH, RT], F32))
        power = ctx.enter_context(nc.sbuf_tensor("power", [P, 4], F32))
        stat = ctx.enter_context(nc.sbuf_tensor("stat", [P, 64], F32))
        small = ctx.enter_context(nc.sbuf_tensor("small", [P, 15, NT, NE], F32))
        causal = ctx.enter_context(nc.sbuf_tensor("causal", [P, 3 * P], F32))
        top8 = ctx.enter_context(nc.sbuf_tensor("top8", [P, 16], F32))
        trips_i = ctx.enter_context(nc.sbuf_tensor("trips_i", [P, 2], I32))

        WORK = 18240
        work = ctx.enter_context(nc.sbuf_tensor("work", [P, WORK], F32))
        top = {}

        def carve(phase, *shape):
            n = int(np.prod(shape))
            at = top.get(phase, 0)
            top[phase] = at + n
            assert top[phase] <= WORK, (phase, top[phase])
            v = work[:, at:at + n]
            if len(shape) == 2:
                v = v.rearrange("p (a b) -> p a b", a=shape[0])
            if len(shape) == 3:
                v = v.rearrange("p (a b c) -> p a b c", a=shape[0], b=shape[1])
            return v

        window = carve("keep1", NT, SEQ)
        cos1 = carve("keep1", NROPE1)
        sin1 = carve("keep1", NROPE1)
        w_router = carve("keep1", KD, P)
        top["mix1"] = top["moe"] = top["keep1"]
        qkv = carve("mix1", NT, QW + 2 * KVW)
        kswap = carve("mix1", NT, KVW)
        rt1 = carve("mix1", 4, NROPE1)
        qT1 = carve("mix1", HEADS // 2, SEQ)
        kT1 = carve("mix1", 2, SEQ)
        gb = carve("mix1", 4, SEQ)
        gc = carve("mix1", 4, SEQ)
        cu = carve("mix1", 4, SEQ + 2)
        yc = carve("mix1", 4, SEQ)
        yc_t = carve("mix1", SEQ)
        yT = carve("mix1", KD, SEQ)
        sq = carve("mix1", KD, SEQ)
        s1 = carve("mix1", 2, NT, SEQ)
        pT1 = carve("mix1", 2, NT, SEQ)
        xg = carve("moe", 2 * KD, 2 * SLOTS)
        pick = carve("moe", NT, PER_GROUP, SLOTS)
        wpick = carve("moe", NT, PER_GROUP, SLOTS)
        comb = carve("moe", 2, SEQ)
        silu_g = carve("moe", 2, DE)
        hid = carve("moe", 2, DE)
        hidT = carve("moe", 2, FE * P)
        ysb = hT[:].rearrange("p a b -> p (a b)").rearrange("p (a b) -> p a b", a=2)
        extra = work[:, WORK - EXTRA * SLOT_F:].rearrange("p (a b) -> p a b", a=EXTRA)

        assert top["moe"] <= WORK - EXTRA * SLOT_F
        gain_second = w_router.rearrange("p a b -> p (a b)")

        def gathered(b, half):
            return xg[:, b * KD + half * KD // 2:b * KD + (half + 1) * KD // 2].rearrange("p a b -> p (a b)")

        xr = carve("b2", RT, SEQ + TAPS2 - 1)
        xc = carve("b2", RT, SEQ)
        ra = carve("b2", RT, SEQ)
        ui = carve("b2", RT, SEQ)
        qT = carve("b2", HEADS, SEQ)
        kT = carve("b2", HEADS, SEQ)
        roped_at = top["b2"]
        roped = carve("b2", 4, 512)
        bias2 = carve("b2", 3 * P)
        iw = carve("b2", NT, IH)
        top["idx"] = roped_at
        relu = carve("idx", 2, 512)
        wk = carve("idx", 2, 3 * P)
        top["att"] = 0
        s2 = carve("att", 2, 3 * P)
        pT2 = carve("att", 2, 3 * P)
        assert top["att"] <= RT * (SEQ + 3)
        tanh_a = xr.rearrange("p a b -> p (a b)")[:, 0:RT * SEQ].rearrange("p (a b) -> p a b", a=RT)
        merged = xc.rearrange("p a b -> p (a b)")[:, 0:KD * SEQ].rearrange("p (a b) -> p a b", a=KD)
        ra_words, ui_words = (z.rearrange("p a b -> p (a b)") for z in (ra, ui))
        iqT = ra_words[:, 0:IH // 2 * SEQ].rearrange("p (a b) -> p a b", a=IH // 2)
        ga_all = iqT
        ikT = ra_words[:, IH // 2 * SEQ:(IH // 2 + 1) * SEQ]
        ropetmp = ui_words[:, 0:1024].rearrange("p (a b) -> p a b", a=2)
        vv = h

        with nc.sbuf_tensor("ring_tail", [P, RING - RING2, SLOT_F], F32) as ring_tail:
            pass
        stream = ctx.enter_context(nc.sbuf_tensor("stream", [P, KD, 2, SEQ], F32R))
        hT_hi, hT_lo = stream[:, :, 0], stream[:, :, 1]
        w_hi = ctx.enter_context(nc.sbuf_tensor("w_hi", [P, CHUNKS, 512], F32R))
        w_lo = ctx.enter_context(nc.sbuf_tensor("w_lo", [P, CHUNKS, 512], F32R))

        banks = [ctx.enter_context(nc.psum_tensor(f"bank{b}", [P, 512], F32)) for b in range(BANKS)]
        psum_full = [sem(f"psum_full_{b}") for b in range(BANKS)]
        psum_read = [sem(f"psum_read_{b}") for b in range(BANKS)]

        x_loaded = [sem(f"x_loaded_{t}") for t in range(NT)]
        rope1_loaded = sem("rope1_loaded")
        consts_loaded = sem("consts_loaded")
        gain_loaded = sem("gain_loaded")
        gain_second_loaded = sem("gain_second_loaded")
        router_loaded = sem("router_loaded")
        masks_ready = sem("masks_ready")
        own_dve = sem("dve_steps")
        own_act = sem("act_steps")
        own_pool = sem("pool_steps")
        sumsq_ready = sem("sumsq_ready")
        mean_ready = sem("mean_ready")
        rstd_ready = sem("rstd_ready")
        h_ready = sem("h_ready")
        roped1 = sem("roped1")
        conv_out = sem("conv_out")
        conv_sq = sem("conv_sq")
        negmax = sem("negmax")
        exps = sem("exps")
        probs = sem("probs")
        route_exp_in = sem("route_exp_in")
        route_exp_out = sem("route_exp_out")
        assign_ready = sem("assign_ready")
        trips_ready = sem("trips_ready")
        angles_ready = sem("angles_ready")
        tables2_ready = sem("tables2_ready")
        lam_in = sem("lam_in")
        lam_exp = sem("lam_exp")
        decay_ready = sem("decay_ready")
        out_stored = sem("out_stored")
        SEGS = ["mix0", "moe0", "mix1", "moe1", "b2"]
        w_loaded = {s: [sem(f"w_loaded_{s}_{k}") for k in range(RING + EXTRA)] for s in SEGS}
        moe = [{n: sem(f"moe{l}_{n}") for n in ["picked", "wpicked", "full4", "full5", "full6", "full7", "read4", "read5",
                                                "read6", "read7", "silu", "scattered", "dve", "act", "x_ready"]}
               for l in range(DEPTH)]
        roped2 = sem("roped2")
        hT_hi_ready = sem("hT_hi_ready")
        hT_lo_ready = sem("hT_lo_ready")
        chunk_hi = sem("chunk_hi")
        chunk_lo = sem("chunk_lo")
        chunk_used = sem("chunk_used")
        conv2_done = sem("conv2_done")
        tanh_ready = sem("tanh_ready")
        tanh_used = sem("tanh_used")
        root_ready = sem("root_ready")
        hidden_ready = sem("hidden_ready")
        relu_done = sem("relu_done")
        negmax2 = sem("negmax2")
        exps2 = sem("exps2")
        probs2 = sem("probs2")
        silu_gr = sem("silu_gr")
        silu_ga = sem("silu_ga")
        attn_gated = sem("attn_gated")
        sig_ready = sem("sig_ready")
        merged_ready = sem("merged_ready")
        xr_half = sem("xr_half")
        merged_hi = sem("merged_hi")
        merged_lo = sem("merged_lo")

        def bank(name):
            return banks[TILE[name] % BANKS]

        def hT_part(j):
            return hT[:, 4 * (j % 2):4 * (j % 2) + 4, j // 2 * P:(j // 2 + 1) * P]

        def uses(name):
            return TILE[name] // BANKS + 1

        def full(eng, name):
            eng.wait_ge(psum_full[TILE[name] % BANKS], uses(name))

        def emptied(eng, name):
            eng.wait_ge(psum_read[TILE[name] % BANKS], uses(name))

        def col(layer, name, k, rows_=slice(0, P)):
            a, n = COLS[name]
            return cols[rows_, layer, a + k:a + k + 1]

        SINK0 = DEPTH * ROUTER_W
        INV0 = SINK0 + DEPTH * HEADS

        def mixer_piece(j):
            return (j + RING - 1) % RING

        def mixer_count(j):
            return 32 if j == RING else 16

        MIX_PIECES = [("in", 0, QW), ("in", QW, 2 * KVW), ("in", QW + 2 * KVW + CW, CW),
                      ("in", QW + 2 * KVW + 2 * CW, CW), ("in", QW + 2 * KVW, CW), ("out", 0, 512), ("out", 512, 512)]
        MIX_LAST = [("q", 1), ("kv", 1), ("gc", 3), ("u", 3), ("gb", 3), ("out1", 3), ("out1", 7)]
        B2_PIECES = ([("in", Q2, 512), ("in", Q2 + 512, 512), ("in", K2, 512), ("in", K2 + 512, 512)]
                     + [("in", IQ2, 512), ("in", IQ2 + 512, 512), ("in", IK2, 128)]
                     + [("in", XR2, 512), ("in", XR2 + 512, 512), ("in", XR2 + 1024, 384)]
                     + [("in", V2, 512), ("in", V2 + 512, 512)]
                     + [("lru", 0, NBP * P), ("lru", 1, NBP * P)]
                     + [("in", GR2, 512), ("in", GR2 + 512, 512), ("in", GR2 + 1024, 384)]
                     + [("in", GA2, 512), ("in", GA2 + 512, 512)]
                     + [(kind, c0 + c, 256) for c in range(0, D, 256) for kind, c0 in (("in", MB2), ("or", 0))]
                     + [("in", MA2, 512), ("oa", 0, 512), ("in", MA2 + 512, 512), ("oa", 512, 512)]
                     + [("o", 0, 512), ("o", 512, 512)])
        NB2 = len(B2_PIECES)
        B2_LAST = ([("rope", c) for c in (1, 3, 5, 7, 9, 11, 13)] + [("xr", 3), ("xr", 7), ("xr", 10)]
                   + [("v", 1), ("v", 3)] + [("gates", RT - 1)] * 2 + [("gr", 1), ("gr", 3), ("gr", 5), ("ga", 3), ("ga", 7)]
                   + [("mb", 2 * (j // 2) + 1) for j in range(8)]
                   + [("ma", 3), ("ma", 3), ("ma", 7), ("ma", 7), ("out2", 1), ("out2", 3)])
        PROPE, PXR, PV, PLRU, PGR, PGA, PMB, PMA, PO = 0, 7, 10, 12, 14, 17, 19, 27, 31

        def piece(slot, k, n):
            if slot < RING2:
                words = ring[:, slot, 0:k * n]
            elif slot < RING:
                words = ring_tail[:, slot - RING2, 0:k * n]
            else:
                words = extra[:, slot - RING, 0:k * n]
            return words.rearrange("p (k n) -> p k n", k=k)

        def arrive2(eng, layer, j):
            at = layer * NB2 + j
            kind, _, n = B2_PIECES[j]
            eng.wait_ge(w_loaded["b2"][at % RING2], 16 * (at // RING2 + 1))
            if kind == "lru":
                return ring[:, at % RING2, 0:n].rearrange("p (b n) -> p b n", n=P)
            return piece(at % RING2, RT if kind == "or" else KD, n)

        SPLIT = ([(PROPE + c // 2, ("rope", c + 1)) for c in range(2, 12, 2)]
                 + [(PXR, ("xr", 3)), (PXR + 1, ("xr", 7)), (PXR + 2, ("xr", 10))]
                 + [(PV, ("v", 1)), (PV + 1, ("v", 3)), (PO, ("out2", 1))])
        QXR, QV, QO = 5, 8, 10

        def chunk(layer, q, k):
            return (layer * len(SPLIT) + q) * KD + k

        def chunk_left(eng, g):
            if g % KD == KD - 1:
                layer, q = divmod(g // KD, len(SPLIT))
                nm, j = SPLIT[q][1]
                full(eng, (nm, layer, j))
            else:
                eng.wait_ge(chunk_used, g // KD * (KD - 1) + g % KD + 1)

        T_COMB, T_GU, T_NEXT, T_HID, T_OUT, PAIR_TILES = 0, 1, 3, 5, 6, 8
        MOE_TILES = 4 * PAIR_TILES
        PER_BANK = MOE_TILES // MOE_BANKS

        PER_PAIR = 6
        TURN = 4 * PER_PAIR
        MOE_RING = RING + EXTRA
        ROUND_TRIPS = TURN // MOE_RING
        assert TURN % MOE_RING == 0

        def piece_last(n):
            pair, idx = n // PER_PAIR, n % PER_PAIR
            return PAIR_TILES * pair + (T_GU, T_GU, T_GU + 1, T_GU + 1, T_OUT + 1, T_OUT + 1)[idx]

        block = ctx.enter_context(nc.Block())

        @block.sync
        def _(sp):
            for t in range(NT):
                sp.dma_start(x[:, t], x_in[t * P:(t + 1) * P]).then_inc(x_loaded[t], 16)
            for dst, src in ((rows[:], rows_in), (cols[:], cols_in), (pos_i[:], positions)):
                sp.dma_start(dst, src).then_inc(consts_loaded, 16)

            def left_by_experts(layer, slot):
                m = piece_last(TURN - MOE_RING + slot)
                sp.wait_ge(moe[layer][f"full{4 + m % 4}"], last_turn * PER_BANK + (m // 4 + 1))

            def mixer(layer):
                for j, (kind, c0, n) in enumerate(MIX_PIECES):
                    slot = mixer_piece(j)
                    if j == RING:
                        full(sp, ("q", layer, 1))
                    elif layer > 0:
                        left_by_experts(layer - 1, slot)
                    src = (w_in if kind == "in" else w_out)[layer].rearrange("(k p) n -> p k n", p=P)
                    sp.dma_start(piece(slot, KD, n), src[:, :, c0:c0 + n]).then_inc(w_loaded[f"mix{layer}"][slot], 16)

            def expert_piece(layer, e0, n):
                p, idx, slot = n // PER_PAIR, n % PER_PAIR, n % MOE_RING
                e = e0 + (2 * p + (idx % 2 if idx >= 4 else idx // 2))
                if idx >= 4:
                    src = w_down[layer].rearrange("e (k p) n -> e p k n", p=P)
                    dst = piece(slot, FE, D)
                else:
                    src = (w_gate if idx % 2 == 0 else w_up)[layer].rearrange("e (k p) n -> e p k n", p=P)
                    dst = piece(slot, KD, DE)
                sp.dma_start(dst, src[e]).then_inc(w_loaded[f"moe{layer}"][slot], 16)

            def experts(layer):
                for n in range(TURN):
                    if n < RING:
                        nm, last_tile = MIX_LAST[n + 1]
                        full(sp, (nm, layer, last_tile))
                    elif n < MOE_RING:
                        emptied(sp, ("out1", layer, 7))
                    else:
                        m = piece_last(n - MOE_RING)
                        sp.wait_ge(moe[layer][f"full{4 + m % 4}"], m // 4 + 1)
                    expert_piece(layer, 0, n)
                sp.wait_ge(trips_ready, layer + 1)
                last = sp.value_load(trips_i[0:1, 1:2], min_val=GROUPS - 1, max_val=GROUPS * ROUNDS - 1)
                with sp.Fori(0, last) as i:
                    g = ((i + 1) % GROUPS) * PER_GROUP
                    for n in range(TURN):
                        m = piece_last((n - MOE_RING) % TURN)
                        sp.wait_ge(moe[layer][f"full{4 + m % 4}"],
                                   i * PER_BANK + (m // 4 + 1 + (PER_BANK if n >= MOE_RING else 0)))
                        expert_piece(layer, g, n)
                return last

            last_turn = None
            for layer in range(DEPTH):
                mixer(layer)
                last_turn = experts(layer)
            for layer in range(DEPTH):
                for j, (kind, c0, n) in enumerate(B2_PIECES):
                    at = layer * NB2 + j
                    slot = at % RING2
                    if at < RING2:
                        left_by_experts(DEPTH - 1, slot)
                    else:
                        nm, last = B2_LAST[(at - RING2) % NB2]
                        full(sp, (nm, (at - RING2) // NB2, last))
                    if kind == "lru":
                        dst, src = ring[:, slot, 0:n], w_lru[layer, c0]
                    elif kind == "or":
                        dst = piece(slot, RT, n)
                        src = w_or[layer].rearrange("(k p) n -> p k n", p=P)[:, :, c0:c0 + n]
                    else:
                        w = {"in": w_in2, "oa": w_oa, "o": w_o}[kind]
                        dst = piece(slot, KD, n)
                        src = w[layer].rearrange("(k p) n -> p k n", p=P)[:, :, c0:c0 + n]
                    sp.dma_start(dst, src).then_inc(w_loaded["b2"][slot], 16)
            for t in range(NT):
                sp.wait_ge(h_ready, NT * FINAL + t + 1)
                sp.dma_start(out[t * P:(t + 1) * P], h[:, t]).then_inc(out_stored, 16)
            sp.wait_ge(out_stored, 16 * NT)

        @block.gpsimd
        def _(pool):
            S = Steps(pool, own_pool)
            S(pool.memset(ident[:], 0.0))
            S(pool.memset(ones[:], 1.0))
            S(pool.memset(zeros[:], 0.0))
            S(pool.memset(power[:], -0.5))
            S(pool.memset(window, 0.0))
            S(pool.memset(w_router, 0.0))
            S.settle()
            S(pool.affine_select(out=ident[:], in_=ident[:], compare_op=ALU.not_equal, fill=1.0, base=0,
                                 pattern=[[-1, P]], channel_multiplier=1))
            S(pool.affine_select(out=before[:], in_=ones[:], compare_op=ALU.is_gt, fill=0.0, base=0,
                                 pattern=[[1, P]], channel_multiplier=-1))
            S(pool.affine_select(out=window, in_=window, compare_op=ALU.is_ge, fill=NEG, base=P,
                                 pattern=[[P, NT], [-1, SEQ]], channel_multiplier=1))
            S.settle()
            S(pool.affine_select(out=window, in_=window, compare_op=ALU.is_ge, fill=NEG, base=P,
                                 pattern=[[-P, NT], [1, SEQ]], channel_multiplier=-1))
            S(pool.iota(iota_i[:], [[1, SLOTS]], base=0, channel_multiplier=0))
            S.settle()
            pool.tensor_copy(iota_f[:], iota_i[:]).then_inc(masks_ready, 1)
            pool.dma_start(w_router[:, :, 0:ROUTER_W],
                           router_in[0].rearrange("(k p) n -> p k n", p=P)).then_inc(router_loaded, 16)

            def inverse_root(src, dst, n):
                pool.tensor_tensor(dst, src, power[:, 0:n], ALU.pow).then_inc(rstd_ready, 1)

            def inverse_rms(stage):
                for t in range(NT):
                    pool.wait_ge(mean_ready, NT * stage + t + 1)
                    inverse_root(stat[:, 2 + t:3 + t], stat[:, 4 + t:5 + t], 1)

            for layer in range(DEPTH):
                inverse_rms(2 * layer)
                pool.wait_ge(consts_loaded, 48)
                for f in range(4):
                    emptied(pool, ("u", layer, f))
                    S.settle()
                    S(pool.tensor_scalar(yc[:, f], cu[:, f, 0:SEQ], col(layer, "conv1", f), None, ALU.mult))
                    for tap in (1, 2):
                        S.settle()
                        S(pool.tensor_scalar(yc_t, cu[:, f, tap:tap + SEQ], col(layer, "conv1", 4 * tap + f), None,
                                             ALU.mult))
                        S.settle()
                        S(pool.tensor_tensor(yc[:, f], yc[:, f], yc_t, ALU.add))
                S.settle()
                for f in range(4):
                    emptied(pool, ("gb", layer, f))
                    S(pool.tensor_tensor(yc[:, f], yc[:, f], gb[:, f], ALU.mult), conv_out)
                emptied(pool, ("ss", layer, 0))
                inverse_root(stat[:, 8:12], stat[:, 12:16], 4)
                inverse_rms(2 * layer + 1)
                if layer + 1 < DEPTH:
                    full(pool, ("rank", layer, 0))
                    pool.dma_start(w_router[:, :, 0:ROUTER_W],
                                   router_in[layer + 1].rearrange("(k p) n -> p k n", p=P)).then_inc(router_loaded, 16)
            inverse_rms(BETWEEN)
            for layer in range(DEPTH):
                inverse_rms(SECOND + layer)
                for q in range(len(SPLIT)):
                    w = arrive2(pool, layer, SPLIT[q][0])
                    for k in range(KD):
                        g = chunk(layer, q, k)
                        pool.wait_ge(chunk_hi, g + 1)
                        n = w.shape[2]
                        pool.tensor_tensor(w_lo[:, g % CHUNKS, 0:n], w[:, k], w_hi[:, g % CHUNKS, 0:n], ALU.subtract
                                           ).then_inc(chunk_lo, 1)
            inverse_rms(FINAL)

        @block.scalar
        def _(act):
            S = Steps(act, own_act)

            def load_gain(stage):
                if stage > 0:
                    act.wait_ge(h_ready, 2 * stage)
                act.dma_start(gain[:], gains_in[stage]).then_inc(gain_loaded, 16)

            def square(stage, t):
                S(act.activation(h[:, t], x[:, t], ACT.Square, accum_out=stat[:, t:t + 1]), sumsq_ready)

            def copy_hT(stage, *tiles):
                for j in tiles:
                    full(act, ("hT", stage, j))
                    act.copy(hT_part(j), bank(("hT", stage, j))[:].rearrange("p (a b) -> p a b", b=P)
                             ).then_inc(psum_read[TILE[("hT", stage, j)] % BANKS], 1)

            def empty(name, dst, src, func=ACT.Copy, **kw):
                full(act, name)
                act.activation(dst, src, func, **kw).then_inc(psum_read[TILE[name] % BANKS], 1)

            load_gain(0)
            act.dma_start(cos1, rope1_in[:, 0]).then_inc(rope1_loaded, 16)
            act.dma_start(sin1, rope1_in[:, 1]).then_inc(rope1_loaded, 16)

            def second_block_tables():
                act.wait_ge(consts_loaded, 48)
                act.wait_ge(lam_in, 1)
                act.activation(lam_t[:, 1], lam_t[:, 0], ACT.Exp, scale=-1.0).then_inc(lam_exp, 1)
                act.wait_ge(angles_ready, 1)
                S(act.activation(sin2[:], sin2[:], ACT.Sin))
                S(act.activation(cos2[:], cos2[:], ACT.Sin), tables2_ready)

            for layer in range(DEPTH):
                for t in range(NT):
                    if layer > 0:
                        act.wait_ge(moe[layer - 1]["x_ready"], t + 1)
                    else:
                        act.wait_ge(x_loaded[t], 16)
                    square(2 * layer, t)
                    copy_hT(2 * layer, *((0, 1) if t == 0 else (2,)))
                load_gain(2 * layer + 1)
                if layer == 0:
                    second_block_tables()
                for t in range(NT):
                    empty(("q", layer, t), qkv[:, t, 0:QW], bank(("q", layer, t))[:])
                for t in range(NT):
                    empty(("kv", layer, t), qkv[:, t, QW:], bank(("kv", layer, t))[:, 0:2 * KVW])

                def gate_tile(nm, j):
                    if nm in ("gc", "gb"):
                        empty((nm, layer, j), (gc if nm == "gc" else gb)[:, j], bank((nm, layer, j))[:, 0:SEQ])

                gate_tile("gc", 0)
                gate_tile("gc", 1)
                for j in range(2):
                    empty(("qkT", layer, j), qT1[:, 2 * j:2 * j + 2].rearrange("p a b -> p (a b)"),
                          bank(("qkT", layer, j))[:])
                empty(("qkT", layer, 2), kT1.rearrange("p a b -> p (a b)"), bank(("qkT", layer, 2))[:])

                def exponentials(hh):
                    act.wait_ge(negmax, layer * HEADS + hh + 1)
                    st = stat[:, 16 + 8 * (hh % 2):24 + 8 * (hh % 2)]
                    for qb in range(NT):
                        S(act.activation(s1[:, hh % 2, qb], s1[:, hh % 2, qb], ACT.Exp, bias=st[:, 2 + qb:3 + qb],
                                         accum_out=st[:, 4 + qb:5 + qb]))
                    S(act.activation(st[:, 6:8], st[:, 2:4], ACT.Exp,
                                     bias=rows[:, SINK0 + layer * HEADS + hh:SINK0 + layer * HEADS + hh + 1]), exps)

                def convolved(f):
                    act.wait_ge(conv_out, 4 * layer + f + 1)
                    S(act.activation(sq[:, 4 + f], yc[:, f], ACT.Square))
                    S(act.activation(yT[:, 4 + f], yc[:, f], ACT.Copy, scale=col(layer, "g_conv", f)), conv_sq)

                exponentials(0)
                for hh in range(HEADS):
                    if hh == 6:
                        convolved(3)
                    empty(("PT1", layer, hh), pT1[:, hh % 2].rearrange("p a b -> p (a b)"),
                          bank(("PT1", layer, hh))[:])
                    if hh + 1 < HEADS:
                        exponentials(hh + 1)
                    for nm, j in BESIDE_HEAD[hh]:
                        gate_tile(nm, j)
                    if hh == 5:
                        for f in range(3):
                            convolved(f)
                    if hh % 2 == 1:
                        j = hh // 2
                        full(act, ("Y1", layer, j))
                        S(act.activation(sq[:, j], bank(("Y1", layer, j))[:, 0:SEQ], ACT.Square))
                        empty(("Y1", layer, j), yT[:, j], bank(("Y1", layer, j))[:, 0:SEQ], ACT.Copy,
                              scale=col(layer, "g_attn", j))

                for t in range(NT):
                    emptied(act, ("out1", layer, 5 + 2 * t))
                    square(2 * layer + 1, t)
                copy_hT(2 * layer + 1, 0, 1, 2)
                load_gain(2 * layer + 2)
                act.wait_ge(route_exp_in, 2 * layer + 1)
                act.activation(small[:, 3, :, 0:GROUPS], small[:, 2, :, 0:GROUPS], ACT.Exp).then_inc(route_exp_out, 1)
                act.wait_ge(route_exp_in, 2 * layer + 2)
                act.activation(stat[:, 40:42], stat[:, 38:40], ACT.Exp).then_inc(route_exp_out, 1)
                if layer == DEPTH - 1:
                    full(act, ("rank", layer, 0))
                    act.dma_start(gain_second, gains_in[SECOND]).then_inc(gain_second_loaded, 16)
                empty(("gather", layer, 0), gathered(0, 0), bank(("gather", layer, 0))[:])
                act.wait_ge(trips_ready, layer + 1)
                n = act.value_load(trips_i[0:1, 0:1], min_val=GROUPS, max_val=GROUPS * ROUNDS)
                M = moe[layer]
                with act.Fori(0, n) as i:
                    def m_full(m):
                        act.wait_ge(M[f"full{4 + m % 4}"], i * PER_BANK + (m // 4 + 1))

                    def m_bank(m):
                        return banks[4 + m % 4]

                    for p in range(4):
                        b = p % 2
                        m0 = PAIR_TILES * p
                        for side in range(2):
                            m = m0 + T_GU + side
                            up, gate = (slice(0, 64), slice(64, P)) if side == 0 else (slice(64, P), slice(0, 64))
                            m_full(m)
                            act.activation(silu_g[up, b], m_bank(m)[gate, :], ACT.Silu).then_inc(M["silu"], 1)
                        m = m0 + T_NEXT
                        m_full(m)
                        act.copy(gathered(1 - b, 0), m_bank(m)[:]).then_inc(M[f"read{4 + m % 4}"], 1)
                        m = m0 + T_HID
                        m_full(m)
                        act.copy(hidT[:, b], m_bank(m)[:]).then_inc(M[f"read{4 + m % 4}"], 1)
                        m = m0 + T_OUT
                        m_full(m)
                        act.copy(ysb[:, b, 0:512], m_bank(m)[:]).then_inc(M[f"read{4 + m % 4}"], 1)

            for t in range(NT):
                act.wait_ge(moe[DEPTH - 1]["x_ready"], t + 1)
                square(BETWEEN, t)
            for layer in range(DEPTH):
                stage = SECOND + layer
                for t in range(NT):
                    if layer == 0:
                        act.wait_ge(h_ready, NT * BETWEEN + t + 1)
                    else:
                        emptied(act, ("out2", layer - 1, 2 + t))
                    square(stage, t)
                    copy_hT(stage, *((0, 1) if t == 0 else (2,)))
                load_gain(stage + 1)
                for j in range(4):
                    emptied(act, ("hT", stage, j))
                act.copy(hT_hi, hT[:]).then_inc(hT_hi_ready, 1)

                def round_weights(q, k0, k1):
                    w = arrive2(act, layer, SPLIT[q][0])
                    for k in range(k0, k1):
                        g = chunk(layer, q, k)
                        if g >= CHUNKS:
                            chunk_left(act, g - CHUNKS)
                        act.copy(w_hi[:, g % CHUNKS, 0:w.shape[2]], w[:, k]).then_inc(chunk_hi, 1)

                def empty_ropeT(c):
                    name = ("ropeT", layer, c)
                    if c < 12:
                        dst = (qT, kT, iqT)[c // 4]
                        pc, t = (c % 4) // 2, c % 2
                        empty(name, dst[:, 4 * pc:4 * pc + 4, t * P:(t + 1) * P],
                              bank(name)[:].rearrange("p (a b) -> p a b", a=4))
                    else:
                        t = c - 12
                        empty(name, ikT[:, t * P:(t + 1) * P], bank(name)[:, 0:P])

                def empty_v(j):
                    pc, t = j // 2, j % 2
                    empty(("v", layer, j), vv[:, t, pc * 512:(pc + 1) * 512], bank(("v", layer, j))[:])

                round_weights(0, 0, KD)
                for q in range(1, 5):
                    round_weights(q, 0, CHUNKS)
                    empty_ropeT(2 * q - 2)
                    empty_ropeT(2 * q - 1)
                    round_weights(q, CHUNKS, KD)
                round_weights(QXR, 0, CHUNKS)
                for c in range(8, 14):
                    empty_ropeT(c)
                round_weights(QXR, CHUNKS, KD)
                for q in (QXR, QXR + 1, QXR + 2):
                    round_weights(q + 1, 0, CHUNKS)
                    for j in range(4 * (q - QXR), min(4 * (q - QXR) + 4, RT)):
                        full(act, ("xr", layer, j))
                        act.copy(xr[:, j, TAPS2 - 1:], bank(("xr", layer, j))[:, 0:SEQ]).then_inc(xr_half, 1)
                    round_weights(q + 1, CHUNKS, KD)
                round_weights(QV + 1, 0, CHUNKS)
                empty_v(0)
                empty_v(1)
                round_weights(QV + 1, CHUNKS, KD)
                empty_v(2)
                empty_v(3)
                for j in range(12):
                    full(act, ("dots", layer, j))
                    if layer * 12 + j >= 2:
                        act.wait_ge(relu_done, layer * 12 + j - 1)
                    empty(("dots", layer, j), relu[:, j % 2], bank(("dots", layer, j))[:], ACT.Relu)
                act.wait_ge(roped2, 14 * (layer + 1))
                for j in range(RT):
                    full(act, ("gates", layer, j))
                    S(act.activation(ra[:, j], bank(("gates", layer, j))[:, 0:SEQ], ACT.Sigmoid,
                                     bias=col(layer, "b_rg", j)))
                    empty(("gates", layer, j), ui[:, j], bank(("gates", layer, j))[:, SEQ:2 * SEQ], ACT.Sigmoid,
                          bias=col(layer, "b_ig", j))
                S.settle()
                act.wait_ge(decay_ready, 1)
                act.wait_ge(conv2_done, layer + 1)
                for j in range(RT):
                    S(act.activation(tanh_a[:, j], ra[:, j], ACT.Tanh, scale=decay[:, layer, j:j + 1]),
                      tanh_ready if j == RT - 1 else None)
                act.wait_ge(relu_done, 12 * (layer + 1))
                act.wait_ge(tanh_used, layer + 1)
                S(act.activation(tanh_a, tanh_a, ACT.Sqrt), root_ready)
                for j in range(6):
                    w = min(2, RT - 2 * j)
                    name = ("gr", layer, j)
                    full(act, name)
                    if j >= 2:
                        emptied(act, ("gr", layer, j - 2))
                    S(act.activation(roped[:, j % 2, 0:w * SEQ], bank(name)[:, 0:w * SEQ], ACT.Silu), silu_gr)

                def exponentials2(hh):
                    act.wait_ge(negmax2, layer * HEADS + hh + 1)
                    st = stat[:, 16 + 8 * (hh % 2):24 + 8 * (hh % 2)]
                    b = hh % 2
                    S(act.activation(s2[:, b, 0:P], s2[:, b, 0:P], ACT.Exp, bias=st[:, 2:3], accum_out=st[:, 4:5]))
                    S(act.activation(s2[:, b, P:], s2[:, b, P:], ACT.Exp, bias=st[:, 3:4], accum_out=st[:, 5:6]), exps2)

                act.wait_ge(hidden_ready, layer + 1)
                def gate(hh):
                    empty(("ga", layer, hh), ga_all[:, hh], bank(("ga", layer, hh))[:, 0:SEQ])

                exponentials2(0)
                gate(0)
                for hh in range(HEADS):
                    empty(("PT2", layer, hh), pT2[:, hh % 2], bank(("PT2", layer, hh))[:, 0:3 * P])
                    if hh + 1 < HEADS:
                        exponentials2(hh + 1)
                        gate(hh + 1)
                emptied(act, ("ga", layer, HEADS - 1))
                for half in range(2):
                    g = ga_all[:, 4 * half:4 * half + 4]
                    S(act.activation(g, g, ACT.Silu), silu_ga)

                def round_merged(k):
                    act.wait_ge(merged_ready, KD * layer + k + 1)
                    act.copy(hT_hi[:, k], merged[:, k]).then_inc(merged_hi, 1)

                for nm in ("mb", "ma"):
                    for j in range(8):
                        if (nm, j) == ("ma", 6):
                            round_weights(QO, 0, CHUNKS)
                        full(act, (nm, layer, j))
                        if (nm, j) not in (("mb", 0), ("mb", 1)):
                            emptied(act, (nm, layer, j - 2) if j >= 2 else ("mb", layer, 6 + j))
                        S(act.activation(s2.rearrange("p a b -> p (a b)")[:, (j % 2) * SEQ:(j % 2 + 1) * SEQ],
                                         bank((nm, layer, j))[:, 0:SEQ], ACT.Sigmoid), sig_ready)
                        if nm == "ma" and j > 0:
                            round_merged(j - 1)
                round_merged(KD - 1)
                round_weights(QO, CHUNKS, KD)
            for t in range(NT):
                emptied(act, ("out2", DEPTH - 1, 2 + t))
                square(FINAL, t)

        @block.vector
        def _(dve):
            S = Steps(dve, own_dve)

            def normalise(stage, t, dst=h):
                k = NT * stage + t + 1
                dve.wait_ge(sumsq_ready, k)
                dve.tensor_scalar(stat[:, 2 + t:3 + t], stat[:, t:t + 1], 1.0 / D, EPS, ALU.mult, ALU.add
                                  ).then_inc(mean_ready, 1)
                dve.wait_ge(rstd_ready, k + min((stage + 1) // 2, DEPTH))
                if stage == SECOND:
                    dve.wait_ge(gain_second_loaded, 16)
                else:
                    dve.wait_ge(gain_loaded, 16 * (stage + (stage < SECOND)))
                S(dve.scalar_tensor_tensor(out=dst[:, t], in0=x[:, t], scalar=stat[:, 4 + t:5 + t],
                                           in1=gain_second if stage == SECOND else gain[:],
                                           op0=ALU.mult, op1=ALU.mult), h_ready)

            def last_hT(stage):
                name = ("hT", stage, 3)
                full(dve, name)
                dve.tensor_copy(hT_part(3), bank(name)[:].rearrange("p (a b) -> p a b", b=P)
                                ).then_inc(psum_read[TILE[name] % BANKS], 1)

            for t in range(NT):
                dve.wait_ge(x_loaded[t], 16)
                normalise(0, t)
            dve.wait_ge(masks_ready, 1)

            def second_block_tables():
                dve.wait_ge(consts_loaded, 48)
                lam = cols[:, :, COLS["lam"][0]:COLS["lam"][0] + RT]
                S(dve.tensor_scalar(lam_t[:, 3], lam, -1.0, None, ALU.mult))
                S.settle()
                dve.tensor_tensor(lam_t[:, 0], lam, lam_t[:, 3], ALU.max).then_inc(lam_in, 1)
                S(dve.tensor_copy(pos_f[:], pos_i[:]))
                S.settle()
                for t in range(NT):
                    S(dve.tensor_scalar(ang[:, t], rows[:, INV0:INV0 + INV2], pos_f[:, t:t + 1], None, ALU.mult))
                S.settle()
                S(dve.tensor_scalar(cos2[:], ang[:], float(1.0 / (2 * np.pi)), ROUNDER, ALU.mult, ALU.add))
                S.settle()
                S(dve.tensor_scalar(cos2[:], cos2[:], ROUNDER, None, ALU.subtract))
                for part in TWO_PI_PARTS:
                    S.settle()
                    S(dve.scalar_tensor_tensor(out=ang[:], in0=cos2[:], scalar=-part, in1=ang[:],
                                               op0=ALU.mult, op1=ALU.add))
                S.settle()
                S(dve.tensor_scalar(sin2[:], ang[:], 3.1415925, -3.1415925, ALU.min, ALU.max))
                S.settle()
                S(dve.scalar_tensor_tensor(out=cos2[:], in0=sin2[:], scalar=-1.0, in1=sin2[:], op0=ALU.mult, op1=ALU.max))
                S.settle()
                S(dve.tensor_scalar(cos2[:], cos2[:], -1.0, float(np.pi / 2), ALU.mult, ALU.add), angles_ready)
                dve.wait_ge(lam_exp, 1)
                S(dve.tensor_scalar(lam_t[:, 2], lam_t[:, 1], 2.0, None, ALU.add))
                S.settle()
                S(dve.reciprocal(lam_t[:, 2], lam_t[:, 2]))
                S.settle()
                S(dve.tensor_tensor(lam_t[:, 1], lam_t[:, 1], lam_t[:, 2], ALU.mult))
                S.settle()
                S(dve.tensor_tensor(lam_t[:, 2], lam_t[:, 1], lam_t[:, 1], ALU.mult))
                S.settle()
                S(dve.tensor_scalar(lam_t[:, 0], lam_t[:, 2], 2.0 / 17, None, ALU.mult))
                for n in (15, 13, 11, 9, 7, 5, 3):
                    S.settle()
                    S(dve.scalar_tensor_tensor(out=lam_t[:, 0], in0=lam_t[:, 0], scalar=2.0 / n, in1=lam_t[:, 2],
                                               op0=ALU.add, op1=ALU.mult))
                S.settle()
                S(dve.scalar_tensor_tensor(out=lam_t[:, 0], in0=lam_t[:, 0], scalar=2.0, in1=lam_t[:, 1],
                                           op0=ALU.add, op1=ALU.mult))
                S.settle()
                S(dve.scalar_tensor_tensor(out=lam_t[:, 3], in0=lam_t[:, 3], scalar=0.0, in1=lam_t[:, 0],
                                           op0=ALU.max, op1=ALU.add))
                S.settle()
                S(dve.tensor_scalar(decay[:], lam_t[:, 3], LRU_C / 2, None, ALU.mult), decay_ready)

            def first_mixer(layer):
                stage = 2 * layer
                last_hT(stage)
                if layer == 0:
                    second_block_tables()
                for t in range(NT):
                    emptied(dve, ("q", layer, t))
                    emptied(dve, ("kv", layer, t))
                dve.wait_ge(rope1_loaded, 32)
                heads = [qkv[:, t, 0:QW + KVW].rearrange("p (h d) -> p h d", d=HD1) for t in range(NT)]
                tab = [[z.rearrange("p (t h d) -> p t h d", t=NT, d=ROT1)[:, t] for t in range(NT)] for z in (cos1, sin1)]
                tmp = [[rt1[:, z].rearrange("p (t h d) -> p t h d", t=NT, d=ROT1)[:, t] for t in range(NT)]
                       for z in range(4)]
                for t in range(NT):
                    a, b = heads[t][:, :, 0:ROT1], heads[t][:, :, ROT1:2 * ROT1]
                    S(dve.tensor_tensor(tmp[0][t], a, tab[0][t], ALU.mult))
                    S(dve.tensor_tensor(tmp[1][t], b, tab[1][t], ALU.mult))
                    S(dve.tensor_tensor(tmp[2][t], b, tab[0][t], ALU.mult))
                    S(dve.tensor_tensor(tmp[3][t], a, tab[1][t], ALU.mult))
                S.settle()
                for t in range(NT):
                    a, b = heads[t][:, :, 0:ROT1], heads[t][:, :, ROT1:2 * ROT1]
                    S(dve.tensor_tensor(a, tmp[0][t], tmp[1][t], ALU.subtract))
                    S(dve.tensor_tensor(b, tmp[2][t], tmp[3][t], ALU.add))
                S.settle()
                S(dve.tensor_copy(kswap[:, :, 0:HD1], qkv[:, :, QW + HD1:QW + KVW]))
                S(dve.tensor_copy(kswap[:, :, HD1:], qkv[:, :, QW:QW + HD1]), roped1)
                S(dve.memset(cu[:, :, 0:1], 0.0))
                S(dve.memset(cu[:, :, SEQ + 1:], 0.0))

                def gated_input(j):
                    name = ("u", layer, j)
                    emptied(dve, ("gc", layer, j))
                    full(dve, name)
                    S.settle()
                    S.marks(dve.tensor_tensor(cu[:, j, 1:SEQ + 1], bank(name)[:, 0:SEQ], gc[:, j], ALU.mult),
                            psum_read[TILE[name] % BANKS], uses(name))

                sink = rows[:, SINK0 + layer * HEADS:SINK0 + (layer + 1) * HEADS]

                def logits(hh):
                    name = ("S1", layer, hh)
                    st = stat[:, 16 + 8 * (hh % 2):24 + 8 * (hh % 2)]
                    full(dve, name)
                    if hh >= 2:
                        full(dve, ("PT1", layer, hh - 2))
                    S.marks(dve.scalar_tensor_tensor(out=s1[:, hh % 2], in0=bank(name)[:].rearrange("p (a b) -> p a b", a=2),
                                                     scalar=HD1 ** -0.5, in1=window, op0=ALU.mult, op1=ALU.add),
                            psum_read[TILE[name] % BANKS], uses(name))
                    S.settle()
                    S(dve.tensor_reduce(st[:, 0:2], s1[:, hh % 2], AX.X, ALU.max))
                    S.settle()
                    S(dve.tensor_scalar(st[:, 2:4], st[:, 0:2], sink[:, hh:hh + 1], -1.0, ALU.max, ALU.mult), negmax)

                def weights(hh):
                    st = stat[:, 16 + 8 * (hh % 2):24 + 8 * (hh % 2)]
                    dve.wait_ge(exps, layer * HEADS + hh + 1)
                    S(dve.tensor_tensor(st[:, 4:6], st[:, 4:6], st[:, 6:8], ALU.add))
                    S.settle()
                    S(dve.reciprocal(st[:, 4:6], st[:, 4:6]))
                    S.settle()
                    for qb in range(NT):
                        S(dve.tensor_scalar(s1[:, hh % 2, qb], s1[:, hh % 2, qb], st[:, 4 + qb:5 + qb], None, ALU.mult),
                          probs if qb == NT - 1 else None)

                logits(0)
                weights(0)
                gated_input(0)
                for hh in range(HEADS):
                    if hh + 1 < HEADS:
                        logits(hh + 1)
                        weights(hh + 1)
                    for nm, j in BESIDE_HEAD[hh]:
                        if nm == "u":
                            gated_input(j)
                name = ("ss", layer, 0)
                full(dve, name)
                S.marks(dve.tensor_scalar(stat[:, 8:12], bank(name)[:].rearrange("p (a b) -> p a b", b=P)[:, :, 0],
                                          1.0 / CW, EPS, ALU.mult, ALU.add), psum_read[TILE[name] % BANKS], uses(name))
                dve.wait_ge(rstd_ready, 5 * layer + 3)
                for i in range(8):
                    hf, t, part = OUT1[i]
                    name = ("out1", layer, i)
                    full(dve, name)
                    S.settle()
                    xs = x[:, t, hf * 512:(hf + 1) * 512]
                    S.marks(dve.scalar_tensor_tensor(out=xs, in0=bank(name)[:], scalar=stat[:, 12 + 2 * part + t:13 + 2 * part + t],
                                                     in1=xs, op0=ALU.mult, op1=ALU.add),
                            psum_read[TILE[name] % BANKS], uses(name))
                    if i in (5, 7):
                        S.settle()
                        normalise(stage + 1, t)

            def pick_first(dst, src, mx, idx, wide, far):
                n = src.shape[-1]
                S(dve.tensor_tensor(dst, src, mx.unsqueeze(2).to_broadcast([P, NT, n]), ALU.is_equal))
                S.settle()
                S(dve.scalar_tensor_tensor(out=wide, in0=dst, scalar=-far, in1=idx, op0=ALU.mult, op1=ALU.add))
                S.settle()
                S(dve.tensor_reduce(stat[:, 42:44], wide, AX.X, ALU.min))
                S.settle()
                S(dve.tensor_tensor(dst, wide, stat[:, 42:44].unsqueeze(2).to_broadcast([P, NT, n]), ALU.is_equal))
                S.settle()

            def router(layer):
                name = ("logits", layer, 0)
                full(dve, name)
                lg = bank(name)[:, 0:2 * P].rearrange("p (t n) -> p t n", t=NT)
                bias = rows[:, layer * ROUTER_W:(layer + 1) * ROUTER_W]
                idx = iota_f[:, 0:NE]
                for t in range(NT):
                    S(dve.tensor_tensor(small[:, 0, t, 0:GROUPS], lg[:, t, 0:GROUPS], bias[:, 0:GROUPS], ALU.add))
                S(dve.tensor_tensor(small[:, 1, 0], lg[:, 0, GROUPS:ROUTER_W], bias[:, GROUPS:], ALU.add))
                S.marks(dve.tensor_tensor(small[:, 1, 1], lg[:, 1, GROUPS:ROUTER_W], bias[:, GROUPS:], ALU.add),
                        psum_read[TILE[name] % BANKS], uses(name))
                S.settle()
                gl = small[:, 0, :, 0:GROUPS]
                gmax = stat[:, 32:34]
                S(dve.tensor_reduce(gmax, gl, AX.X, ALU.max))
                S.settle()
                S(dve.tensor_tensor(small[:, 2, :, 0:GROUPS], gl, gmax.unsqueeze(2).to_broadcast([P, NT, GROUPS]),
                                    ALU.subtract), route_exp_in)
                oh = small[:, 4, :, 0:GROUPS]
                idx_g = idx[:, 0:GROUPS].unsqueeze(1).to_broadcast([P, NT, GROUPS])
                pick_first(oh, gl, gmax, idx_g, small[:, 5, :, 0:GROUPS], 64.0)
                S(dve.tensor_scalar(oh, oh, -NEG, NEG, ALU.mult, ALU.add))
                S.settle()
                for t in range(NT):
                    S(dve.tensor_tensor(small[:, 6, t].rearrange("p (g e) -> p g e", g=GROUPS),
                                        small[:, 1, t].rearrange("p (g e) -> p g e", g=GROUPS),
                                        small[:, 4, t, 0:GROUPS].unsqueeze(2).to_broadcast([P, GROUPS, PER_GROUP]), ALU.add))
                S.settle()
                idx_e = idx.unsqueeze(1).to_broadcast([P, NT, NE])
                m1, m2 = stat[:, 34:36], stat[:, 36:38]
                S(dve.tensor_reduce(m1, small[:, 6], AX.X, ALU.max))
                S.settle()
                pick_first(small[:, 7], small[:, 6], m1, idx_e, small[:, 5], 64.0)
                S(dve.scalar_tensor_tensor(out=small[:, 8], in0=small[:, 7], scalar=TAKEN, in1=small[:, 6],
                                           op0=ALU.mult, op1=ALU.add))
                S.settle()
                S(dve.tensor_reduce(m2, small[:, 8], AX.X, ALU.max))
                S.settle()
                pick_first(small[:, 9], small[:, 8], m2, idx_e, small[:, 5], 64.0)
                S(dve.tensor_tensor(small[:, 10], small[:, 7], small[:, 9], ALU.add), assign_ready)
                S(dve.tensor_tensor(stat[:, 38:40], m2, m1, ALU.subtract), route_exp_in)
                dve.wait_ge(route_exp_out, 2 * layer + 2)
                S(dve.tensor_reduce(stat[:, 44:46], small[:, 3, :, 0:GROUPS], AX.X, ALU.add))
                S(dve.tensor_scalar(stat[:, 46:48], stat[:, 40:42], 1.0, None, ALU.add))
                S.settle()
                S(dve.tensor_tensor(stat[:, 46:48], stat[:, 46:48], stat[:, 44:46], ALU.mult))
                S.settle()
                S(dve.reciprocal(stat[:, 46:48], stat[:, 46:48]))
                S.settle()
                S(dve.tensor_tensor(stat[:, 48:50], stat[:, 46:48], stat[:, 40:42], ALU.mult))
                S.settle()
                for t in range(NT):
                    S(dve.tensor_scalar(small[:, 11, t], small[:, 7, t], stat[:, 46 + t:47 + t], None, ALU.mult))
                S.settle()
                for t in range(NT):
                    S(dve.scalar_tensor_tensor(out=small[:, 12, t], in0=small[:, 9, t], scalar=stat[:, 48 + t:49 + t],
                                               in1=small[:, 11, t], op0=ALU.mult, op1=ALU.add))
                name = ("rank", layer, 0)
                full(dve, name)
                rk = bank(name)[:, 0:3 * NE].rearrange("p (a n) -> p a n", a=3)
                S(dve.scalar_tensor_tensor(out=small[:, 13], in0=rk[:, 0:NT], scalar=1.0, in1=small[:, 10],
                                           op0=ALU.add, op1=ALU.mult))
                S.settle()
                S(dve.tensor_scalar(small[:, 14], small[:, 13], -1.0, None, ALU.add))
                S.marks(dve.tensor_reduce(stat[:, 50:51], rk[:, 2], AX.X, ALU.max),
                        psum_read[TILE[name] % BANKS], uses(name))
                S.settle()

            def turns(layer):
                S.settle()
                for r in range(1, ROUNDS):
                    S(dve.tensor_scalar(stat[:, 50 + r:51 + r], stat[:, 50:51], float(SLOTS * r), float(GROUPS),
                                        ALU.is_gt, ALU.mult))
                S.settle()
                S(dve.tensor_reduce(stat[:, 54:55], stat[:, 51:50 + ROUNDS], AX.X, ALU.add))
                S.settle()
                S(dve.tensor_scalar(trips_i[:, 1:2], stat[:, 54:55], float(GROUPS - 1), None, ALU.add))
                S(dve.tensor_scalar(trips_i[:, 0:1], stat[:, 54:55], float(GROUPS), None, ALU.add), trips_ready)
                S.settle()

            def experts(layer):
                M = moe[layer]

                def picks(T, g):
                    slots = small[:, 14, :, bass.ds(g, PER_GROUP)]
                    for t in range(NT):
                        T(dve.tensor_tensor(pick[:, t], iota_f[:].unsqueeze(1).to_broadcast([P, PER_GROUP, SLOTS]),
                                            slots[:, t].unsqueeze(2).to_broadcast([P, PER_GROUP, SLOTS]), ALU.is_equal))
                    T.settle()
                    T(dve.tensor_scalar(slots, slots, -float(SLOTS), None, ALU.add), M["picked"])

                def weighted_picks(T, g):
                    gates = small[:, 12, :, bass.ds(g, PER_GROUP)]
                    T.settle()
                    for t in range(NT):
                        T(dve.tensor_tensor(wpick[:, t], pick[:, t],
                                            gates[:, t].unsqueeze(2).to_broadcast([P, PER_GROUP, SLOTS]), ALU.mult),
                          M["wpicked"] if t == NT - 1 else None)
                    T.settle()

                picks(S, 0)
                turns(layer)
                weighted_picks(S, 0)
                name = ("gather", layer, 1)
                full(dve, name)
                dve.tensor_copy(gathered(0, 1), bank(name)[:]).then_inc(psum_read[TILE[name] % BANKS], 1)
                n = dve.value_load(trips_i[0:1, 0:1], min_val=GROUPS, max_val=GROUPS * ROUNDS)
                STEPS = 3
                with dve.Fori(0, n) as i:
                    T = Steps(dve, M["dve"], {M["dve"].name: i * STEPS, M["picked"].name: i + 1,
                                              M["wpicked"].name: i + 1})
                    next_group = ((i + 1) % GROUPS) * PER_GROUP

                    def m_full(m):
                        dve.wait_ge(M[f"full{4 + m % 4}"], i * PER_BANK + (m // 4 + 1))

                    def m_bank(m):
                        return banks[4 + m % 4]

                    for p in range(4):
                        b = p % 2
                        m0 = PAIR_TILES * p
                        m = m0 + T_COMB
                        m_full(m)
                        dve.tensor_copy(comb[:, b], m_bank(m)[:, 0:SEQ]).then_inc(M[f"read{4 + m % 4}"], 1)
                        for side in range(2):
                            m = m0 + T_GU + side
                            up = slice(0, 64) if side == 0 else slice(64, P)
                            dve.wait_ge(M["silu"], i * 8 + (2 * p + side + 1))
                            dve.tensor_tensor(hid[up, b], silu_g[up, b], m_bank(m)[up, :], ALU.mult
                                              ).then_inc(M[f"read{4 + m % 4}"], 1)
                        if p == 3:
                            weighted_picks(T, next_group)
                        m = m0 + T_NEXT + 1
                        m_full(m)
                        dve.tensor_copy(gathered(1 - b, 1), m_bank(m)[:]).then_inc(M[f"read{4 + m % 4}"], 1)
                        if p == 2:
                            picks(T, next_group)
                        m = m0 + T_OUT + 1
                        m_full(m)
                        dve.tensor_copy(ysb[:, b, 512:], m_bank(m)[:]).then_inc(M[f"read{4 + m % 4}"], 1)
                    assert T.n[M["dve"].name] == STEPS
                dve.wait_ge(M["scattered"], n)
                for t in range(NT):
                    for hf in range(2):
                        xs = x[:, t, hf * 512:(hf + 1) * 512]
                        S(dve.tensor_tensor(xs, banks[2 * t + hf][:], xs, ALU.add), M["x_ready"] if hf else None)
                for t in range(NT):
                    normalise(2 * layer + 2, t, h if layer + 1 < DEPTH else x)

            def second(layer):
                stage = SECOND + layer
                if layer == 0:
                    dve.wait_ge(tables2_ready, 1)
                    S.settle()
                S(dve.memset(xr[:, :, 0:TAPS2 - 1], 0.0))
                last_hT(stage)
                dve.wait_ge(hT_hi_ready, layer + 1)
                dve.tensor_tensor(hT_lo, hT[:], hT_hi, ALU.subtract).then_inc(hT_lo_ready, 1)
                for c in range(14):
                    name = ("rope", layer, c)
                    t = c % 2
                    full(dve, name)
                    if c >= 4:
                        full(dve, ("ropeT", layer, c - 4))
                    half = HD2 // 2 if c < 8 else ID // 2
                    t0 = 0 if c < 8 else HD2 // 2
                    nh = 512 // (2 * half) if c < 12 else 1
                    src = bank(name)[:, 0:nh * 2 * half].rearrange("p (h s d) -> p h s d", h=nh, s=2)
                    dst = roped[:, c % 4, 0:nh * 2 * half].rearrange("p (h s d) -> p h s d", h=nh, s=2)
                    tmp = ropetmp[:, c % 2, 0:nh * 2 * half].rearrange("p (h s d) -> p h s d", h=nh, s=2)
                    cs = cos2[:, t, t0:t0 + half].unsqueeze(1).to_broadcast([P, nh, half])
                    sn = sin2[:, t, t0:t0 + half].unsqueeze(1).to_broadcast([P, nh, half])
                    for s in range(2):
                        S(dve.tensor_tensor(dst[:, :, s], src[:, :, s], cs, ALU.mult))
                        S(dve.tensor_tensor(tmp[:, :, s], src[:, :, 1 - s], sn, ALU.mult))
                    if c >= 12:
                        S(dve.tensor_scalar(iw[:, t], bank(name)[:, ID:ID + IH], IH ** -0.5 * ID ** -0.5, None, ALU.mult))
                    S.settle()
                    S.marks(dve.tensor_tensor(dst[:, :, 0], dst[:, :, 0], tmp[:, :, 0], ALU.subtract),
                            psum_read[TILE[name] % BANKS], uses(name))
                    S(dve.tensor_tensor(dst[:, :, 1], dst[:, :, 1], tmp[:, :, 1], ALU.add), roped2 if c < 12 else None)
                    if c >= 12:
                        S.settle()
                        S(dve.tensor_copy(roped[:, c % 4, ID:2 * ID], roped[:, c % 4, 0:ID]), roped2)
                for j in range(RT):
                    if j % 4 == 0:
                        for jj in range(j, min(j + 4, RT)):
                            name = ("xr", layer, jj)
                            dve.wait_ge(xr_half, RT * layer + jj + 1)
                            S.marks(dve.tensor_tensor(xr[:, jj, TAPS2 - 1:], xr[:, jj, TAPS2 - 1:], bank(name)[:, SEQ:],
                                                      ALU.add), psum_read[TILE[name] % BANKS], uses(name))
                        S.settle()
                    S(dve.tensor_scalar(xc[:, j], xr[:, j, 0:SEQ], col(layer, "conv2", j), col(layer, "conv2_b", j),
                                        ALU.mult, ALU.add))
                    for tap in range(1, TAPS2):
                        S.settle()
                        S(dve.scalar_tensor_tensor(out=xc[:, j], in0=xr[:, j, tap:tap + SEQ],
                                                   scalar=col(layer, "conv2", tap * RT + j), in1=xc[:, j],
                                                   op0=ALU.mult, op1=ALU.add),
                          conv2_done if (j, tap) == (RT - 1, TAPS2 - 1) else None)
                for j in range(12):
                    emptied(dve, ("dots", layer, j))
                    for piece_ in range(4 if j < 4 else 2):
                        if j < 4:
                            hd = 8 * (j // 2) + 2 * piece_ + j % 2
                            acc, src, qb = wk[:, 0, 0:P], relu[:, j % 2, piece_ * P:(piece_ + 1) * P], 0
                        else:
                            jj = j - 4
                            hd = 4 * (jj // 2) + 2 * piece_ + jj % 2
                            acc, src, qb = wk[:, 0, P:], relu[:, j % 2, piece_ * SEQ:(piece_ + 1) * SEQ], 1
                        lastp = piece_ == (3 if j < 4 else 1)
                        S.settle()
                        if hd == 0:
                            ins = dve.tensor_scalar(acc, src, iw[:, qb, hd:hd + 1], None, ALU.mult)
                        else:
                            ins = dve.scalar_tensor_tensor(out=acc, in0=src, scalar=iw[:, qb, hd:hd + 1], in1=acc,
                                                           op0=ALU.mult, op1=ALU.add)
                        S(ins, relu_done if lastp else None)
                S.settle()
                S(dve.tensor_tensor(wk[:, 0], wk[:, 0], causal[:], ALU.add))
                S.settle()
                for r in range(TOPK // 8):
                    a, b = r % 2, (r + 1) % 2
                    for sl in (slice(0, P), slice(P, 3 * P)):
                        o = 0 if sl.start == 0 else 8
                        S(dve.max(top8[:, o:o + 8], wk[:, a, sl]))
                    S.settle()
                    for sl in (slice(0, P), slice(P, 3 * P)):
                        o = 0 if sl.start == 0 else 8
                        S(dve.match_replace(wk[:, b, sl], top8[:, o:o + 8], wk[:, a, sl], TAKEN))
                    S.settle()
                S(dve.tensor_scalar(wk[:, 1], wk[:, 0], TAKEN, -NEG, ALU.is_equal, ALU.mult))
                S.settle()
                S(dve.scalar_tensor_tensor(out=bias2, in0=wk[:, 1], scalar=NEG, in1=causal[:], op0=ALU.add, op1=ALU.add))
                S.settle()
                emptied(dve, ("gates", layer, RT - 1))
                S(dve.tensor_tensor(ui, ui, xc, ALU.mult))
                S.settle()
                dve.wait_ge(tanh_ready, layer + 1)
                S(dve.tensor_scalar(xc, tanh_a, 1.0, None, ALU.add), tanh_used)
                S.settle()
                S(dve.reciprocal(xc, xc))
                S.settle()
                S(dve.tensor_scalar(ra, xc, 2.0, -1.0, ALU.mult, ALU.add))
                S(dve.scalar_tensor_tensor(out=ui, in0=xc, scalar=2.0, in1=ui, op0=ALU.mult, op1=ALU.mult))
                S.settle()
                dve.wait_ge(root_ready, layer + 1)
                S(dve.tensor_tensor(ui, ui, tanh_a, ALU.mult))
                S.settle()
                for j in range(RT):
                    S(dve.tensor_tensor_scan(xc[:, j], ra[:, j], ui[:, j], 0.0, ALU.mult, ALU.add),
                      hidden_ready if j == RT - 1 else None)
                S.settle()
                for j in range(6):
                    w = min(2, RT - 2 * j)
                    name = ("gr", layer, j)
                    dve.wait_ge(silu_gr, layer * 6 + j + 1)
                    S.marks(dve.tensor_tensor(ui[:, 2 * j:2 * j + w], xc[:, 2 * j:2 * j + w],
                                              roped[:, j % 2, 0:w * SEQ].rearrange("p (a b) -> p a b", a=w), ALU.mult),
                            psum_read[TILE[name] % BANKS], uses(name))
                S.settle()

                def logits(hh):
                    name = ("S2", layer, hh)
                    st = stat[:, 16 + 8 * (hh % 2):24 + 8 * (hh % 2)]
                    b = hh % 2
                    full(dve, name)
                    if hh >= 2:
                        full(dve, ("PT2", layer, hh - 2))
                    S.marks(dve.scalar_tensor_tensor(out=s2[:, b], in0=bank(name)[:, 0:3 * P], scalar=HD2 ** -0.5,
                                                     in1=bias2, op0=ALU.mult, op1=ALU.add),
                            psum_read[TILE[name] % BANKS], uses(name))
                    S.settle()
                    S(dve.tensor_reduce(st[:, 0:1], s2[:, b, 0:P], AX.X, ALU.max))
                    S(dve.tensor_reduce(st[:, 1:2], s2[:, b, P:], AX.X, ALU.max))
                    S.settle()
                    S(dve.tensor_scalar(st[:, 2:4], st[:, 0:2], -1.0, None, ALU.mult), negmax2)

                def weights(hh):
                    st = stat[:, 16 + 8 * (hh % 2):24 + 8 * (hh % 2)]
                    b = hh % 2
                    dve.wait_ge(exps2, layer * HEADS + hh + 1)
                    S(dve.reciprocal(st[:, 4:6], st[:, 4:6]))
                    S.settle()
                    S(dve.tensor_scalar(s2[:, b, 0:P], s2[:, b, 0:P], st[:, 4:5], None, ALU.mult))
                    S(dve.tensor_scalar(s2[:, b, P:], s2[:, b, P:], st[:, 5:6], None, ALU.mult), probs2)

                def attended(hh):
                    name = ("Y2", layer, hh)
                    full(dve, name)
                    S.marks(dve.tensor_copy(qT[:, hh], bank(name)[:, 0:SEQ]), psum_read[TILE[name] % BANKS], uses(name))

                logits(0)
                weights(0)
                for hh in range(HEADS):
                    if hh + 1 < HEADS:
                        logits(hh + 1)
                        weights(hh + 1)
                    attended(hh)
                S.settle()
                for half in range(2):
                    dve.wait_ge(silu_ga, 2 * layer + half + 1)
                    y = qT[:, 4 * half:4 * half + 4]
                    S(dve.tensor_tensor(y, y, ga_all[:, 4 * half:4 * half + 4], ALU.mult), attn_gated)
                sig = [s2.rearrange("p a b -> p (a b)")[:, b * SEQ:(b + 1) * SEQ] for b in range(2)]
                for j in range(8):
                    name = ("mb", layer, j)
                    dve.wait_ge(sig_ready, layer * 16 + j + 1)
                    S.marks(dve.tensor_tensor(merged[:, j], sig[j % 2], bank(name)[:, SEQ:], ALU.mult),
                            psum_read[TILE[name] % BANKS], uses(name))

                def rest_of_merged(k):
                    dve.wait_ge(merged_hi, KD * layer + k + 1)
                    dve.tensor_tensor(hT_lo[:, k], merged[:, k], hT_hi[:, k], ALU.subtract).then_inc(merged_lo, 1)

                for j in range(8):
                    name = ("ma", layer, j)
                    dve.wait_ge(sig_ready, layer * 16 + 8 + j + 1)
                    S.settle()
                    S.marks(dve.tensor_tensor(pT2[:, 0, 0:SEQ], sig[j % 2], bank(name)[:, SEQ:], ALU.mult),
                            psum_read[TILE[name] % BANKS], uses(name))
                    S.settle()
                    S(dve.tensor_tensor(merged[:, j], merged[:, j], pT2[:, 0, 0:SEQ], ALU.add), merged_ready)
                    if j > 0:
                        rest_of_merged(j - 1)
                rest_of_merged(KD - 1)
                for i in range(4):
                    name = ("out2", layer, i)
                    pc, t = i // 2, i % 2
                    full(dve, name)
                    xs = x[:, t, pc * 512:(pc + 1) * 512]
                    S.marks(dve.tensor_tensor(xs, bank(name)[:], xs, ALU.add), psum_read[TILE[name] % BANKS], uses(name))
                    if pc == 1:
                        S.settle()
                        normalise(stage + 1, t)

            S(dve.tensor_scalar(causal[:, 0:P], before[:], NEG, None, ALU.mult))
            S(dve.memset(causal[:, P:2 * P], 0.0))
            S(dve.tensor_scalar(causal[:, 2 * P:], before[:], NEG, None, ALU.mult))
            S.settle()
            for layer in range(DEPTH):
                first_mixer(layer)
                last_hT(2 * layer + 1)
                router(layer)
                experts(layer)
            for t in range(NT):
                normalise(SECOND, t)
            for layer in range(DEPTH):
                second(layer)

        @block.tensor
        def _(pe):
            def claim(name):
                if TILE[name] >= BANKS:
                    pe.wait_ge(psum_read[TILE[name] % BANKS], uses(name) - 1)

            def done(mm, name):
                mm.then_inc(psum_full[TILE[name] % BANKS], 1)

            def keep_clock(name, n):
                claim(name)
                for _ in range(n):
                    pe.matmul(bank(name)[:, 0:P], zeros[:], ones[:], start=True, stop=True)

            def turn_h(stage, t, idle=0):
                if idle > 0:
                    after_experts = stage == SECOND or (stage > 0 and stage % 2 == 0)
                    keep_clock(next(("hT", stage, j) for j in range(2 * t, 4)
                                    if not after_experts or TILE[("hT", stage, j)] % BANKS >= MOE_BANKS), idle)
                pe.wait_ge(h_ready, NT * stage + t + 1)
                for j in (2 * t, 2 * t + 1):
                    name = ("hT", stage, j)
                    claim(name)
                    for k in range(4):
                        f = 4 * (j % 2) + k
                        mm = pe.transpose(bank(name)[:, k * P:(k + 1) * P], h[:, t, f * P:(f + 1) * P], ident[:])
                    done(mm, name)
                for j in (2 * t, 2 * t + 1):
                    emptied(pe, ("hT", stage, j))

            def by_token(name, w, n, t):
                claim(name)
                for k in range(KD):
                    mm = pe.matmul(bank(name)[:, 0:n], hT[:, k, t * P:(t + 1) * P], w[:, k, 0:n],
                                   start=(k == 0), stop=(k == KD - 1))
                done(mm, name)

            def by_feature(dst, w, f, rhs=None, nk=KD):
                rhs = hT if rhs is None else rhs
                for k in range(nk):
                    mm = pe.matmul(dst, w[:, k, f * P:(f + 1) * P], rhs[:, k], start=(k == 0), stop=(k == nk - 1))
                return mm

            def gather(dst, half, pair):
                for kk in range(KD // 2):
                    k = half * KD // 2 + kk
                    for t in range(NT):
                        mm = pe.matmul(dst[:, kk * P:(kk + 1) * P], h[:, t, k * P:(k + 1) * P],
                                       pick[:, t, 2 * pair:2 * pair + 2].rearrange("p a b -> p (a b)"),
                                       start=(t == 0), stop=(t == NT - 1))
                return mm

            pe.wait_ge(masks_ready, 1)

            for layer in range(DEPTH):
                seg = f"mix{layer}"

                def arrive(j):
                    pe.wait_ge(w_loaded[seg][mixer_piece(j)], mixer_count(j))
                    return piece(mixer_piece(j), KD, MIX_PIECES[j][2])

                for t in range(NT):
                    turn_h(2 * layer, t, (IDLE_START if layer == 0 else IDLE_EXPERTS) if t == 0 else 0)
                    w = arrive(0)
                    by_token(("q", layer, t), w, 512, t)
                w = arrive(1)
                for t in range(NT):
                    by_token(("kv", layer, t), w, 2 * KVW, t)

                def gate_tile(nm, j):
                    w_ = arrive({"gc": 2, "u": 3, "gb": 4}[nm])
                    name = (nm, layer, j)
                    claim(name)
                    done(by_feature(bank(name)[:, 0:SEQ], w_, j), name)

                gate_tile("gc", 0)
                gate_tile("gc", 1)
                pe.wait_ge(roped1, layer + 1)
                for j in range(3):
                    name = ("qkT", layer, j)
                    claim(name)
                    for k in range(2):
                        for t in range(NT):
                            src = (qkv[:, t, (2 * j + k) * P:(2 * j + k + 1) * P] if j < 2 else
                                   (qkv[:, t, QW:QW + KVW] if k == 0 else kswap[:, t]))
                            mm = pe.transpose(bank(name)[:, k * SEQ + t * P:k * SEQ + (t + 1) * P], src, ident[:])
                    done(mm, name)
                for j in range(3):
                    emptied(pe, ("qkT", layer, j))

                def scores(hh):
                    name = ("S1", layer, hh)
                    claim(name)
                    r = slice(64 * (hh % 2), 64 * (hh % 2) + 64)
                    kk = kT1[r, 0 if hh % 2 == hh // 4 else 1]
                    for qb in range(NT):
                        mm = pe.matmul(bank(name)[:, qb * SEQ:(qb + 1) * SEQ], qT1[r, hh // 2, qb * P:(qb + 1) * P], kk,
                                       start=True, stop=True)
                    done(mm, name)

                def mixer_out(i):
                    hf, t, part = OUT1[i]
                    name = ("out1", layer, i)
                    w_ = arrive(5 + hf)
                    claim(name)
                    for j in range(4):
                        mm = pe.matmul(bank(name)[:], yT[:, 4 * part + j, t * P:(t + 1) * P], w_[:, 4 * part + j],
                                       start=(j == 0), stop=(j == 3))
                    done(mm, name)

                scores(0)
                gate_tile("u", 0)
                for hh in range(HEADS):
                    if hh + 1 < HEADS:
                        scores(hh + 1)
                    name = ("PT1", layer, hh)
                    claim(name)
                    pe.wait_ge(probs, layer * HEADS + hh + 1)
                    for kb in range(NT):
                        for qb in range(NT):
                            mm = pe.transpose(bank(name)[:, kb * SEQ + qb * P:kb * SEQ + (qb + 1) * P],
                                              s1[:, hh % 2, qb, kb * P:(kb + 1) * P], ident[:])
                    done(mm, name)
                    for nm, j in BESIDE_HEAD[hh]:
                        if nm == "out1":
                            pe.wait_ge(conv_sq, 4 * layer + 4)
                            mixer_out(j)
                        else:
                            gate_tile(nm, j)
                    emptied(pe, ("PT1", layer, hh))
                    yn = ("Y1", layer, hh // 2)
                    if hh % 2 == 0:
                        claim(yn)
                    r = slice(64 * (hh % 2), 64 * (hh % 2) + 64)
                    v0 = QW + KVW + (hh // 4) * HD1
                    for kb in range(NT):
                        mm = pe.matmul(bank(yn)[r, 0:SEQ], qkv[:, kb, v0:v0 + HD1], pT1[:, hh % 2, kb],
                                       start=(kb == 0), stop=(kb == NT - 1))
                    if hh % 2 == 1:
                        done(mm, yn)
                for j in range(4):
                    emptied(pe, ("Y1", layer, j))
                name = ("ss", layer, 0)
                claim(name)
                for part in range(2):
                    for t in range(NT):
                        o = (2 * part + t) * P
                        for j in range(4):
                            mm = pe.matmul(bank(name)[:, o:o + P], sq[:, 4 * part + j, t * P:(t + 1) * P], ones[:],
                                           start=(j == 0), stop=(j == 3))
                done(mm, name)
                for i in range(2, 8):
                    mixer_out(i)

                pe.wait_ge(router_loaded, 16 * (layer + 1))
                name = ("logits", layer, 0)
                for t in range(NT):
                    turn_h(2 * layer + 1, t, 0 if t == 0 else IDLE_MIXER)
                    if t == 0:
                        claim(name)
                    for k in range(KD):
                        mm = pe.matmul(bank(name)[:, t * P:(t + 1) * P], hT[:, k, t * P:(t + 1) * P], w_router[:, k],
                                       start=(k == 0), stop=(k == KD - 1))
                done(mm, name)
                name = ("rank", layer, 0)
                keep_clock(name, IDLE_ROUTER)
                pe.wait_ge(assign_ready, layer + 1)
                A = small[:, 10]
                pe.matmul(bank(name)[:, 0:NE], before[:], A[:, 0], start=True, stop=True)
                pe.matmul(bank(name)[:, NE:2 * NE], before[:], A[:, 1], start=True, stop=False)
                pe.matmul(bank(name)[:, NE:2 * NE], ones[:], A[:, 0], start=False, stop=True)
                pe.matmul(bank(name)[:, 2 * NE:3 * NE], ones[:], A[:, 0], start=True, stop=False)
                mm = pe.matmul(bank(name)[:, 2 * NE:3 * NE], ones[:], A[:, 1], start=False, stop=True)
                done(mm, name)

                keep_clock(("gather", layer, 0), IDLE_PICKS)
                pe.wait_ge(moe[layer]["picked"], 1)
                for half in range(2):
                    name = ("gather", layer, half)
                    claim(name)
                    done(gather(bank(name), half, 0), name)
                M = moe[layer]
                seg = f"moe{layer}"
                last_static = TILE[("gather", layer, 1)]
                for b in range(BANKS):
                    n_b = last_static // BANKS + (1 if b <= last_static % BANKS else 0)
                    pe.wait_ge(psum_read[b], n_b)
                for b in range(4):
                    pe.matmul(banks[b][:], zeros[:], x[:, 0, 0:512], start=True, stop=True, skip_group_check=True)
                pe.wait_ge(trips_ready, layer + 1)
                n = pe.value_load(trips_i[0:1, 0:1], min_val=GROUPS, max_val=GROUPS * ROUNDS)
                with pe.Fori(0, n) as i:
                    def m_claim(m):
                        if m >= MOE_BANKS:
                            pe.wait_ge(M[f"read{4 + m % 4}"], i * PER_BANK + m // 4)

                    def m_emptied(m):
                        pe.wait_ge(M[f"read{4 + m % 4}"], i * PER_BANK + (m // 4 + 1))

                    def m_bank(m):
                        return banks[4 + m % 4]

                    def m_done(mm, m):
                        mm.then_inc(M[f"full{4 + m % 4}"], 1)

                    def weights_in(p, idx):
                        n = PER_PAIR * p + idx
                        pe.wait_ge(w_loaded[seg][n % MOE_RING], (i * ROUND_TRIPS + (n // MOE_RING + 1)) * 16)
                        return piece(n % MOE_RING, *((KD, DE) if idx < 4 else (FE, D)))

                    def scatter(p):
                        b = p % 2
                        m_emptied(PAIR_TILES * p + T_COMB)
                        for hf in range(2):
                            m_emptied(PAIR_TILES * p + T_OUT + hf)
                            for t in range(NT):
                                mm = pe.matmul(banks[2 * t + hf][:], comb[:, b, t * P:(t + 1) * P],
                                               ysb[:, b, hf * 512:(hf + 1) * 512], start=False, stop=True,
                                               skip_group_check=True)
                        return mm

                    for p in range(4):
                        b = p % 2
                        m0 = PAIR_TILES * p
                        m_claim(m0)
                        if p == 0:
                            pe.wait_ge(M["wpicked"], i + 1)
                        for t in range(NT):
                            mm = pe.transpose(m_bank(m0)[:, t * P:(t + 1) * P],
                                              wpick[:, t, 2 * p:2 * p + 2].rearrange("p a b -> p (a b)"), ident[:])
                        m_done(mm, m0)
                        if p > 0:
                            m_emptied(m0 - PAIR_TILES + T_NEXT)
                            m_emptied(m0 - PAIR_TILES + T_NEXT + 1)
                        for side in range(2):
                            m = m0 + T_GU + side
                            up, gate = (slice(0, 64), slice(64, P)) if side == 0 else (slice(64, P), slice(0, 64))
                            wg, wu = weights_in(p, 2 * side), weights_in(p, 2 * side + 1)
                            m_claim(m)
                            for k in range(KD):
                                lhs = xg[:, b * KD + k, side * SLOTS:(side + 1) * SLOTS]
                                pe.matmul(m_bank(m)[gate, :], lhs, wg[:, k], start=(k == 0), stop=(k == KD - 1),
                                          skip_group_check=True)
                                mu = pe.matmul(m_bank(m)[up, :], lhs, wu[:, k], start=(k == 0), stop=(k == KD - 1),
                                               skip_group_check=True)
                            m_done(mu, m)
                        if p > 0:
                            scatter(p - 1)
                        if p == 3:
                            pe.wait_ge(M["picked"], i + 2)
                        for half in range(2):
                            m = m0 + T_NEXT + half
                            m_claim(m)
                            m_done(gather(m_bank(m), half, (p + 1) % 4), m)
                        m = m0 + T_HID
                        m_claim(m)
                        m_emptied(m0 + T_GU)
                        m_emptied(m0 + T_GU + 1)
                        for f in range(FE):
                            mm = pe.transpose(m_bank(m)[:, f * P:(f + 1) * P], hid[:, b, f * P:(f + 1) * P], ident[:])
                        m_done(mm, m)
                        m_claim(m0 + T_OUT)
                        m_claim(m0 + T_OUT + 1)
                        wd = [weights_in(p, 4), weights_in(p, 5)]
                        m_emptied(m)
                        for hf in range(2):
                            for f in range(FE):
                                for side in range(2):
                                    r = slice(64 * side, 64 * side + 64)
                                    mm = pe.matmul(m_bank(m0 + T_OUT + hf)[r, :],
                                                   hidT[:, b, f * P + 64 * side:f * P + 64 * side + 64],
                                                   wd[side][:, f, hf * 512:(hf + 1) * 512],
                                                   start=(f == 0), stop=(f == FE - 1), skip_group_check=True)
                                    if f == FE - 1 and side == 1:
                                        m_done(mm, m0 + T_OUT + hf)
                    scatter(3).then_inc(M["scattered"], 1)
                    for half in range(2):
                        m_emptied(PAIR_TILES * 3 + T_NEXT + half)

            for layer in range(DEPTH):
                def rnn_gates():
                    for j in range(6):
                        if j % 2 == 0:
                            w_ = arrive2(pe, layer, PGR + j // 2)
                        name = ("gr", layer, j)
                        claim(name)
                        for f in range(min(2, RT - 2 * j)):
                            mm = by_feature(bank(name)[:, f * SEQ:(f + 1) * SEQ], w_, 2 * (j % 2) + f)
                        done(mm, name)

                def turn_rope(c):
                    name = ("ropeT", layer, c)
                    claim(name)
                    pe.wait_ge(roped2, 14 * layer + c + 1)
                    for k in range(4 if c < 12 else 1):
                        mm = pe.transpose(bank(name)[:, k * P:(k + 1) * P], roped[:, c % 4, k * P:(k + 1) * P], ident[:])
                    done(mm, name)

                def split_by_feature(q, f0, f1):
                    names = [("xr", layer, f) for f in range(f0, f1)]
                    for name in names:
                        claim(name)
                    for k in range(KD):
                        g = chunk(layer, q, k)
                        pe.wait_ge(chunk_lo, g + 1)
                        for f, name in enumerate(names):
                            fs = slice(f * P, (f + 1) * P)
                            pe.matmul(bank(name)[:], w_hi[:, g % CHUNKS, fs], stream[:, k].rearrange("p a b -> p (a b)"),
                                      start=(k == 0), stop=(k == KD - 1), skip_group_check=True)
                            mm = pe.matmul(bank(name)[:, 0:SEQ], w_lo[:, g % CHUNKS, fs], hT_hi[:, k],
                                           start=False, stop=(k == KD - 1), skip_group_check=True)
                            if k == KD - 1:
                                done(mm, name)
                        if k < KD - 1:
                            mm.then_inc(chunk_used, 1)

                def split_product(q, ready=None):
                    nm, last = SPLIT[q][1]
                    names = [(nm, layer, last - 1), (nm, layer, last)]
                    for name in names:
                        claim(name)
                    for k in range(KD):
                        g = chunk(layer, q, k)
                        pe.wait_ge(chunk_lo, g + 1)
                        if ready is not None:
                            pe.wait_ge(ready, KD * layer + k + 1)
                        for t in range(NT):
                            dst, ts = bank(names[t])[:], slice(t * P, (t + 1) * P)
                            pe.matmul(dst, hT_hi[:, k, ts], w_hi[:, g % CHUNKS], start=(k == 0), stop=False)
                            pe.matmul(dst, hT_lo[:, k, ts], w_hi[:, g % CHUNKS], start=False, stop=False)
                            mm = pe.matmul(dst, hT_hi[:, k, ts], w_lo[:, g % CHUNKS], start=False, stop=(k == KD - 1))
                            if k == KD - 1:
                                done(mm, names[t])
                        if k < KD - 1:
                            mm.then_inc(chunk_used, 1)

                w = arrive2(pe, layer, PROPE)
                for t in range(NT):
                    turn_h(SECOND + layer, t, IDLE_BETWEEN if layer == 0 and t == 0 else 0)
                    by_token(("rope", layer, t), w, 512, t)
                pe.wait_ge(hT_lo_ready, layer + 1)
                for c in range(2, 14, 2):
                    if c < 12:
                        split_product(c // 2 - 1)
                    else:
                        w = arrive2(pe, layer, PROPE + 6)
                        for t in range(NT):
                            by_token(("rope", layer, c + t), w, P, t)
                    turn_rope(c - 2)
                    turn_rope(c - 1)
                turn_rope(12)
                turn_rope(13)
                for q in range(3):
                    split_by_feature(QXR + q, 4 * q, min(4 * q + 4, RT))
                split_product(QV)
                split_product(QV + 1)
                for c in range(8, 14):
                    emptied(pe, ("ropeT", layer, c))
                for j in range(0, 12, 2):
                    names = [("dots", layer, j), ("dots", layer, j + 1)]
                    for n_ in names:
                        claim(n_)
                    cnt, w_ = (4, P) if j < 4 else (2, SEQ)
                    for k in range(cnt):
                        for odd in range(2):
                            if j < 4:
                                hd, qb = 8 * (j // 2) + 2 * k + odd, 0
                            else:
                                hd, qb = 4 * ((j - 4) // 2) + 2 * k + odd, 1
                            r = slice(64 * odd, 64 * odd + 64)
                            mm = pe.matmul(bank(names[odd])[:, k * w_:(k + 1) * w_], iqT[r, hd // 2, qb * P:(qb + 1) * P],
                                           ikT[r, 0:w_], start=True, stop=True)
                            if k == cnt - 1:
                                done(mm, names[odd])
                wr, wi = arrive2(pe, layer, PLRU), arrive2(pe, layer, PLRU + 1)
                pe.wait_ge(conv2_done, layer + 1)
                for j in range(RT):
                    name = ("gates", layer, j)
                    claim(name)
                    mine = [(n, i) for n, (jj, i) in enumerate(BLOCK_PAIRS) if jj == j]
                    for g, wg_ in enumerate((wr, wi)):
                        for n, i in mine:
                            mm = pe.matmul(bank(name)[:, g * SEQ:(g + 1) * SEQ], wg_[:, n], xc[:, i],
                                           start=(n == mine[0][0]), stop=(n == mine[-1][0]))
                    done(mm, name)
                rnn_gates()

                def scores2(hh):
                    name = ("S2", layer, hh)
                    claim(name)
                    pe.matmul(bank(name)[:, 0:P], qT[:, hh, 0:P], kT[:, hh, 0:P], start=True, stop=True)
                    mm = pe.matmul(bank(name)[:, P:3 * P], qT[:, hh, P:], kT[:, hh], start=True, stop=True)
                    done(mm, name)

                for c in range(8):
                    emptied(pe, ("ropeT", layer, c))
                for j in range(4):
                    emptied(pe, ("v", layer, j))
                def gate(hh):
                    name = ("ga", layer, hh)
                    w_ = arrive2(pe, layer, PGA + hh // 4)
                    claim(name)
                    done(by_feature(bank(name)[:, 0:SEQ], w_, hh % 4), name)

                scores2(0)
                gate(0)
                for hh in range(HEADS):
                    if hh + 1 < HEADS:
                        scores2(hh + 1)
                    name = ("PT2", layer, hh)
                    claim(name)
                    pe.wait_ge(probs2, layer * HEADS + hh + 1)
                    b = hh % 2
                    pe.transpose(bank(name)[:, 0:P], s2[:, b, 0:P], ident[:])
                    pe.transpose(bank(name)[:, P:2 * P], s2[:, b, P:2 * P], ident[:])
                    done(pe.transpose(bank(name)[:, 2 * P:3 * P], s2[:, b, 2 * P:], ident[:]), name)
                    if hh + 1 < HEADS:
                        gate(hh + 1)
                    emptied(pe, name)
                    yn = ("Y2", layer, hh)
                    claim(yn)
                    hs = slice(hh * HD2, (hh + 1) * HD2)
                    pe.matmul(bank(yn)[:, 0:SEQ], vv[:, 0, hs], pT2[:, b, 0:SEQ], start=True, stop=False)
                    done(pe.matmul(bank(yn)[:, P:SEQ], vv[:, 1, hs], pT2[:, b, 2 * P:], start=False, stop=True), yn)
                for j in range(6):
                    emptied(pe, ("gr", layer, j))
                for pc in range(4):
                    wm, wb = arrive2(pe, layer, PMB + 2 * pc), arrive2(pe, layer, PMB + 2 * pc + 1)
                    for f in range(2):
                        name = ("mb", layer, 2 * pc + f)
                        claim(name)
                        by_feature(bank(name)[:, 0:SEQ], wm, f)
                        done(by_feature(bank(name)[:, SEQ:], wb, f, ui, RT), name)
                pe.wait_ge(attn_gated, 2 * layer + 2)
                for pc in range(2):
                    wm, wa = arrive2(pe, layer, PMA + 2 * pc), arrive2(pe, layer, PMA + 2 * pc + 1)
                    for f in range(4):
                        name = ("ma", layer, 4 * pc + f)
                        claim(name)
                        by_feature(bank(name)[:, 0:SEQ], wm, f)
                        done(by_feature(bank(name)[:, SEQ:], wa, f, qT), name)
                split_product(QO, merged_lo)
                w = arrive2(pe, layer, PO + 1)
                for t in range(NT):
                    name = ("out2", layer, NT + t)
                    claim(name)
                    for k in range(KD):
                        mm = pe.matmul(bank(name)[:], merged[:, k, t * P:(t + 1) * P], w[:, k], start=(k == 0),
                                       stop=(k == KD - 1))
                    done(mm, name)


def _columns(v):
    return v.reshape(-1, P).T


def _block_diagonal(w):
    whole = np.zeros((RNN, RNN), w.dtype)
    for b in range(RB):
        whole[b * RBD:(b + 1) * RBD, b * RBD:(b + 1) * RBD] = w[b]
    return np.concatenate([whole[i * P:(i + 1) * P, j * P:(j + 1) * P] for j, i in BLOCK_PAIRS], axis=1)


def kernel(**inputs):
    import concourse.bacc as bacc
    from concourse.bass_utils import run_bass_kernel_spmd

    a = {k: np.asarray(v) for k, v in inputs.items()}
    f = np.float32
    cols = np.stack([np.concatenate(
        [_columns(a["norm_attn_out"][l]), _columns(a["norm_conv_out"][l]), _columns(a["conv_w"][l].reshape(-1)),
         _columns(a["conv_w_2"][l].reshape(-1)), _columns(a["conv_b_2"][l]), _columns(a["b_rg_2"][l]),
         _columns(a["b_ig_2"][l]), _columns(a["lru_lambda_2"][l])], axis=1) for l in range(DEPTH)], axis=1)

    def inverse_frequencies(theta, dim):
        return (f(theta) ** (-np.arange(0, dim, 2, dtype=f) / f(dim))).astype(f)

    inv2 = np.concatenate([inverse_frequencies(10000.0, HD2), inverse_frequencies(10000.0, ID)])
    rows = np.concatenate(
        [np.concatenate([a["b_router_group"][l], a["b_router_expert"][l]]) for l in range(DEPTH)]
        + [a["attn_sink"][l] for l in range(DEPTH)] + [inv2])
    rows = np.broadcast_to(rows, (P, rows.size))
    angle = np.arange(SEQ, dtype=f)[:, None] * inverse_frequencies(500000.0, 2 * ROT1)
    rope1 = np.stack([np.broadcast_to(g(angle).reshape(NT, P, 1, ROT1), (NT, P, HEADS + KVH, ROT1))
                      .transpose(1, 0, 2, 3).reshape(P, -1) for g in (np.cos, np.sin)], axis=1)
    gains = np.stack([a["norm_mix"][0], a["norm_ffn"][0], a["norm_mix"][1], a["norm_ffn"][1],
                      a["norm_final"], a["norm_g_2"][0], a["norm_g_2"][1], a["final_g_2"]])
    gains = np.broadcast_to(gains[:, None], (gains.shape[0], P, D))
    router = np.concatenate([a["w_router_group"], a["w_router_expert"]], axis=2)
    lru = np.stack([np.stack([_block_diagonal(a[n][l]) for n in ("w_rg_2", "w_ig_2")]) for l in range(DEPTH)])
    arrays = {
        "x_in": a["x"].reshape(SEQ, D), "cols_in": cols, "rows_in": rows, "rope1_in": rope1, "gains_in": gains,
        "router_in": router, "w_in": a["w_in"], "w_out": a["w_out"], "w_gate": a["w_expert_gate"],
        "w_up": a["w_expert_up"], "w_down": a["w_expert_down"], "positions": a["positions_2"].reshape(NT, P).T,
        "w_in2": a["w_in_2"], "w_lru": lru, "w_oa": a["w_out_attn_2"], "w_or": a["w_out_rnn_2"], "w_o": a["w_o_2"],
    }
    arrays = {k: np.ascontiguousarray(v) for k, v in arrays.items()}
    nc = bacc.Bacc("TRN2", target_bir_lowering=False, num_devices=1)
    args = {k: nc.dram_tensor(f"{k}_dram", v.shape, mybir.dt.from_np(v.dtype), kind="ExternalInput").ap()
            for k, v in arrays.items()}
    out = nc.dram_tensor("out_dram", (SEQ, D), F32, kind="ExternalOutput").ap()
    program(nc, *args.values(), out)
    r = run_bass_kernel_spmd(nc, [{f"{k}_dram": v for k, v in arrays.items()}], core_ids=[0])
    return r.results[0]["out_dram"].reshape(1, SEQ, D)
```
